# Optimizing a Trainium2 kernel written in Bass

```python
import math
import jax, jax.numpy as jnp
from jax import lax
import numpy as np

D_MODEL = 1024
BATCH = 1
SEQ = 256
DEPTH = 1

D_MIX = 2 * D_MODEL
ATTN_WIDTH = D_MIX // 2
SB_HEAD_DIM = 64
SB_HEADS = ATTN_WIDTH // SB_HEAD_DIM
SB_BLOCK = 128
SSD_WIDTH = D_MIX - ATTN_WIDTH
SSD_HEAD_DIM = 64
SSD_HEADS = SSD_WIDTH // SSD_HEAD_DIM
SSD_GROUPS = 2
SSD_STATE = 128
SSD_CONV_K = 4
SSD_CHUNK = 128
SSD_CONV_CH = SSD_WIDTH + 2 * SSD_GROUPS * SSD_STATE
IN_SPLITS = (ATTN_WIDTH, ATTN_WIDTH, ATTN_WIDTH, SSD_WIDTH, SSD_WIDTH,
             SSD_GROUPS * SSD_STATE, SSD_GROUPS * SSD_STATE, SSD_HEADS)
D_IN = sum(IN_SPLITS)
MEM_LEN = 256
XA_HEADS = 4
XA_HEAD_DIM = D_MODEL // XA_HEADS
D_FF = 2816
EPS = 1e-6


def rmsnorm(x, g):
    x32 = x.astype(jnp.float32)
    y = x32 * lax.rsqrt(jnp.mean(x32 * x32, axis=-1, keepdims=True) + EPS)
    return (y * g.astype(jnp.float32)).astype(x.dtype)

def swiglu(h, w_gu, w_down):
    gu = h @ w_gu
    g, u = jnp.split(gu, 2, axis=-1)
    return (jax.nn.silu(g) * u) @ w_down

def stick_breaking_attention(q, k, v):
    b_, h_, s_, d_ = q.shape
    scale = 1.0 / math.sqrt(d_)
    outs = []
    for i in range(s_ // SB_BLOCK):
        t0, t1 = i * SB_BLOCK, (i + 1) * SB_BLOCK
        qb = q[:, :, t0:t1].astype(jnp.float32)
        kb = k[:, :, :t1].astype(jnp.float32)
        vb = v[:, :, :t1]
        z = jnp.einsum('bhtd,bhsd->bhts', qb, kb) * scale
        t_idx = t0 + jnp.arange(SB_BLOCK)
        s_idx = jnp.arange(t1)
        causal = s_idx[None, :] < t_idx[:, None]
        log_1mb = jnp.where(causal, jax.nn.log_sigmoid(-z), 0.0)
        suffix = lax.cumsum(log_1mb, axis=3, reverse=True) - log_1mb
        log_a = jnp.where(causal, jax.nn.log_sigmoid(z) + suffix, -jnp.inf)
        a = jnp.exp(log_a)
        outs.append(jnp.einsum('bhts,bhsd->bhtd', a, vb.astype(jnp.float32)))
    return jnp.concatenate(outs, axis=2).astype(v.dtype)

def ssd_chunked(xs, dt, a, bmat, cmat):
    b_, s_, h_, p_ = xs.shape
    L, G, N = SSD_CHUNK, SSD_GROUPS, SSD_STATE
    R = h_ // G
    nc = s_ // L
    x = (xs.astype(jnp.float32) * dt[..., None]).reshape(b_, nc, L, G, R, p_)
    adt = (dt * a).reshape(b_, nc, L, G, R).transpose(0, 3, 4, 1, 2)
    a_cs = jnp.cumsum(adt, axis=-1)
    bc = bmat.astype(jnp.float32).reshape(b_, nc, L, G, N)
    cc = cmat.astype(jnp.float32).reshape(b_, nc, L, G, N)
    tri = jnp.tril(jnp.ones((L, L), dtype=bool))
    diff = a_cs[..., :, None] - a_cs[..., None, :]
    lmat = jnp.exp(jnp.where(tri, diff, -jnp.inf))
    cb = jnp.einsum('bclgn,bcsgn->bcgls', cc, bc)
    y_diag = jnp.einsum('bcgls,bgrcls,bcsgrp->bclgrp', cb, lmat, x)
    decay_states = jnp.exp(a_cs[..., -1:] - a_cs)
    states = jnp.einsum('bclgn,bgrcl,bclgrp->bcgrpn', bc, decay_states, x)
    chunk_decay = jnp.exp(a_cs[..., -1])

    def step(h, inp):
        st, dec = inp
        return h * dec[..., None, None] + st, h

    h0 = jnp.zeros_like(states[:, 0])
    _, states_in = lax.scan(step, h0, (jnp.moveaxis(states, 1, 0),
                                       jnp.moveaxis(chunk_decay, -1, 0)))
    states_in = jnp.moveaxis(states_in, 0, 1)
    y_off = jnp.einsum('bclgn,bcgrpn,bgrcl->bclgrp', cc, states_in, jnp.exp(a_cs))
    return (y_diag + y_off).reshape(b_, s_, h_, p_)

def hybrid_mixer(u, w_in, conv_w, conv_b, dt_bias, a_log, d_skip,
                 ssd_norm_g, attn_norm_g, w_out):
    b_, s_, _ = u.shape
    proj = u @ w_in
    q, k, v, z, xs, bm, cm, dt_raw = jnp.split(proj, np.cumsum(IN_SPLITS)[:-1], axis=-1)
    def heads(t):
        return t.reshape(b_, s_, SB_HEADS, SB_HEAD_DIM).transpose(0, 2, 1, 3)
    o_att = stick_breaking_attention(heads(q), heads(k), heads(v))
    o_att = o_att.transpose(0, 2, 1, 3).reshape(b_, s_, ATTN_WIDTH)
    o_att = rmsnorm(o_att, attn_norm_g)
    xbc = jnp.concatenate([xs, bm, cm], axis=-1)
    xbc = lax.conv_general_dilated(
        xbc, conv_w.astype(xbc.dtype)[:, None, :], window_strides=(1,),
        padding=[(SSD_CONV_K - 1, 0)], dimension_numbers=('NWC', 'WIO', 'NWC'),
        feature_group_count=SSD_CONV_CH)
    xbc = jax.nn.silu(xbc + conv_b)
    xs, bm, cm = jnp.split(xbc, [SSD_WIDTH, SSD_WIDTH + SSD_GROUPS * SSD_STATE], axis=-1)
    xs = xs.reshape(b_, s_, SSD_HEADS, SSD_HEAD_DIM)
    bm = bm.reshape(b_, s_, SSD_GROUPS, SSD_STATE)
    cm = cm.reshape(b_, s_, SSD_GROUPS, SSD_STATE)
    dt = jax.nn.softplus(dt_raw.astype(jnp.float32) + dt_bias.astype(jnp.float32))
    a = -jnp.exp(a_log.astype(jnp.float32))
    y = ssd_chunked(xs, dt, a, bm, cm)
    y = y + d_skip.astype(jnp.float32)[:, None] * xs.astype(jnp.float32)
    y = y.reshape(b_, s_, SSD_WIDTH) * jax.nn.silu(z.astype(jnp.float32))
    y = rmsnorm(y.reshape(b_, s_, SSD_GROUPS, SSD_WIDTH // SSD_GROUPS),
                ssd_norm_g.reshape(SSD_GROUPS, SSD_WIDTH // SSD_GROUPS))
    o_ssd = y.reshape(b_, s_, SSD_WIDTH).astype(u.dtype)
    return jnp.concatenate([o_att, o_ssd], axis=-1) @ w_out

def memory_cross_attention(h, mem_n, wq, wkv, wo):
    b_, s_, _ = h.shape
    q = (h @ wq).reshape(b_, s_, XA_HEADS, XA_HEAD_DIM)
    kv = mem_n @ wkv
    k, v = jnp.split(kv, 2, axis=-1)
    k = k.reshape(b_, MEM_LEN, XA_HEADS, XA_HEAD_DIM)
    v = v.reshape(b_, MEM_LEN, XA_HEADS, XA_HEAD_DIM)
    sc = jnp.einsum('bshd,bmhd->bhsm', q.astype(jnp.float32), k.astype(jnp.float32))
    p = jax.nn.softmax(sc / math.sqrt(XA_HEAD_DIM), axis=-1)
    o = jnp.einsum('bhsm,bmhd->bshd', p, v.astype(jnp.float32)).astype(h.dtype)
    return o.reshape(b_, s_, D_MODEL) @ wo

def first_inputs(seed: int = 0) -> dict:
    key = jax.random.key(seed)
    ks = iter(jax.random.split(key, 40))

    def w(shape, fan_in):
        return jax.random.normal(next(ks), (DEPTH,) + shape, jnp.float32) * fan_in ** -0.5

    def gain(n):
        return 1.0 + 0.02 * jax.random.normal(next(ks), (DEPTH, n), jnp.float32)

    x = jax.random.normal(next(ks), (BATCH, SEQ, D_MODEL), jnp.float32)
    mem = jax.random.normal(next(ks), (BATCH, MEM_LEN, D_MODEL), jnp.float32)
    dt0 = jnp.exp(jax.random.uniform(next(ks), (DEPTH, SSD_HEADS), jnp.float32,
                                     math.log(1e-3), math.log(1e-1)))
    dt_bias = dt0 + jnp.log(-jnp.expm1(-dt0))
    a_log = jnp.log(jax.random.uniform(next(ks), (DEPTH, SSD_HEADS), jnp.float32, 1.0, 16.0))
    return {
        "x": x, "mem": mem,
        "ffn1_pre_g": gain(D_MODEL),
        "ffn1_w_gu": w((D_MODEL, 2 * D_FF), D_MODEL),
        "ffn1_w_down": w((D_FF, D_MODEL), D_FF),
        "ffn1_post_g": gain(D_MODEL),
        "mix_pre_g": gain(D_MODEL),
        "w_in": w((D_MODEL, D_IN), D_MODEL),
        "conv_w": w((SSD_CONV_K, SSD_CONV_CH), SSD_CONV_K),
        "conv_b": 0.02 * jax.random.normal(next(ks), (DEPTH, SSD_CONV_CH), jnp.float32),
        "dt_bias": dt_bias,
        "a_log": a_log,
        "d_skip": 1.0 + 0.1 * jax.random.normal(next(ks), (DEPTH, SSD_HEADS), jnp.float32),
        "ssd_norm_g": gain(SSD_WIDTH),
        "attn_norm_g": gain(ATTN_WIDTH),
        "w_out": w((D_MIX, D_MODEL), D_MIX),
        "mix_post_g": gain(D_MODEL),
        "xa_pre_g": gain(D_MODEL),
        "mem_g": gain(D_MODEL),
        "xa_wq": w((D_MODEL, D_MODEL), D_MODEL),
        "xa_wkv": w((D_MODEL, 2 * D_MODEL), D_MODEL),
        "xa_wo": w((D_MODEL, D_MODEL), D_MODEL),
        "xa_post_g": gain(D_MODEL),
        "ffn2_pre_g": gain(D_MODEL),
        "ffn2_w_gu": w((D_MODEL, 2 * D_FF), D_MODEL),
        "ffn2_w_down": w((D_FF, D_MODEL), D_FF),
        "ffn2_post_g": gain(D_MODEL),
    }

def first_block(x, mem, ffn1_pre_g, ffn1_w_gu, ffn1_w_down, ffn1_post_g,
              mix_pre_g, w_in, conv_w, conv_b, dt_bias, a_log, d_skip,
              ssd_norm_g, attn_norm_g, w_out, mix_post_g,
              xa_pre_g, mem_g, xa_wq, xa_wkv, xa_wo, xa_post_g,
              ffn2_pre_g, ffn2_w_gu, ffn2_w_down, ffn2_post_g):
    h = x
    for l in range(DEPTH):
        f = swiglu(rmsnorm(h, ffn1_pre_g[l]), ffn1_w_gu[l], ffn1_w_down[l])
        h = h + 0.5 * rmsnorm(f, ffn1_post_g[l])
        m = hybrid_mixer(rmsnorm(h, mix_pre_g[l]), w_in[l], conv_w[l], conv_b[l],
                         dt_bias[l], a_log[l], d_skip[l], ssd_norm_g[l],
                         attn_norm_g[l], w_out[l])
        h = h + rmsnorm(m, mix_post_g[l])
        c = memory_cross_attention(rmsnorm(h, xa_pre_g[l]), rmsnorm(mem, mem_g[l]),
                                   xa_wq[l], xa_wkv[l], xa_wo[l])
        h = h + rmsnorm(c, xa_post_g[l])
        f = swiglu(rmsnorm(h, ffn2_pre_g[l]), ffn2_w_gu[l], ffn2_w_down[l])
        h = h + 0.5 * rmsnorm(f, ffn2_post_g[l])
    return h


D_CONV = 512
CONV_GROUPS = 8
CONV_WIDTH = 3
HG_HEADS = 4
HG_KD = 128
HG_VD = 128
D_HG = HG_HEADS * HG_KD
D_MIX_2 = D_CONV + D_HG
D_IN_2 = 3 * D_CONV + 4 * D_HG
CHUNK = 32
PEER_HEADS = 8
N_KEYS = 128
N_EXPERTS = N_KEYS * N_KEYS
D_QUERY = 256
HALF_Q = D_QUERY // 2
PEER_TOPK = 16
TOKEN_BLOCK = 128


def rmsnorm_2(x, gain):
    x32 = x.astype(jnp.float32)
    y = x32 * lax.rsqrt(jnp.mean(x32 * x32, axis=-1, keepdims=True) + EPS)
    return (y * gain.astype(jnp.float32)).astype(x.dtype)

def group_rmsnorm(x, gain, groups):
    shp = x.shape
    xg = x.reshape(shp[:-1] + (groups, shp[-1] // groups)).astype(jnp.float32)
    y = xg * lax.rsqrt(jnp.mean(xg * xg, axis=-1, keepdims=True) + EPS)
    return (y.reshape(shp) * gain.astype(jnp.float32)).astype(x.dtype)

def short_conv_mixer(c_gate, h, b_gate, conv_w, gain):
    u = c_gate * h
    s = u.shape[1]
    up = jnp.pad(u, ((0, 0), (CONV_WIDTH - 1, 0), (0, 0)))
    y = conv_w[0] * up[:, 0:s]
    for j in range(1, CONV_WIDTH):
        y = y + conv_w[j] * up[:, j:j + s]
    y = b_gate * y
    return group_rmsnorm(y, gain, CONV_GROUPS)

def hgrn2_mixer(q, f_pre, v, g, lb, gain):
    f32 = jnp.float32
    bsz, s, _ = q.shape
    n_chunks = s // CHUNK

    def heads(t):
        return t.reshape(bsz, n_chunks, CHUNK, HG_HEADS, -1).transpose(0, 3, 1, 2, 4)

    qh = heads(jax.nn.silu(q.astype(f32)) * (HG_KD ** -0.5))
    f = lb + (1.0 - lb) * jax.nn.sigmoid(f_pre.astype(f32))
    kh = heads(1.0 - f)
    logf = heads(jnp.log(f))
    vh = heads(v.astype(f32))
    G = jnp.cumsum(logf, axis=3)
    G_last = G[:, :, :, -1:, :]
    q_dec = qh * jnp.exp(G)
    k_dec = kh * jnp.exp(-G)
    causal = jnp.tril(jnp.ones((CHUNK, CHUNK), dtype=bool))
    A = jnp.einsum('bhnck,bhnsk->bhncs', q_dec, k_dec)
    A = jnp.where(causal, A, 0.0)
    o_intra = jnp.einsum('bhncs,bhnsv->bhncv', A, vh)
    k_end = kh * jnp.exp(G_last - G)
    decay = jnp.exp(G_last[:, :, :, 0, :])

    def step(state, xs):
        dec_n, k_n, v_n, q_n = xs
        o_n = jnp.einsum('bhck,bhkv->bhcv', q_n, state)
        state = dec_n[..., None] * state + jnp.einsum('bhck,bhcv->bhkv', k_n, v_n)
        return state, o_n

    state0 = jnp.zeros((bsz, HG_HEADS, HG_KD, HG_VD), f32)
    _, o_inter = lax.scan(step, state0, (jnp.moveaxis(decay, 2, 0), jnp.moveaxis(k_end, 2, 0),
                                         jnp.moveaxis(vh, 2, 0), jnp.moveaxis(q_dec, 2, 0)))
    o = o_intra + jnp.moveaxis(o_inter, 0, 2)
    o = o * lax.rsqrt(jnp.mean(o * o, axis=-1, keepdims=True) + EPS) * gain.astype(f32)
    o = o * jax.nn.silu(heads(g.astype(f32)))
    o = o.transpose(0, 2, 3, 1, 4).reshape(bsz, s, HG_HEADS * HG_VD)
    return o.astype(q.dtype)

def peer_ffn(x, wq, keys, u_tab, v_tab):
    bsz, s, d = x.shape
    t = bsz * s
    xt = x.reshape(t, d)
    q = (xt @ wq).reshape(t, PEER_HEADS, 2, HALF_Q)
    scores = jnp.einsum('thpd,hpnd->thpn', q, keys).astype(jnp.float32)
    s_top, i_top = lax.top_k(scores, PEER_TOPK)
    cand = (s_top[:, :, 0, :, None] + s_top[:, :, 1, None, :]).reshape(t, PEER_HEADS, PEER_TOPK * PEER_TOPK)
    c_score, c_idx = lax.top_k(cand, PEER_TOPK)
    i1 = jnp.take_along_axis(i_top[:, :, 0], c_idx // PEER_TOPK, axis=-1)
    i2 = jnp.take_along_axis(i_top[:, :, 1], c_idx % PEER_TOPK, axis=-1)
    expert = i1 * N_KEYS + i2
    gates = jax.nn.softmax(c_score, axis=-1)
    n_blocks = t // TOKEN_BLOCK

    def block(args):
        xb, eb, gb = args
        u = jnp.take(u_tab, eb, axis=0)
        a = jax.nn.gelu(jnp.einsum('td,thkd->thk', xb, u).astype(jnp.float32), approximate=False)
        w = (gb * a).astype(xb.dtype)
        vv = jnp.take(v_tab, eb, axis=0)
        return jnp.einsum('thk,thkd->td', w, vv)

    y = lax.map(block, (xt.reshape(n_blocks, TOKEN_BLOCK, d),
                        expert.reshape(n_blocks, TOKEN_BLOCK, PEER_HEADS, PEER_TOPK),
                        gates.reshape(n_blocks, TOKEN_BLOCK, PEER_HEADS, PEER_TOPK)))
    return y.reshape(bsz, s, d)

def second_inputs(seed: int = 0) -> dict:
    key = jax.random.key(seed)
    ks = jax.random.split(key, 16)
    f32 = jnp.float32
    nrm = lambda k, shp: jax.random.normal(k, shp, f32)
    return {
        "x": nrm(ks[0], (BATCH, SEQ, D_MODEL)),
        "norm_mix": 1.0 + 0.02 * nrm(ks[1], (DEPTH, D_MODEL)),
        "w_in": nrm(ks[2], (DEPTH, D_MODEL, D_IN_2)) * D_MODEL ** -0.5,
        "conv_w": nrm(ks[3], (DEPTH, CONV_WIDTH, D_CONV)) * CONV_WIDTH ** -0.5,
        "conv_gain": 1.0 + 0.02 * nrm(ks[4], (DEPTH, D_CONV)),
        "hg_lb_logits": 0.1 * nrm(ks[5], (DEPTH + 1, D_HG)),
        "hg_gain": 1.0 + 0.02 * nrm(ks[6], (DEPTH, HG_VD)),
        "w_out": nrm(ks[7], (DEPTH, D_MIX_2, D_MODEL)) * D_MIX_2 ** -0.5,
        "norm_ffn": 1.0 + 0.02 * nrm(ks[8], (DEPTH, D_MODEL)),
        "peer_wq": nrm(ks[9], (DEPTH, D_MODEL, PEER_HEADS * D_QUERY)) * D_MODEL ** -0.5,
        "peer_keys": nrm(ks[10], (DEPTH, PEER_HEADS, 2, N_KEYS, HALF_Q)) * HALF_Q ** -0.5,
        "peer_u": nrm(ks[11], (DEPTH, N_EXPERTS, D_MODEL)) * D_MODEL ** -0.5,
        "peer_v": nrm(ks[12], (DEPTH, N_EXPERTS, D_MODEL)) * PEER_HEADS ** -0.5,
        "norm_f": 1.0 + 0.02 * nrm(ks[13], (D_MODEL,)),
    }

def second_block(x, norm_mix, w_in, conv_w, conv_gain, hg_lb_logits, hg_gain, w_out,
              norm_ffn, peer_wq, peer_keys, peer_u, peer_v, norm_f):
    lb_all = jnp.cumsum(jax.nn.softmax(hg_lb_logits.astype(jnp.float32), axis=0), axis=0)
    splits = [D_CONV, 2 * D_CONV, 3 * D_CONV, 3 * D_CONV + D_HG, 3 * D_CONV + 2 * D_HG, 3 * D_CONV + 3 * D_HG]
    for l in range(DEPTH):
        h = rmsnorm_2(x, norm_mix[l])
        proj = h @ w_in[l]
        c_gate, hc, b_gate, q, f_pre, v, g = jnp.split(proj, splits, axis=-1)
        conv_out = short_conv_mixer(c_gate, hc, b_gate, conv_w[l], conv_gain[l])
        hg_out = hgrn2_mixer(q, f_pre, v, g, lb_all[l], hg_gain[l])
        mix = jnp.concatenate([conv_out, hg_out], axis=-1)
        x = x + mix @ w_out[l]
        h2 = rmsnorm_2(x, norm_ffn[l])
        x = x + peer_ffn(h2, peer_wq[l], peer_keys[l], peer_u[l], peer_v[l])
    return rmsnorm_2(x, norm_f)


def setup_inputs(seed=0):
    out = dict(first_inputs(seed))
    for name, value in second_inputs(seed + 1).items():
        if name != "x":
            out[name + "_2"] = value
    return out


def reference(
    x, mem, ffn1_pre_g, ffn1_w_gu, ffn1_w_down, ffn1_post_g, mix_pre_g, w_in, conv_w, conv_b,
    dt_bias, a_log, d_skip, ssd_norm_g, attn_norm_g, w_out, mix_post_g, xa_pre_g, mem_g, xa_wq,
    xa_wkv, xa_wo, xa_post_g, ffn2_pre_g, ffn2_w_gu, ffn2_w_down, ffn2_post_g, norm_mix_2,
    w_in_2, conv_w_2, conv_gain_2, hg_lb_logits_2, hg_gain_2, w_out_2, norm_ffn_2, peer_wq_2,
    peer_keys_2, peer_u_2, peer_v_2, norm_f_2,
):
    x = first_block(
        x, mem, ffn1_pre_g, ffn1_w_gu, ffn1_w_down, ffn1_post_g, mix_pre_g, w_in, conv_w,
        conv_b, dt_bias, a_log, d_skip, ssd_norm_g, attn_norm_g, w_out, mix_post_g, xa_pre_g,
        mem_g, xa_wq, xa_wkv, xa_wo, xa_post_g, ffn2_pre_g, ffn2_w_gu, ffn2_w_down, ffn2_post_g,
    )
    return second_block(
        x, norm_mix_2, w_in_2, conv_w_2, conv_gain_2, hg_lb_logits_2, hg_gain_2, w_out_2,
        norm_ffn_2, peer_wq_2, peer_keys_2, peer_u_2, peer_v_2, norm_f_2,
    )


_drawn_inputs = setup_inputs


def setup_inputs(seed=0):
    import zlib

    import numpy as np

    out = dict(_drawn_inputs(seed))
    spreads = {}
    factors = {'ffn1_post_g': 3.427,
     'conv_b': 2.771,
     'ssd_norm_g': 3.692,
     'attn_norm_g': 3.743,
     'mix_post_g': 2.876,
     'xa_pre_g': 3.299,
     'xa_post_g': 3.294,
     'ffn2_pre_g': 11.729,
     'ffn2_post_g': 20.773,
     'norm_mix_2': 3.147,
     'conv_gain_2': 45.72,
     'hg_lb_logits_2': 8.0,
     'hg_gain_2': 22.562,
     'norm_ffn_2': 31.027,
     'norm_f_2': 7.709}
    for name, (base, spread) in spreads.items():
        noise = np.random.default_rng([zlib.crc32(name.encode()), seed]).standard_normal(out[name].shape)
        drawn = base * np.exp(spread * noise) if base else spread * noise
        out[name] = __import__('jax').numpy.asarray(drawn.astype(out[name].dtype))
    for name, factor in factors.items():
        out[name] = (out[name] * factor).astype(out[name].dtype)
    return out
```

```python
from contextlib import ExitStack

import numpy as np

import concourse.bass as bass
from concourse import mybir

F32 = mybir.dt.float32
F32R = mybir.dt.float32r
U32 = mybir.dt.uint32
ACT = mybir.ActivationFunctionType
ALU = mybir.AluOpType
AX_X = mybir.AxisListType.X

P = 128
SEQ = 256
TT = SEQ // P
D = 1024
KT = D // P
D_FF = 2816
FFN_PANELS = D_FF // 256
FFN_KT = D_FF // P
EPS = 1e-6
BLK = 1024
SLOTS = 4
PB = 4
KB = 1024

STREAM = [
    ("xa_kv", 16), ("ffn1_up", 44), ("ffn1_down", 22), ("w_in", 44), ("w_out", 16),
    ("xa_q", 8), ("xa_o", 8), ("ffn2_up", 44), ("ffn2_down", 22), ("w_in_2", 28),
    ("w_out_2", 8), ("peer_q", 16), ("peer", 256),
]
BASE, N_BLOCKS = {}, 0
for _name, _n in STREAM:
    BASE[_name] = N_BLOCKS
    N_BLOCKS += _n

EVAC, N_EVAC = {}, 0
for _name, _n in (("xa_kv", 4), ("w_in", 11), ("xa_q", 2), ("w_in_2", 7), ("peer_q", 4)):
    EVAC[_name] = N_EVAC
    N_EVAC += _n

GAIN_COL = {"mem": 0, "ffn1": 8, "mix": 16, "xa": 24, "ffn2": 32, "mix2": 40, "peer": 48,
            "attn": 56, "ssd": 64}
CONV_GAIN2, HG_GAIN, CONV_B, CONV_W, CONV_W2, LB = 72, 76, 77, 89, 137, 149
N_COLS = 157
HG_CHUNK = 32
SQUARES = [0, 2, 4, 6, 8, 12, 14, 16, 18, 20]



class Chain:

    def __init__(self, engine, semaphore):
        self.engine, self.semaphore, self.count = engine, semaphore, 0
        self.dyn, self.scale = None, 1

    def __call__(self, instruction):
        self.count += 1
        instruction.then_inc(self.semaphore, 1)
        self.engine.wait_ge(self.semaphore, at(self.count, self.dyn, self.scale))

    def enter(self, dyn, each):
        self.dyn, self.scale, self.began = dyn, each, self.count

    def leave(self, times):
        assert self.count - self.began == self.scale
        self.count, self.dyn, self.scale = self.began + times * self.scale, None, 1


def at(static, dyn=None, scale=1):
    return static if dyn is None else dyn * scale + static


def build(nc, stream, w_dt, cols, small_row, rows, x, mem, keys, out):
    ctx = ExitStack()
    B0 = 16512

    def sb(name, shape, kb, dt=F32):
        return nc.alloc_sbuf_tensor_at(name, shape, dt, offset=B0 + int(kb * KB))

    def sem(name):
        return ctx.enter_context(nc.semaphore(name))

    PS = ctx.enter_context(nc.psum_tensor("ps", [P, 4096], F32))
    PAIR = [PS[:, 0:1024], PS[:, 1024:2048]]
    ACC = PS[:, 2048:4096].rearrange("p (t n) -> p t n", t=TT)
    XT_PS = PS[:, 0:2048].rearrange("p (k t) -> p k t", k=KT)
    RING = sb("ring", [P, SLOTS, BLK], 0)
    WH = sb("w_high", [P, SLOTS, BLK], 16, F32R)
    WL = sb("w_low", [P, SLOTS, BLK], 32, F32R)
    XTH = sb("xT_high", [P, KT, SEQ], 48, F32R)
    XTL = sb("xT_low", [P, KT, SEQ], 56, F32R)
    IDENT = sb("ident", [P, P], 64)
    H = sb("h", [P, TT, D], 65)
    XN = sb("xn", [P, TT, D], 73)
    TMP = sb("tmp", [P, TT, D], 81)
    ROWG = sb("row_gain", [P, D], 89)
    COLS = sb("cols", [P, N_COLS], 93)
    STAT = sb("stat", [P, 64], 93.75)
    XAK = sb("xa_kT", [P, 8, SEQ], 97)
    XAV = sb("xa_v", [P, 2, TT, 512], 105)
    HTH = sb("hT_high", [P, FFN_KT, SEQ], 113, F32R)
    HTL = sb("hT_low", [P, FFN_KT, SEQ], 135, F32R)
    SG = sb("silu_gate", [P, 2, TT, 256], 157)
    HN = sb("hidden", [P, 2, TT, 256], 161)
    MEM = sb("mem_sb", [P, TT, D], 165)
    UPTO = sb("upto", [P, P], 94)
    FROM = sb("from", [P, P], 94.5)
    ONES = sb("ones", [P, P], 95)
    BEFORE = sb("before", [P, P], 95.5)
    CAP = sb("cap", [P, P], 96)
    SMALL = sb("small_row_sb", [P, 48], 96.5)
    R = sb("projections", [P, 11, 1024], 113)
    QT = R[:, 0:2, :].rearrange("p a (b t) -> p (a b) t", t=SEQ)
    KTT = R[:, 2:4, :].rearrange("p a (b t) -> p (a b) t", t=SEQ)
    V = R[:, 4:6, :].rearrange("p a (t n) -> p a t n", t=TT)
    XBC = R[:, 6:9, :].rearrange("p a (b t) -> p (a b) t", t=SEQ)
    Z = R[:, 9:11, :].rearrange("p a (t n) -> p a t n", t=TT)
    AO = sb("attention_out", [P, TT, D], 81)
    ZS = sb("scores", [P, 2, 768], 157)
    SPL = sb("softplus", [P, 2, 768], 163)
    LOGA = sb("log_attention", [P, 2, 768], 169)
    S_PS = PS[:, 2048:3072].rearrange("p (h n) -> p h n", h=2)
    C_PS = PS[:, 3072:4096].rearrange("p (h n) -> p h n", h=2)
    PE_ = sb("xa_probs", [P, TT, 4, SEQ], 157)
    PT = sb("xa_probsT", [P, 8, SEQ], 165)
    def r2(n):
        return R[:, n, :].rearrange("p (b t) -> p b t", t=SEQ)

    CG, HC, BG, Q2, F2 = (r2(n) for n in range(5))
    V2, G2 = (R[:, n, :].rearrange("p (t n) -> p t n", t=TT) for n in (5, 6))
    U = sb("conv_u", [P, 4, SEQ], 141)
    Y = sb("conv_y", [P, 4, SEQ], 145)
    MS = sb("conv_ms", [P, 4, SEQ], 149)
    FG = sb("forget", [P, 4, SEQ], 153)
    KH = sb("hg_k", [P, 4, SEQ], 157)
    GC = sb("log_decay", [P, 4, SEQ], 161)
    EG = sb("exp_decay", [P, 4, SEQ], 165)
    KD = sb("k_dec", [P, 4, SEQ], 169)
    QD = sb("q_dec", [P, 4, SEQ], 173)
    KEN = sb("k_end", [P, 4, SEQ], 177)
    KE = sb("k_end_tokens", [P, TT, 4, P], 181)
    ABD = sb("hg_scores", [P, TT, 4, P], 185)
    ST2 = sb("hg_states", [P, 7, 4, P], 189)
    GROUP64 = sb("group64", [P, P], 203)
    IN_CHUNK = sb("in_chunk", [P, P], 203.5)
    CHUNK_ON = sb("chunk_on", [P, 4 * SEQ], 85)
    LBS = sb("lower_bound", [P, 8, 4], 204)
    QP = R[:, 0:4, :].rearrange("p a (b t) -> p (a b) t", t=SEQ)
    SC = sb("key_scores", [P, TT, 16, P], 129)
    KEYS = sb("keys_sb", [P, 16, P], 145)
    TOP = sb("top", [P, TT, 16, 16], 153)
    TOP_AT = sb("top_at", [P, TT, 16, 16], 155, U32)
    TOP_ATF = sb("top_at_f", [P, TT, 16, 16], 157)
    CAND = sb("candidates", [P, TT, 8, 256], 159)
    CTOP = sb("cand_top", [P, TT, 8, 16], 175)
    CAT = sb("cand_at", [P, TT, 8, 16], 176, U32)
    CDIG = sb("cand_digits", [P, TT, 2, 128], 177, U32)
    CDIGF = sb("cand_digits_f", [P, TT, 2, 128], 179)
    HOT = sb("digit_hot", [P, 2, 128, 16], 181)
    ROUTE = sb("route", [P, TT, 3, 128], 197)
    GSUM = sb("gate_sum", [P, 16], 200)
    OA = sb("gate_at_key1", [P, 8, P], 65)
    OB = sb("one_at_key2", [P, 8, P], 69)
    ROUTE_T = sb("routeT", [P, 3, SEQ], 73)
    IOTA = sb("iota", [P, P], 76)
    GE = sb("gelu_out", [P, 1024], 65)
    WTH = sb("expert_w_high", [P, 4, SEQ], 69, F32R)
    WTL = sb("expert_w_low", [P, 4, SEQ], 73, F32R)
    GATES = sb("gates", [P, P, SEQ], 77)
    WDT = sb("w_dt_sb", [P, KT * 16], 201)
    WDTH = sb("w_dt_high", [P, KT * 16], 201.5, F32R)
    WDTL = sb("w_dt_low", [P, KT * 16], 202, F32R)
    SS = sb("ssd_small", [P, 16, 32], 202.5)
    FUTURE = sb("future", [P, P], 204.5)
    CV = sb("conv_out", [P, 12, SEQ], 157)
    XSN = sb("xs_tokens", [P, TT, D], 169)
    AU = sb("adt_upto", [P, 16, P], 177)
    LM = sb("decay", [P, 16, P], 185)
    XD = sb("xs_dt", [P, TT, D], 193)
    XDD = sb("xs_dt_decay", [P, D], 73)
    ST = sb("state", [P, D], 77)
    YS = sb("ssd_out", [P, TT, D], 177)
    BN = sb("b_tokens", [P, 2, P], 145)
    CBM = sb("cb_masked", [P, TT, 2, P], 146)

    def mixer_dst(n, dyn):
        return R[:, n, :] if dyn is None else R[:, bass.ds(dyn + n, 1), :].rearrange("p a n -> p (a n)")

    def kv_dst(n, _):
        kv = XAK[:, 4 * n:4 * n + 4, :] if n < 2 else XAV[:, n - 2, :, :]
        return kv.rearrange("p a b -> p (a b)")

    def by_head(t, k):
        return t[:, k % 2, :].rearrange("p (h n) -> p h n", h=2)

    loaded = [sem(f"loaded{i}") for i in range(SLOTS)]
    w_high, w_split, w_used = sem("w_high_done"), sem("w_split_done"), sem("w_used")
    const_in, x_in, mem_in, row_in = sem("const_in"), sem("x_in"), sem("mem_in"), sem("row_in")
    out_done = sem("out_done")
    ident_zero, ident_ok = sem("ident_zero"), sem("ident_ok")
    act_chain, dve_chain = sem("act_chain"), sem("dve_chain")
    sq_done, inv_done, rs_done = sem("square_sum"), sem("inverse_ms"), sem("rms_scale")
    xn_act, xn_dve = sem("xn_tile0"), sem("xn_tile1")
    xt_ps, xt_high, xt_low = sem("xT_psum"), sem("xT_high_done"), sem("xT_low_done")
    evac_a, evac_d = sem("evac_act"), sem("evac_dve")
    silu_done, hidden_done, ht_ps = sem("silu_done"), sem("hidden_done"), sem("hT_psum")
    ht_high, ht_low = sem("hT_high_done"), sem("hT_low_done")
    psq_done, pinv_done, prs_done = sem("post_square_sum"), sem("post_inverse"), sem("post_scale")
    h_done = sem("h_done")
    masks_one, masks_ok = sem("masks_one"), sem("masks_ok")
    sc_ps, sc_sb, abs_done, ln_done, sp_done = (sem("scores_psum"), sem("scores_copied"), sem("abs_done"),
                                                sem("ln_done"), sem("softplus_done"))
    sum_ps, loga_done, a_done, o_ps, o_done = (sem("suffix_psum"), sem("log_a_done"), sem("a_done"),
                                               sem("o_psum"), sem("o_copied"))
    wdt_high, wdt_ok, dt_ps = sem("w_dt_high_done"), sem("w_dt_split"), sem("dt_psum")
    dt_a, dt_d, conv_done, cv_done = sem("dt_act"), sem("dt_dve"), sem("conv_done"), sem("conv_silu")
    xs_ps, xs_sb, cb_ps, cb_ok = sem("xs_psum"), sem("xs_copied"), sem("cb_psum"), sem("cb_masked_done")
    acs_ps, acs_ok, au_ok, row_ps, lm_ok = (sem("a_cumsum_psum"), sem("a_cumsum_ok"), sem("adt_upto_ok"),
                                            sem("a_rows_psum"), sem("decay_exp"))
    m_ok, xd_ok, st_ps, st_ok, y_ps, y_used = (sem("m_ok"), sem("xs_dt_ok"), sem("state_psum"), sem("state_ok"),
                                       sem("y_psum"), sem("y_used"))
    hg_one, hg_ok = sem("hg_masks_one"), sem("hg_masks_ok")
    xs_sc, xs_max, xs_exp, xs_norm = sem("xa_scores"), sem("xa_max"), sem("xa_exp"), sem("xa_norm")
    xp_ps, xp_sb, xo_ps, xo_high, xo_low = (sem("xa_probsT_psum"), sem("xa_probsT_ok"), sem("xa_o_psum"),
                                            sem("xa_o_high"), sem("xa_o_low"))
    c2_d, c2_a, c2_p = sem("conv2_dve"), sem("conv2_act"), sem("conv2_pe")
    hg_d, hg_a, hg_p = sem("hg_dve"), sem("hg_act"), sem("hg_pe")
    kv_ps, s_ok = sem("kv_psum"), sem("states_ok")
    keys_in, iota_ok, injected = sem("keys_in"), sem("iota_ok"), sem("residual_in_psum")
    ks_ps, ks_sb, hot_one, hot_ok, hot_used = (
        sem("key_scores_psum"), sem("key_scores_copied"), sem("hot_one"), sem("hot_ok"), sem("hot_used"))
    gd_ok, gexp_ok, route_ok, rt_ps, rt_ok = (sem("gate_diff"), sem("gate_exp"), sem("route_ok"), sem("routeT_psum"),
                                              sem("routeT_ok"))
    eq_ok, oa_ok, ob_ok, g_ps, g_sb = sem("one_hot"), sem("one_hot_a"), sem("one_hot_b"), sem("gates_psum"), sem("gates_copied")
    gelu_ok, et_ps, prod_ok, wt_high, wt_low = (sem("gelu_done"), sem("expertsT_psum"), sem("weighted"),
                                                sem("weighted_high"), sem("weighted_low"))
    final_ok = sem("final_ok")
    yz_ok, z_silu, y_done = sem("yz_ok"), sem("z_silu"), sem("y_done")

    block = ctx.enter_context(nc.Block())

    @block.sync
    def _(sp):
        sp.dma_start(MEM[:], mem.rearrange("(t p) d -> p t d", p=P)).then_inc(mem_in, 16)
        sp.dma_start(COLS[:], cols).then_inc(const_in, 16)
        sp.dma_start(WDT[:], w_dt).then_inc(const_in, 16)
        sp.dma_start(SMALL[:], small_row[0].partition_broadcast(P)).then_inc(const_in, 16)
        for n in range(SLOTS):
            sp.dma_start(RING[:, n, :], stream[n]).then_inc(loaded[n], 16)
        sp.dma_start(H[:], x.rearrange("(t p) d -> p t d", p=P)).then_inc(x_in, 16)
        with sp.Fori(1, N_BLOCKS // SLOTS) as i:
            for j in range(SLOTS):
                sp.wait_ge(w_split, i * SLOTS + (j - SLOTS + 1))
                sp.dma_start(RING[:, j, :], stream[bass.ds(i * SLOTS + j, 1)].rearrange("a p c -> (a p) c")
                             ).then_inc(loaded[j], 16)
        sp.wait_ge(final_ok, 2)
        sp.dma_start(out.rearrange("(t p) d -> p t d", p=P), TMP[:]).then_inc(out_done, 16)
        sp.wait_ge(out_done, 16)

    @block.gpsimd
    def _(pool):
        pool.memset(IDENT[:], 0.0).then_inc(ident_zero, 1)
        pool.wait_ge(ident_zero, 1)
        pool.affine_select(out=IDENT[:], in_=IDENT[:], compare_op=ALU.not_equal, fill=1.0, base=0,
                           pattern=[[-1, P]], channel_multiplier=1).then_inc(ident_ok, 1)
        pool.dma_start(ROWG[:], rows[0].partition_broadcast(P)).then_inc(row_in, 16)
        for mask in (UPTO, FROM, BEFORE, CAP, ONES):
            pool.memset(mask[:], 1.0).then_inc(masks_one, 1)
        pool.memset(FUTURE[:], 0.0).then_inc(masks_one, 1)
        pool.wait_ge(masks_one, 6)
        for mask, sign, compare, fill in ((UPTO, 1, ALU.is_ge, 0.0), (FROM, -1, ALU.is_ge, 0.0),
                                          (BEFORE, 1, ALU.is_gt, 0.0), (CAP, 1, ALU.is_gt, -1e30),
                                          (FUTURE, 1, ALU.is_ge, -1e30)):
            pool.affine_select(out=mask[:], in_=mask[:], compare_op=compare, fill=fill, base=0,
                               pattern=[[sign, P]], channel_multiplier=-sign).then_inc(masks_ok, 1)

        def row_gain(k):
            pool.wait_ge(h_done, 2 * k)
            pool.dma_start(ROWG[:], rows[k].partition_broadcast(P)).then_inc(row_in, 16)

        def per_head(dst, src, heads):
            return pool.tensor_tensor(dst.rearrange("p (h d) -> p h d", d=64), src.rearrange("p (h d) -> p h d", d=64),
                                      heads.unsqueeze(2).to_broadcast([P, 16, 64]), ALU.mult)

        def ssd():
            pool.wait_ge(dt_d, 3)
            for tt in range(TT):
                if tt:
                    pool.wait_ge(row_ps, 1)
                pool.tensor_tensor(AU[:], SS[:, 12, tt * 16:tt * 16 + 16].unsqueeze(2).to_broadcast([P, 16, P]),
                                   UPTO[:].unsqueeze(1).to_broadcast([P, 16, P]), ALU.mult).then_inc(au_ok, 1)
                pool.wait_ge(xs_sb, 2 * (tt + 1))
                per_head(XD[:, tt, :], XSN[:, tt, :], SS[:, 10, tt * 16:tt * 16 + 16]).then_inc(xd_ok, 1)
                if tt == 0:
                    pool.wait_ge(dt_a, 4)
                    pool.wait_ge(xd_ok, 1)
                    per_head(XDD[:], XD[:, 0, :], SS[:, 15, 0:16]).then_inc(xd_ok, 1)
            pool.wait_ge(row_ps, 2)
            for tt in range(TT):
                per_head(YS[:, tt, :], XSN[:, tt, :], SMALL[:, 32:48]).then_inc(yz_ok, 1)

        row_gain(1)
        ssd()
        row_gain(2)
        row_gain(3)
        pool.wait_ge(h_done, 8)
        pool.memset(CHUNK_ON[:], 1.0).then_inc(hg_one, 1)
        pool.memset(ABD[:], 0.0).then_inc(hg_one, 1)
        pool.memset(GROUP64[:], 1.0 / 64).then_inc(hg_one, 1)
        pool.tensor_copy(IN_CHUNK[:], UPTO[:]).then_inc(hg_one, 1)
        pool.wait_ge(hg_one, 4)
        pool.memset(CHUNK_ON[:].rearrange("p (n c) -> p n c", c=HG_CHUNK)[:, :, 0:1], 0.0).then_inc(hg_ok, 1)
        pool.affine_select(out=IN_CHUNK[:], in_=IN_CHUNK[:], compare_op=ALU.is_ge, fill=0.0, base=0,
                           pattern=[[-HG_CHUNK, 4], [0, HG_CHUNK]], channel_multiplier=1).then_inc(hg_ok, 1)
        pool.affine_select(out=GROUP64[:], in_=GROUP64[:], compare_op=ALU.is_ge, fill=0.0, base=0,
                           pattern=[[-64, 2], [0, 64]], channel_multiplier=1).then_inc(hg_ok, 1)
        pool.wait_ge(hg_ok, 3)
        pool.affine_select(out=GROUP64[:], in_=GROUP64[:], compare_op=ALU.is_ge, fill=0.0, base=63,
                           pattern=[[64, 2], [0, 64]], channel_multiplier=-1).then_inc(hg_ok, 1)
        pool.wait_ge(h_done, 10)
        pool.dma_start(KEYS[:], keys).then_inc(keys_in, 16)
        pool.wait_ge(xt_ps, 4 * 9)
        pool.iota(IOTA[:], pattern=[[1, P]], base=0, channel_multiplier=0,
                  allow_small_or_imprecise_dtypes=True).then_inc(iota_ok, 1)
        pool.wait_ge(iota_ok, 1)
        for tt in range(TT):
            for p in range(2):
                pool.wait_ge(hot_one, 2 * tt + p + 1)
                hot = HOT[:, p, :, :].rearrange("p (h k) j -> p h k j", h=8)
                pool.tensor_tensor(hot, hot, TOP_ATF[:, tt, p:16:2, :].unsqueeze(2).to_broadcast([P, 8, 16, 16]),
                                   ALU.mult).then_inc(hot_ok, 1)

        def weigh_hot(q, group, dyn=None):
            pool.wait_ge(eq_ok, at(group + 1, dyn))
            t = at(4 * group, dyn, 4)
            t = bass.ds(t, 4) if dyn is not None else slice(t, t + 4)
            o = OA[:, 4 * q:4 * q + 4, :]
            pool.tensor_tensor(o, o, ROUTE_T[:, 2, t].unsqueeze(2).to_broadcast([P, 4, P]), ALU.mult).then_inc(oa_ok, 1)

        weigh_hot(0, 0)
        weigh_hot(1, 1)
        with pool.Fori(1, 32) as i:
            weigh_hot(0, 0, i * 2)
            weigh_hot(1, 1, i * 2)
        pool.wait_ge(prod_ok, 32)
        pool.dma_start(ROWG[:], rows[4].partition_broadcast(P)).then_inc(row_in, 16)

    @block.scalar
    def _(act):
        chain = Chain(act, act_chain)

        def split(n0, count, dyn=None):
            for n in range(n0, n0 + count):
                act.wait_ge(loaded[n % SLOTS], at(16 * (n // SLOTS + 1), dyn, 16 // SLOTS))
                if dyn is not None or n >= SLOTS:
                    act.wait_ge(w_used, at(n - SLOTS + 1, dyn))
                act.activation(WH[:, n % SLOTS, :], RING[:, n % SLOTS, :], ACT.Copy).then_inc(w_high, 1)

        def split_run(n0, count):
            groups = count // SLOTS
            if groups > 1:
                with act.Fori(0, groups) as i:
                    split(n0, SLOTS, i * SLOTS)
            else:
                groups = 0
            split(n0 + groups * SLOTS, count - groups * SLOTS)

        def prenorm(k, src, gain, high=XTH, k0=0, groups=1, updates=None):
            w = D // groups
            for tt in range(TT):
                if updates is not None:
                    act.wait_ge(h_done, updates + tt + 1)
                for g in range(groups):
                    n = tt * groups + g
                    act.activation(XN[:, tt, g * w:g * w + w], src[:, tt, g * w:g * w + w], ACT.Square,
                                   accum_out=STAT[:, n:n + 1]).then_inc(sq_done, 1)
            act.wait_ge(inv_done, k + 1)
            n = TT * groups
            chain(act.activation(STAT[:, 8:8 + n], STAT[:, 4:4 + n], ACT.Sqrt))
            act.activation(STAT[:, 12:12 + n], STAT[:, 8:8 + n], ACT.Copy).then_inc(rs_done, 1)
            for g in range(groups):
                last = act.activation(XN[:, 0, g * w:g * w + w], src[:, 0, g * w:g * w + w], ACT.Copy,
                                      scale=STAT[:, 8 + g:9 + g])
            last.then_inc(xn_act, 1)
            for kt in range(KT):
                act.wait_ge(xt_ps, k * KT // 2 + kt // 2 + 1)
                act.activation(high[:, k0 + kt, :], XT_PS[:, kt, :], ACT.Copy,
                               scale=COLS[:, GAIN_COL[gain] + kt:GAIN_COL[gain] + kt + 1]).then_inc(xt_high, 1)

        def evac(stage, dst, n, parity, dyn=None):
            act.wait_ge(w_used, at(BASE[stage] + PB * (n + 1), dyn, PB))
            act.activation(dst(n, dyn)[:, 0:512], PAIR[parity][:, 0:512], ACT.Copy).then_inc(evac_a, 1)

        def ffn_up(stage, f):
            b, e = BASE[stage], f * FFN_PANELS

            def silu(p, parity, dyn=None):
                act.wait_ge(w_used, at(b + PB * (p + 1), dyn, PB))
                if dyn is not None or e + p >= 2:
                    act.wait_ge(hidden_done, at(e + p - 1, dyn))
                act.activation(SG[:, parity, :, :],
                               PAIR[parity].rearrange("p (t n) -> p t n", t=TT)[:, :, 0:256],
                               ACT.Silu).then_inc(silu_done, 1)

            def high(p, parity, dyn=None):
                act.wait_ge(ht_ps, at(e + p + 1, dyn))
                act.activation(HTH[:, bass.ds(at(2 * p, dyn, 2), 2), :] if dyn is not None
                               else HTH[:, 2 * p:2 * p + 2, :],
                               ACC[:, 0, 512 * parity:512 * parity + 512].rearrange("p (k t) -> p k t", k=2),
                               ACT.Copy).then_inc(ht_high, 1)

            split(b + PB, PB)
            silu(0, 0)
            with act.Fori(0, (FFN_PANELS - 3) // 2) as i:
                for p in (2, 3):
                    split(b + PB * p, PB, i * (2 * PB))
                    silu(p - 1, (p - 1) % 2, i * 2)
                    high(p - 2, p % 2, i * 2)
            p = FFN_PANELS - 1
            split(b + PB * p, PB)
            silu(p - 1, (p - 1) % 2)
            high(p - 2, p % 2)
            split(b + PB * FFN_PANELS, PB)
            silu(p, p % 2)
            high(p - 1, (p - 1) % 2)
            high(p, p % 2)

        def post_square(k):
            for tt in range(TT):
                act.activation(XN[:, tt, :], ACC[:, tt, :], ACT.Square,
                               accum_out=STAT[:, 16 + tt:17 + tt]).then_inc(psq_done, 1)
            act.wait_ge(pinv_done, k + 1)
            act.activation(STAT[:, 20:22], STAT[:, 18:20], ACT.Sqrt).then_inc(prs_done, 1)

        def plain(stage, panels, dst):
            b = BASE[stage]
            for n in range(1, panels):
                split(b + PB * n, PB)
                evac(stage, dst, n - 1, (n - 1) % 2)
            split(b + PB * panels, PB)
            evac(stage, dst, panels - 1, (panels - 1) % 2)

        split(0, PB)
        act.wait_ge(const_in, 48)
        act.activation(WDTH[:], WDT[:], ACT.Copy).then_inc(wdt_high, 1)
        act.wait_ge(mem_in, 16)
        prenorm(0, MEM, "mem")
        plain("xa_kv", 4, kv_dst)
        act.wait_ge(x_in, 16)
        prenorm(1, H, "ffn1")
        ffn_up("ffn1_up", 0)
        split_run(BASE["ffn1_down"] + PB, FFN_KT)
        act.wait_ge(w_used, BASE["w_in"])
        post_square(0)

        def attention_half(k):
            if k < 8:
                act.wait_ge(sc_ps, k + 1)
                if k >= 2:
                    act.wait_ge(sp_done, k - 1)
                    act.wait_ge(loga_done, k - 1)
                act.activation(by_head(ZS, k), S_PS[:, :, 0:384], ACT.Copy, scale=0.125).then_inc(sc_sb, 1)
                act.wait_ge(abs_done, k + 1)
                if k >= 2:
                    act.wait_ge(sum_ps, k - 1)
                chain(act.activation(SPL[:, k % 2, :], SPL[:, k % 2, :], ACT.Exp))
                act.activation(SPL[:, k % 2, :], SPL[:, k % 2, :], ACT.Ln, bias=1.0).then_inc(ln_done, 1)
            if 1 <= k <= 8:
                act.wait_ge(loga_done, k)
                act.activation(LOGA[:, (k - 1) % 2, :], LOGA[:, (k - 1) % 2, :], ACT.Exp).then_inc(a_done, 1)
            if k >= 2:
                act.wait_ge(o_ps, k - 1)
                act.activation(AO[:, :, (k - 2) * P:(k - 1) * P].rearrange("p t (h n) -> p h t n", h=2),
                               C_PS[:, :, 384:512].rearrange("p h (t n) -> p h t n", t=TT), ACT.Copy).then_inc(o_done, 1)

        prenorm(2, H, "mix", updates=0)
        b = BASE["w_in"]
        with act.Fori(0, 3) as i:
            for p in (0, 1):
                split(b + PB * (p + 1), PB, i * (2 * PB))
                evac("w_in", mixer_dst, p, p, i * 2)
        act.preload_act_table_set("natural_log_exp_and_others")
        for k in range(10):
            attention_half(k)
            split(b + PB * 7 + 2 * k, 2)
            if k % 2:
                evac("w_in", mixer_dst, 6 + k // 2, (k // 2) % 2)
        act.activation(SS[:, 11, 0:16], SMALL[:, 16:32], ACT.Exp).then_inc(dt_a, 1)
        act.wait_ge(dt_d, 1)
        act.activation(SS[:, 2, :], SS[:, 1, :], ACT.Exp).then_inc(dt_a, 1)
        act.wait_ge(dt_d, 2)
        act.activation(SS[:, 4, :], SS[:, 3, :], ACT.Ln).then_inc(dt_a, 1)
        act.wait_ge(acs_ok, 1)
        act.activation(SS[:, 15, 0:16], SS[:, 14, 0:16], ACT.Exp)
        act.activation(SS[:, 15, 16:32], SS[:, 13, 16:32], ACT.Exp, scale=-1.0).then_inc(dt_a, 1)
        for b3 in range(3):
            act.wait_ge(conv_done, 4 * (b3 + 1))
            act.activation(CV[:, 4 * b3:4 * b3 + 4, :], CV[:, 4 * b3:4 * b3 + 4, :], ACT.Silu).then_inc(cv_done, 1)
        act.wait_ge(evac_d, EVAC["w_in"] + 11)
        act.wait_ge(evac_a, EVAC["w_in"] + 11)
        act.activation(Z, Z, ACT.Silu).then_inc(z_silu, 1)
        for tt in range(TT):
            act.wait_ge(xs_ps, tt + 1)
            act.activation(XSN[:, tt, 0:512], PS[:, 0:512], ACT.Copy).then_inc(xs_sb, 1)
            act.wait_ge(row_ps, tt + 1)
            if tt:
                act.wait_ge(y_ps, 1)
            for h in range(16):
                last = act.activation(LM[:, h, :], PS[:, 2048 + h * P:2048 + (h + 1) * P], ACT.Exp,
                                      bias=SS[:, 13, tt * 16 + h:tt * 16 + h + 1])
            last.then_inc(lm_ok, 1)
            if tt == 0:
                act.wait_ge(st_ps, 1)
                act.activation(ST[:], PS[:, 1024:2048], ACT.Copy).then_inc(st_ok, 1)
        act.wait_ge(y_done, 2)
        prenorm(3, AO, "attn", HTH)
        prenorm(4, YS, "ssd", HTH, 8, groups=2)
        split_run(BASE["w_out"] + PB, 16)
        act.wait_ge(w_used, BASE["xa_q"])
        post_square(1)
        prenorm(5, H, "xa", updates=2)
        plain("xa_q", 2, mixer_dst)
        for tt in range(TT):
            act.wait_ge(xs_max, tt + 1)
            for h in range(4):
                n = tt * 4 + h
                last = act.activation(PE_[:, tt, h, :], ACC[:, tt, h * SEQ:(h + 1) * SEQ], ACT.Exp, scale=1.0 / 16,
                                      bias=STAT[:, 32 + n:33 + n], accum_out=STAT[:, 40 + n:41 + n])
            last.then_inc(xs_exp, 1)
        act.wait_ge(xp_ps, 1)
        act.activation(PT[:, 0:4, :], XT_PS[:, 0:4, :], ACT.Copy).then_inc(xp_sb, 1)
        for bank in range(4):
            act.wait_ge(xo_ps, bank + 1)
            act.activation(HTH[:, 2 * bank:2 * bank + 2, :],
                           PS[:, 2048 + bank * 512:2560 + bank * 512].rearrange("p (k t) -> p k t", k=2),
                           ACT.Copy).then_inc(xo_high, 1)
        split_run(BASE["xa_o"] + PB, 8)
        act.wait_ge(w_used, BASE["ffn2_up"])
        post_square(2)
        prenorm(6, H, "ffn2", updates=4)
        ffn_up("ffn2_up", 1)
        split_run(BASE["ffn2_down"] + PB, FFN_KT)
        act.wait_ge(w_used, BASE["w_in_2"])
        post_square(3)
        prenorm(7, H, "mix2", updates=6)
        plain("w_in_2", 7, mixer_dst)
        act.wait_ge(evac_a, EVAC["w_in_2"] + 7)
        act.wait_ge(evac_d, EVAC["w_in_2"] + 7)
        act.wait_ge(hg_d, 1)
        act.activation(LBS[:, 2:4, :], LBS[:, 0:2, :], ACT.Exp).then_inc(hg_a, 1)
        act.activation(FG[:], F2, ACT.Sigmoid).then_inc(hg_a, 1)
        act.activation(Q2, Q2, ACT.Silu)
        act.activation(G2, G2, ACT.Silu).then_inc(hg_a, 1)
        act.preload_act_table_set("natural_log_exp_and_others")
        act.wait_ge(hg_d, 2)
        act.activation(GC[:], FG[:], ACT.Ln).then_inc(hg_a, 1)
        act.wait_ge(hg_d, 3)
        act.activation(EG[:], GC[:], ACT.Exp).then_inc(hg_a, 1)
        act.activation(KD[:], GC[:], ACT.Exp, scale=-1.0).then_inc(hg_a, 1)
        act.wait_ge(hg_d, 4)
        act.activation(KEN[:], KEN[:], ACT.Exp).then_inc(hg_a, 1)
        act.wait_ge(c2_d, 1)
        act.activation(MS[:], Y[:], ACT.Square).then_inc(c2_a, 1)
        act.wait_ge(hg_p, 1)
        act.activation(KE[:].rearrange("p t h n -> p (t h n)"), PS[:, 0:1024], ACT.Copy).then_inc(hg_a, 1)
        act.wait_ge(kv_ps, 1)
        act.activation(ST2[:, 0, :, :].rearrange("p h n -> p (h n)"), PS[:, 2048:2560], ACT.Copy).then_inc(s_ok, 1)
        act.wait_ge(c2_d, 2)
        act.activation(MS[:], MS[:], ACT.Sqrt).then_inc(c2_a, 1)
        act.wait_ge(c2_d, 3)
        act.activation(XTH[:, 0:4, :], Y[:], ACT.Copy).then_inc(c2_a, 1)
        act.wait_ge(hg_p, 4)
        for n in range(8):
            last = act.activation(U[:, n // 2, n % 2 * P:n % 2 * P + P], PS[:, n * P:(n + 1) * P], ACT.Square, accum_out=STAT[:, 32 + n:33 + n])
        last.then_inc(hg_a, 1)
        act.wait_ge(hg_d, 8)
        act.activation(STAT[:, 48:56], STAT[:, 40:48], ACT.Sqrt).then_inc(hg_a, 1)
        act.wait_ge(hg_p, 5)
        act.activation(XTH[:, 4:8, :], XT_PS[:, 4:8, :], ACT.Copy, scale=COLS[:, HG_GAIN:HG_GAIN + 1]).then_inc(hg_a, 1)
        split_run(BASE["w_out_2"] + PB, 8)

        prenorm(8, H, "peer", updates=8)
        plain("peer_q", 4, mixer_dst)
        for tt in range(TT):
            act.wait_ge(ks_ps, tt + 1)
            act.activation(SC[:, tt, :, :].rearrange("p a n -> p (a n)"), PS[:, 0:2048], ACT.Copy).then_inc(ks_sb, 1)
        for tt in range(TT):
            act.wait_ge(gd_ok, tt + 1)
            act.activation(CTOP[:, tt, :, :], CTOP[:, tt, :, :], ACT.Exp).then_inc(gexp_ok, 1)

        def route_copy(tt):
            act.wait_ge(rt_ps, tt + 1)
            act.activation(ROUTE_T[:, :, tt * P:(tt + 1) * P], PS[:, 1024:1408].rearrange("p (a n) -> p a n", a=3),
                           ACT.Copy).then_inc(rt_ok, 1)

        def gates_copy(q, group, dyn=None):
            act.wait_ge(g_ps, at(group + 1, dyn))
            t = bass.ds(at(4 * group, dyn, 4), 4) if dyn is not None else slice(4 * group, 4 * group + 4)
            act.activation(GATES[:, :, t], PS[:, 512 * q:512 * q + 512].rearrange("p (t n) -> p n t", t=4),
                           ACT.Copy).then_inc(g_sb, 1)

        route_copy(0)
        route_copy(1)
        gates_copy(0, 0)
        gates_copy(1, 1)
        with act.Fori(1, 32) as i:
            gates_copy(0, 0, i * 2)
            gates_copy(1, 1, i * 2)

        def gelu(s, used, dyn=None):
            act.wait_ge(w_used, used if dyn is None else dyn * 8 + used)
            if dyn is not None:
                act.wait_ge(wt_low, dyn * 1)
            act.activation(GE[:], PAIR[0], ACT.Gelu).then_inc(gelu_ok, 1)

        def weighted_high(s, dyn=None):
            act.wait_ge(prod_ok, at(s + 1, dyn))
            act.activation(WTH[:].rearrange("p a t -> p (a t)"), GE[:], ACT.Copy).then_inc(wt_high, 1)

        b = BASE["peer"]
        gelu(0, b + PB)
        split(b + PB, PB)
        weighted_high(0)
        with act.Fori(1, 32) as i:
            split(b, PB, i * 8)
            gelu(0, b, i)
            split(b + PB, PB, i * 8)
            weighted_high(0, i)
        act.wait_ge(w_used, N_BLOCKS)
        post_square(4)

    @block.vector
    def _(dve):
        chain = Chain(dve, dve_chain)

        def split(n0, count, dyn=None):
            for n in range(n0, n0 + count):
                dve.wait_ge(w_high, at(n + 1, dyn))
                dve.tensor_tensor(WL[:, n % SLOTS, :], RING[:, n % SLOTS, :],
                                  WH[:, n % SLOTS, :].bitcast(F32), ALU.subtract).then_inc(w_split, 1)

        def split_run(n0, count):
            groups = count // SLOTS
            if groups > 1:
                with dve.Fori(0, groups) as i:
                    split(n0, SLOTS, i * SLOTS)
            else:
                groups = 0
            split(n0 + groups * SLOTS, count - groups * SLOTS)

        def inverse(src, dst, width=D):
            chain(dve.tensor_scalar(dst, src, 1.0 / width, EPS, ALU.mult, ALU.add))
            return dve.reciprocal(dst, dst)

        def prenorm(k, src, gain, high=XTH, low=XTL, k0=0, groups=1):
            n, w = TT * groups, D // groups
            dve.wait_ge(sq_done, SQUARES[k + 1])
            inverse(STAT[:, 0:n], STAT[:, 4:4 + n], w).then_inc(inv_done, 1)
            dve.wait_ge(rs_done, k + 1)
            for g in range(groups):
                last = dve.tensor_scalar(XN[:, 1, g * w:g * w + w], src[:, 1, g * w:g * w + w],
                                         STAT[:, 12 + groups + g:13 + groups + g], None, ALU.mult)
            last.then_inc(xn_dve, 1)
            for kt in range(KT):
                dve.wait_ge(xt_high, k * KT + (kt | 1) + 1)
                dve.scalar_tensor_tensor(low[:, k0 + kt, :], XT_PS[:, kt, :],
                                         COLS[:, GAIN_COL[gain] + kt:GAIN_COL[gain] + kt + 1],
                                         high[:, k0 + kt, :].bitcast(F32), ALU.mult, ALU.subtract).then_inc(xt_low, 1)

        def evac(stage, dst, n, parity, dyn=None):
            dve.wait_ge(w_used, at(BASE[stage] + PB * (n + 1), dyn, PB))
            dve.tensor_copy(dst(n, dyn)[:, 512:1024], PAIR[parity][:, 512:1024]).then_inc(evac_d, 1)

        def ffn_up(stage, f):
            b, e = BASE[stage], f * FFN_PANELS

            def hidden(p, parity, dyn=None):
                dve.wait_ge(silu_done, at(e + p + 1, dyn))
                if dyn is not None or e + p >= 2:
                    dve.wait_ge(ht_ps, at(e + p - 1, dyn))
                dve.tensor_tensor(HN[:, parity, :, :], SG[:, parity, :, :],
                                  PAIR[parity].rearrange("p (t n) -> p t n", t=TT)[:, :, 256:512],
                                  ALU.mult).then_inc(hidden_done, 1)

            def low(p, parity, dyn=None):
                dve.wait_ge(ht_high, at(e + p + 1, dyn))
                w = bass.ds(at(2 * p, dyn, 2), 2) if dyn is not None else slice(2 * p, 2 * p + 2)
                dve.tensor_tensor(HTL[:, w, :],
                                  ACC[:, 0, 512 * parity:512 * parity + 512].rearrange("p (k t) -> p k t", k=2),
                                  HTH[:, w, :].bitcast(F32), ALU.subtract).then_inc(ht_low, 1)

            split(b + PB, PB)
            hidden(0, 0)
            with dve.Fori(0, (FFN_PANELS - 3) // 2) as i:
                for p in (2, 3):
                    split(b + PB * p, PB, i * (2 * PB))
                    hidden(p - 1, (p - 1) % 2, i * 2)
                    low(p - 2, p % 2, i * 2)
            p = FFN_PANELS - 1
            split(b + PB * p, PB)
            hidden(p - 1, (p - 1) % 2)
            low(p - 2, p % 2)
            split(b + PB * FFN_PANELS, PB)
            hidden(p, p % 2)
            low(p - 1, (p - 1) % 2)
            low(p, p % 2)

        def post_add(k, factor):
            dve.wait_ge(psq_done, 2 * (k + 1))
            inverse(STAT[:, 16:18], STAT[:, 18:20]).then_inc(pinv_done, 1)
            dve.wait_ge(prs_done, k + 1)
            dve.wait_ge(row_in, 16 * (k + 1))
            for tt in range(TT):
                chain(dve.scalar_tensor_tensor(TMP[:, tt, :], ACC[:, tt, :], STAT[:, 20 + tt:21 + tt],
                                               ROWG[:], ALU.mult, ALU.mult))
                dve.scalar_tensor_tensor(H[:, tt, :], TMP[:, tt, :], factor, H[:, tt, :],
                                         ALU.mult, ALU.add).then_inc(h_done, 1)

        def plain(stage, panels, dst):
            b = BASE[stage]
            for n in range(1, panels):
                split(b + PB * n, PB)
                evac(stage, dst, n - 1, (n - 1) % 2)
            split(b + PB * panels, PB)
            evac(stage, dst, panels - 1, (panels - 1) % 2)

        split(0, PB)
        dve.wait_ge(const_in, 48)
        dve.wait_ge(wdt_high, 1)
        dve.tensor_tensor(WDTL[:], WDT[:], WDTH[:].bitcast(F32), ALU.subtract).then_inc(wdt_ok, 1)
        dve.wait_ge(mem_in, 16)
        prenorm(0, MEM, "mem")
        plain("xa_kv", 4, kv_dst)
        dve.wait_ge(x_in, 16)
        prenorm(1, H, "ffn1")
        ffn_up("ffn1_up", 0)
        split_run(BASE["ffn1_down"] + PB, FFN_KT)
        post_add(0, 0.5)

        def diagonals(t, k):
            return t[:, k % 2, :].rearrange("p (h x n) -> p h x n", h=2, x=3)[:, :, 0:3:2, :]

        def over_diagonals(mask):
            return mask[:].unsqueeze(1).unsqueeze(1).to_broadcast([P, 2, 2, P])

        def attention_half(k):
            if k < 8:
                dve.wait_ge(sc_sb, k + 1)
                if k >= 2:
                    dve.wait_ge(sum_ps, k - 1)
                dve.scalar_tensor_tensor(SPL[:, k % 2, :], ZS[:, k % 2, :], -1.0, ZS[:, k % 2, :],
                                         ALU.mult, ALU.min).then_inc(abs_done, 1)
                dve.wait_ge(ln_done, k + 1)
                chain(dve.scalar_tensor_tensor(SPL[:, k % 2, :], ZS[:, k % 2, :], 0.0, SPL[:, k % 2, :],
                                               ALU.max, ALU.add))
                dve.tensor_tensor(diagonals(SPL, k), diagonals(SPL, k), over_diagonals(BEFORE),
                                  ALU.mult).then_inc(sp_done, 1)
            if 1 <= k <= 8:
                j = k - 1
                dve.wait_ge(sum_ps, k)
                if j >= 1:
                    dve.wait_ge(o_ps, j)
                if j >= 2:
                    dve.wait_ge(o_ps, j - 1)
                chain(dve.tensor_tensor(by_head(LOGA, j), by_head(ZS, j), C_PS[:, :, 0:384], ALU.subtract))
                dve.tensor_tensor(diagonals(LOGA, j), diagonals(LOGA, j), over_diagonals(CAP),
                                  ALU.min).then_inc(loga_done, 1)

        dve.wait_ge(h_done, 2)
        prenorm(2, H, "mix")
        b = BASE["w_in"]
        with dve.Fori(0, 3) as i:
            for p in (0, 1):
                split(b + PB * (p + 1), PB, i * (2 * PB))
                evac("w_in", mixer_dst, p, p, i * 2)
        dve.wait_ge(masks_ok, 5)
        for k in range(10):
            attention_half(k)
            split(b + PB * 7 + 2 * k, 2)
            if k % 2:
                evac("w_in", mixer_dst, 6 + k // 2, (k // 2) % 2)

        def both(heads):
            return heads.unsqueeze(1).to_broadcast([P, TT, 16])

        def two(row):
            return SS[:, row, :].rearrange("p (t h) -> p t h", t=TT)

        dve.wait_ge(dt_ps, 1)
        chain(dve.tensor_tensor(two(0), PS[:, 1024:1056].rearrange("p (t h) -> p t h", t=TT),
                                both(SMALL[:, 0:16]), ALU.add))
        dve.scalar_tensor_tensor(SS[:, 1, :], SS[:, 0, :], -1.0, SS[:, 0, :], ALU.mult, ALU.min).then_inc(dt_d, 1)
        dve.wait_ge(dt_a, 2)
        chain(dve.tensor_scalar(SS[:, 3, :], SS[:, 2, :], 1.0, None, ALU.add))
        dve.tensor_scalar(SS[:, 6, :], SS[:, 3, :], -1.0, 1e-30, ALU.add, ALU.add).then_inc(dt_d, 1)
        dve.wait_ge(dt_d, 2)
        chain(dve.reciprocal(SS[:, 7, :], SS[:, 6, :]))
        dve.wait_ge(dt_a, 3)
        chain(dve.scalar_tensor_tensor(SS[:, 8, :], SS[:, 4, :], 1e-30, SS[:, 7, :], ALU.add, ALU.mult))
        chain(dve.tensor_tensor(SS[:, 9, :], SS[:, 8, :], SS[:, 2, :], ALU.mult))
        chain(dve.scalar_tensor_tensor(SS[:, 10, :], SS[:, 0, :], 0.0, SS[:, 9, :], ALU.max, ALU.add))
        dve.scalar_tensor_tensor(two(12), two(10), -1.0, both(SS[:, 11, 0:16]), ALU.mult, ALU.mult
                                 ).then_inc(dt_d, 1)
        dve.wait_ge(acs_ps, 1)
        chain(dve.tensor_scalar(SS[:, 13, :], PS[:, 1088:1120], -1.0, None, ALU.mult))
        dve.tensor_tensor(SS[:, 14, 0:16], PS[:, 1120:1136], SS[:, 13, 0:16], ALU.add).then_inc(acs_ok, 1)
        dve.wait_ge(evac_a, EVAC["w_in"] + 9)
        with dve.Fori(0, 12) as i:
            tile, x = CV[:, bass.ds(i, 1), :], XBC[:, bass.ds(i, 1), :]
            tile, x = tile.rearrange("p a t -> p (a t)"), x.rearrange("p a t -> p (a t)")
            tap = [COLS[:, bass.ds(i * 4 + (CONV_W + j), 1)] for j in range(4)]
            chain.enter(i, 3)
            chain(dve.tensor_scalar(tile, x, tap[3], COLS[:, bass.ds(i + CONV_B, 1)], ALU.mult, ALU.add))
            for back in (1, 2):
                chain(dve.scalar_tensor_tensor(tile[:, back:], x[:, :SEQ - back], tap[3 - back], tile[:, back:],
                                               ALU.mult, ALU.add))
            dve.scalar_tensor_tensor(tile[:, 3:], x[:, :SEQ - 3], tap[0], tile[:, 3:],
                                     ALU.mult, ALU.add).then_inc(conv_done, 1)
            chain.leave(12)
        dve.wait_ge(cb_ps, 1)
        dve.tensor_copy(BN[:], PS[:, 1152:1408].rearrange("p (g n) -> p g n", g=2)).then_inc(cb_ok, 1)
        dve.tensor_tensor(CBM[:].rearrange("p t g n -> p (t g) n"), PS[:, 1536:2048].rearrange("p (a n) -> p a n", a=4),
                          UPTO[:].unsqueeze(1).to_broadcast([P, 4, P]), ALU.mult).then_inc(cb_ok, 1)
        dve.wait_ge(cb_ok, 2)
        for tt in range(TT):
            dve.wait_ge(xs_ps, tt + 1)
            dve.tensor_copy(XSN[:, tt, 512:1024], PS[:, 512:1024]).then_inc(xs_sb, 1)
        for tt in range(TT):
            dve.wait_ge(lm_ok, tt + 1)
            for g in range(2):
                m = LM[:, 8 * g:8 * g + 8, :]
                last = dve.tensor_tensor(m, m, CBM[:, tt, g, :].unsqueeze(1).to_broadcast([P, 8, P]), ALU.mult)
            last.then_inc(m_ok, 1)
            dve.wait_ge(y_ps, tt + 1)
            dve.wait_ge(yz_ok, tt + 1)
            y = YS[:, tt, :]
            chain(dve.tensor_tensor(y, y, PS[:, 0:1024], ALU.add))
            if tt:
                chain(dve.tensor_tensor(XDD[:].rearrange("p (h d) -> p h d", d=64),
                                        PS[:, 1024:2048].rearrange("p (h d) -> p h d", d=64),
                                        SS[:, 15, 16:32].unsqueeze(2).to_broadcast([P, 16, 64]), ALU.mult))
                chain(dve.tensor_tensor(y, y, XDD[:], ALU.add))
            dve.wait_ge(z_silu, 1)
            dve.tensor_tensor(y.rearrange("p (a n) -> p a n", a=2), y.rearrange("p (a n) -> p a n", a=2),
                              Z[:, :, tt, :], ALU.mult).then_inc(y_done, 1)
        dve.wait_ge(y_done, 2)
        prenorm(3, AO, "attn", HTH, HTL)
        prenorm(4, YS, "ssd", HTH, HTL, 8, groups=2)
        split_run(BASE["w_out"] + PB, 16)
        post_add(1, 1.0)
        prenorm(5, H, "xa")
        plain("xa_q", 2, mixer_dst)
        for tt in range(TT):
            dve.wait_ge(xs_sc, tt + 1)
            s = slice(tt * 4, tt * 4 + 4)
            chain(dve.reduce_max(STAT[:, 24:32][:, s], ACC[:, tt, :].rearrange("p (h m) -> p h m", h=4), AX_X))
            dve.tensor_scalar(STAT[:, 32:40][:, s], STAT[:, 24:32][:, s], -1.0 / 16, None, ALU.mult).then_inc(xs_max, 1)
        for tt in range(TT):
            dve.wait_ge(xs_exp, tt + 1)
            s = slice(tt * 4, tt * 4 + 4)
            chain(dve.reciprocal(STAT[:, 48:56][:, s], STAT[:, 40:48][:, s]))
            dve.tensor_tensor(PE_[:, tt, :, :], PE_[:, tt, :, :],
                              STAT[:, 48:56][:, s].unsqueeze(2).to_broadcast([P, 4, SEQ]), ALU.mult).then_inc(xs_norm, 1)
        dve.wait_ge(xp_ps, 2)
        dve.tensor_copy(PT[:, 4:8, :], XT_PS[:, 4:8, :]).then_inc(xp_sb, 1)
        for bank in range(4):
            dve.wait_ge(xo_high, bank + 1)
            k2 = slice(2 * bank, 2 * bank + 2)
            dve.tensor_tensor(HTL[:, k2, :], PS[:, 2048 + bank * 512:2560 + bank * 512].rearrange("p (k t) -> p k t", k=2),
                              HTH[:, k2, :].bitcast(F32), ALU.subtract).then_inc(xo_low, 1)
        split_run(BASE["xa_o"] + PB, 8)
        post_add(2, 1.0)
        prenorm(6, H, "ffn2")
        ffn_up("ffn2_up", 1)
        split_run(BASE["ffn2_down"] + PB, FFN_KT)
        post_add(3, 0.5)
        prenorm(7, H, "mix2")
        lb = COLS[:, LB:LB + 8].rearrange("p (r f) -> p r f", r=2)
        chain(dve.tensor_tensor(LBS[:, 4, :], lb[:, 0, :], lb[:, 1, :], ALU.max))
        dve.tensor_tensor(LBS[:, 0:2, :], lb, LBS[:, 4, :].unsqueeze(1).to_broadcast([P, 2, 4]),
                          ALU.subtract).then_inc(hg_d, 1)
        plain("w_in_2", 7, mixer_dst)
        dve.wait_ge(evac_a, EVAC["w_in_2"] + 7)
        dve.wait_ge(evac_d, EVAC["w_in_2"] + 7)
        dve.wait_ge(hg_a, 1)
        chain(dve.tensor_tensor(LBS[:, 4, :], LBS[:, 2, :], LBS[:, 3, :], ALU.add))
        chain(dve.reciprocal(LBS[:, 5, :], LBS[:, 4, :]))
        chain(dve.tensor_tensor(LBS[:, 6, :], LBS[:, 2, :], LBS[:, 5, :], ALU.mult))
        chain(dve.tensor_scalar(LBS[:, 7, :], LBS[:, 6, :], -1.0, 1.0, ALU.mult, ALU.add))
        dve.wait_ge(hg_a, 2)
        for ft in range(4):
            last = dve.tensor_scalar(FG[:, ft, :], FG[:, ft, :], LBS[:, 7, ft:ft + 1], LBS[:, 6, ft:ft + 1],
                                     ALU.mult, ALU.add)
        last.then_inc(hg_d, 1)
        dve.wait_ge(hg_d, 2)
        chain(dve.tensor_scalar(KH[:], FG[:], -1.0, 1.0, ALU.mult, ALU.add))
        dve.wait_ge(hg_a, 4)
        dve.wait_ge(hg_ok, 4)
        flat = GC[:].rearrange("p h t -> p (h t)")
        dve.tensor_tensor_scan(flat, CHUNK_ON[:], flat, 0.0, ALU.mult, ALU.add).then_inc(hg_d, 1)
        dve.wait_ge(hg_d, 3)

        def chunks(t):
            return t[:].rearrange("p h (n c) -> p (h n) c", c=HG_CHUNK)

        dve.tensor_tensor(chunks(KEN), chunks(GC)[:, :, HG_CHUNK - 1:].to_broadcast([P, 32, HG_CHUNK]), chunks(GC),
                          ALU.subtract).then_inc(hg_d, 1)
        dve.wait_ge(hg_a, 6)
        dve.scalar_tensor_tensor(QD[:], Q2, P ** -0.5, EG[:], ALU.mult, ALU.mult)
        dve.tensor_tensor(KD[:], KD[:], KH[:], ALU.mult).then_inc(hg_d, 1)
        dve.wait_ge(hg_a, 7)
        dve.tensor_tensor(KEN[:], KEN[:], KH[:], ALU.mult).then_inc(hg_d, 1)
        chain(dve.tensor_tensor(U[:], CG, HC, ALU.mult))
        for ft in range(4):
            w = [COLS[:, CONV_W2 + 3 * ft + j:CONV_W2 + 3 * ft + j + 1] for j in range(3)]
            chain(dve.tensor_scalar(Y[:, ft, :], U[:, ft, :], w[2], None, ALU.mult))
            for back in (1, 2):
                chain(dve.scalar_tensor_tensor(Y[:, ft, back:], U[:, ft, :SEQ - back], w[2 - back], Y[:, ft, back:],
                                               ALU.mult, ALU.add))
        dve.tensor_tensor(Y[:], Y[:], BG, ALU.mult).then_inc(c2_d, 1)
        dve.wait_ge(hg_p, 2)
        for tt in range(TT):
            last = dve.copy_predicated(ABD[:, tt, :, :], IN_CHUNK[:].bitcast(U32).unsqueeze(1).to_broadcast([P, 4, P]),
                                       PS[:, 1024 + tt * 512:1536 + tt * 512].rearrange("p (h n) -> p h n", h=4))
        last.then_inc(hg_d, 1)
        dve.wait_ge(s_ok, 1)
        for n in range(1, 7):
            if n == 4:
                dve.wait_ge(kv_ps, 2)
            if n > 1:
                dve.wait_ge(s_ok, n)
            for h in range(4):
                last = dve.scalar_tensor_tensor(
                    ST2[:, n, h, :], ST2[:, n - 1, h, :], EG[:, h, (n + 1) * HG_CHUNK - 1:(n + 1) * HG_CHUNK],
                    PS[:, 2048 + n % 4 * 512 + h * P:2048 + n % 4 * 512 + (h + 1) * P], ALU.mult, ALU.add)
            last.then_inc(s_ok, 1)
        dve.wait_ge(c2_p, 1)
        chain(dve.tensor_scalar(MS[:].rearrange("p f t -> p (f t)"), PS[:, 1024:2048], EPS, None, ALU.add))
        dve.reciprocal(MS[:], MS[:]).then_inc(c2_d, 1)
        dve.wait_ge(c2_a, 2)
        for ft in range(4):
            last = dve.scalar_tensor_tensor(Y[:, ft, :], Y[:, ft, :], COLS[:, CONV_GAIN2 + ft:CONV_GAIN2 + ft + 1],
                                            MS[:, ft, :], ALU.mult, ALU.mult)
        last.then_inc(c2_d, 1)
        dve.wait_ge(c2_a, 3)
        dve.tensor_tensor(XTL[:, 0:4, :], Y[:], XTH[:, 0:4, :].bitcast(F32), ALU.subtract).then_inc(c2_d, 1)
        dve.wait_ge(hg_a, 9)
        chain(dve.tensor_scalar(STAT[:, 40:48], STAT[:, 32:40], 1.0 / P, EPS, ALU.mult, ALU.add))
        dve.reciprocal(STAT[:, 40:48], STAT[:, 40:48]).then_inc(hg_d, 1)
        dve.wait_ge(hg_a, 10)
        for tt in range(TT):
            o = U[:, 2 * tt:2 * tt + 2, :].rearrange("p a t -> p (a t)").rearrange("p (h n) -> p h n", h=4)
            chain(dve.tensor_tensor(o, PS[:, tt * 512:tt * 512 + 512].rearrange("p (h n) -> p h n", h=4),
                                    STAT[:, 48 + tt * 4:52 + tt * 4].unsqueeze(2).to_broadcast([P, 4, P]), ALU.mult))
            last = dve.tensor_tensor(o, o, G2[:, tt, :].rearrange("p (h n) -> p h n", h=4), ALU.mult)
        last.then_inc(hg_d, 1)
        dve.wait_ge(hg_a, 11)
        dve.scalar_tensor_tensor(XTL[:, 4:8, :], XT_PS[:, 4:8, :], COLS[:, HG_GAIN:HG_GAIN + 1],
                                 XTH[:, 4:8, :].bitcast(F32), ALU.mult, ALU.subtract).then_inc(hg_d, 1)
        split_run(BASE["w_out_2"] + PB, 8)
        dve.wait_ge(w_used, BASE["peer_q"])
        for tt in range(TT):
            dve.tensor_tensor(H[:, tt, :], H[:, tt, :], ACC[:, tt, :], ALU.add).then_inc(h_done, 1)
        prenorm(8, H, "peer")
        plain("peer_q", 4, mixer_dst)

        def best16(values, rows, top, places):
            def each(instruction):
                for r in range(rows):
                    last = instruction(r)
                chain(last)

            each(lambda r: dve.max(top[:, r, 0:8], values[:, r, :]))
            each(lambda r: dve.max_index(places[:, r, 0:8], top[:, r, 0:8], values[:, r, :]))
            each(lambda r: dve.match_replace(values[:, r, :], top[:, r, 0:8], values[:, r, :], -3.0e38))
            each(lambda r: dve.max(top[:, r, 8:16], values[:, r, :]))
            each(lambda r: dve.max_index(places[:, r, 8:16], top[:, r, 8:16], values[:, r, :]))

        def keys_of(tt):
            dve.wait_ge(hot_ok, 2 * tt + 2)
            for p in range(2):
                last = dve.reduce_sum(ROUTE[:, tt, p, :], HOT[:, p, :, :], AX_X)
            last.then_inc(hot_used, 1)

        dve.wait_ge(iota_ok, 1)
        for tt in range(TT):
            dve.wait_ge(ks_sb, tt + 1)
            best16(SC[:, tt, :, :], 16, TOP[:, tt, :, :], TOP_AT[:, tt, :, :])
            dve.tensor_copy(TOP_ATF[:, tt, :, :], TOP_AT[:, tt, :, :])
            chain(dve.tensor_tensor(CAND[:, tt, :, :].rearrange("p h (a b) -> p h a b", a=16),
                                    TOP[:, tt, 0:16:2, :].unsqueeze(3).to_broadcast([P, 8, 16, 16]),
                                    TOP[:, tt, 1:16:2, :].unsqueeze(2).to_broadcast([P, 8, 16, 16]), ALU.add))
            if tt:
                keys_of(0)
            best16(CAND[:, tt, :, :], 8, CTOP[:, tt, :, :], CAT[:, tt, :, :])
            at_ = CAT[:, tt, :, :].rearrange("p h k -> p (h k)")
            dve.tensor_scalar(CDIG[:, tt, 0, :], at_, 4, None, ALU.logical_shift_right)
            chain(dve.tensor_scalar(CDIG[:, tt, 1, :], at_, 15, None, ALU.bitwise_and))
            chain(dve.tensor_copy(CDIGF[:, tt, :, :], CDIG[:, tt, :, :]))
            if tt:
                dve.wait_ge(hot_used, tt)
            for p in range(2):
                dve.tensor_tensor(HOT[:, p, :, :], CDIGF[:, tt, p, :].unsqueeze(2).to_broadcast([P, 128, 16]),
                                  IOTA[:, 0:16].unsqueeze(1).to_broadcast([P, 128, 16]),
                                  ALU.is_equal).then_inc(hot_one, 1)
            chain(dve.tensor_copy(GSUM[:, 8:16].unsqueeze(2), CTOP[:, tt, :, 0:1]))
            dve.tensor_tensor(CTOP[:, tt, :, :], CTOP[:, tt, :, :],
                              GSUM[:, 8:16].unsqueeze(2).to_broadcast([P, 8, 16]), ALU.subtract).then_inc(gd_ok, 1)
            dve.wait_ge(gexp_ok, tt + 1)
            chain(dve.reduce_sum(GSUM[:, 0:8], CTOP[:, tt, :, :], AX_X))
            chain(dve.reciprocal(GSUM[:, 0:8], GSUM[:, 0:8]))
            dve.tensor_tensor(ROUTE[:, tt, 2, :].rearrange("p (h k) -> p h k", h=8), CTOP[:, tt, :, :],
                              GSUM[:, 0:8].unsqueeze(2).to_broadcast([P, 8, 16]), ALU.mult).then_inc(route_ok, 1)
        keys_of(1)

        def gate_hot(q, group, dyn=None):
            if dyn is not None or group >= 2:
                dve.wait_ge(g_ps, at(group - 1, dyn))
            t = at(4 * group, dyn, 4)
            t = bass.ds(t, 4) if dyn is not None else slice(t, t + 4)
            for p, hot, done in ((0, OA, eq_ok), (1, OB, ob_ok)):
                dve.tensor_tensor(hot[:, 4 * q:4 * q + 4, :], IOTA[:].unsqueeze(1).to_broadcast([P, 4, P]),
                                  ROUTE_T[:, p, t].unsqueeze(2).to_broadcast([P, 4, P]),
                                  ALU.is_equal).then_inc(done, 1)

        dve.wait_ge(injected, 1)
        dve.wait_ge(rt_ok, 2)
        gate_hot(0, 0)
        gate_hot(1, 1)
        with dve.Fori(1, 32) as i:
            gate_hot(0, 0, i * 2)
            gate_hot(1, 1, i * 2)

        def weigh(s, dyn=None):
            dve.wait_ge(et_ps, at(s + 1, dyn))
            g = GATES[:, bass.ds(at(4 * s, dyn, 4), 4), :] if dyn is not None else GATES[:, 4 * s:4 * s + 4, :]
            dve.tensor_tensor(GE[:].rearrange("p (a t) -> p a t", a=4), PAIR[1].rearrange("p (a t) -> p a t", a=4), g,
                              ALU.mult).then_inc(prod_ok, 1)
            dve.wait_ge(wt_high, at(s + 1, dyn))
            dve.tensor_tensor(WTL[:].rearrange("p a t -> p (a t)"), GE[:],
                              WTH[:].bitcast(F32).rearrange("p a t -> p (a t)"), ALU.subtract).then_inc(wt_low, 1)

        b = BASE["peer"]
        dve.wait_ge(g_sb, 64)
        split(b + PB, PB)
        weigh(0)
        with dve.Fori(1, 32) as i:
            split(b, PB, i * 8)
            split(b + PB, PB, i * 8)
            weigh(0, i)
        dve.wait_ge(psq_done, 10)
        inverse(STAT[:, 16:18], STAT[:, 18:20]).then_inc(pinv_done, 1)
        dve.wait_ge(prs_done, 5)
        dve.wait_ge(row_in, 16 * 5)
        for tt in range(TT):
            dve.scalar_tensor_tensor(TMP[:, tt, :], ACC[:, tt, :], STAT[:, 20 + tt:21 + tt],
                                     ROWG[:], ALU.mult, ALU.mult).then_inc(final_ok, 1)

    @block.tensor
    def _(pe):
        def product(out, high, low, w_hi, w_lo, start, stop):
            pe.matmul(out, high, w_hi, start=start, stop=False, skip_group_check=True)
            pe.matmul(out, low, w_hi, start=False, stop=False, skip_group_check=True)
            return pe.matmul(out, high, w_lo, start=False, stop=stop, skip_group_check=True)

        def transpose_norm(k):
            for tt, ready in enumerate((xn_act, xn_dve)):
                pe.wait_ge(ready, k + 1)
                for kt in range(KT):
                    last = pe.transpose(XT_PS[:, kt, tt * P:(tt + 1) * P], XN[:, tt, kt * P:(kt + 1) * P], IDENT[:])
                    if tt == TT - 1 and kt % 2:
                        last.then_inc(xt_ps, 1)
            pe.wait_ge(xt_low, (k + 1) * KT)

        def panel_tokens(n0, pair, dyn=None, blocks=range(PB)):
            for b in blocks:
                s = (n0 + b) % SLOTS
                pe.wait_ge(w_split, at(n0 + b + 1, dyn))
                for kt in (2 * b, 2 * b + 1):
                    w = slice((kt % 2) * 512, (kt % 2) * 512 + 512)
                    for tt in range(TT):
                        t = slice(tt * P, (tt + 1) * P)
                        last = product(pair[:, tt * 512:(tt + 1) * 512], XTH[:, kt, t], XTL[:, kt, t],
                                       WH[:, s, w], WL[:, s, w], kt == 0, kt == KT - 1)
                last.then_inc(w_used, 1)

        def panel_features(n0, pair, dyn=None, blocks=range(PB)):
            for b in blocks:
                s = (n0 + b) % SLOTS
                pe.wait_ge(w_split, at(n0 + b + 1, dyn))
                for kt in (2 * b, 2 * b + 1):
                    for ft in range(4):
                        w = slice((kt % 2) * 512 + ft * P, (kt % 2) * 512 + (ft + 1) * P)
                        last = product(pair[:, ft * SEQ:(ft + 1) * SEQ], WH[:, s, w], WL[:, s, w],
                                       XTH[:, kt, :], XTL[:, kt, :], kt == 0 and ft % 2 == 0, kt == KT - 1)
                last.then_inc(w_used, 1)

        def plain(stage, kinds):
            for n, kind in enumerate(kinds):
                if n >= 2:
                    pe.wait_ge(evac_a, EVAC[stage] + n - 1)
                    pe.wait_ge(evac_d, EVAC[stage] + n - 1)
                (panel_tokens if kind == "t" else panel_features)(BASE[stage] + PB * n, PAIR[n % 2])

        def ffn_up(stage, f):
            b, e = BASE[stage], f * FFN_PANELS

            def up(p, parity, dyn=None):
                if dyn is not None or e + p >= 2:
                    pe.wait_ge(hidden_done, at(e + p - 1, dyn))
                panel_tokens(b + PB * p, PAIR[parity], None if dyn is None else dyn * PB)

            def turn(p, parity, dyn=None):
                pe.wait_ge(hidden_done, at(e + p + 1, dyn))
                if dyn is not None or e + p >= 2:
                    pe.wait_ge(ht_low, at(e + p - 1, dyn))
                for ft in range(2):
                    for tt in range(TT):
                        o = 512 * parity + ft * SEQ + tt * P
                        last = pe.transpose(ACC[:, 0, o:o + P], HN[:, parity, tt, ft * P:(ft + 1) * P], IDENT[:])
                last.then_inc(ht_ps, 1)

            up(0, 0)
            up(1, 1)
            turn(0, 0)
            with pe.Fori(0, (FFN_PANELS - 3) // 2) as i:
                for p in (2, 3):
                    up(p, p % 2, i * 2)
                    turn(p - 1, (p - 1) % 2, i * 2)
            p = FFN_PANELS - 1
            up(p, p % 2)
            turn(p - 1, (p - 1) % 2)
            turn(p, p % 2)
            pe.wait_ge(ht_low, e + FFN_PANELS)

        def rows_product(stage, kts, high=HTH, low=HTL):
            for kt in range(kts):
                n = BASE[stage] + kt
                pe.wait_ge(w_split, n + 1)
                for tt in range(TT):
                    t = slice(tt * P, (tt + 1) * P)
                    for half in range(2):
                        w = slice(half * 512, half * 512 + 512)
                        last = product(ACC[:, tt, w], high[:, kt, t], low[:, kt, t],
                                       WH[:, n % SLOTS, w], WL[:, n % SLOTS, w], kt == 0, kt == kts - 1)
                last.then_inc(w_used, 1)

        pe.wait_ge(ident_ok, 1)
        transpose_norm(0)
        plain("xa_kv", "fftt")
        pe.wait_ge(evac_a, EVAC["w_in"])
        pe.wait_ge(evac_d, EVAC["w_in"])
        transpose_norm(1)
        ffn_up("ffn1_up", 0)
        rows_product("ffn1_down", FFN_KT)
        transpose_norm(2)
        plain("w_in", "fffftt")
        pe.wait_ge(masks_ok, 5)
        pe.wait_ge(evac_a, EVAC["w_in"] + 4)
        pe.wait_ge(evac_d, EVAC["w_in"] + 4)

        def scores(k):
            if k:
                pe.wait_ge(sc_sb, k)
            for h in range(2):
                d = slice(64 * h, 64 * h + 64)
                pe.matmul(S_PS[:, h, 0:SEQ], KTT[d, k, 0:P], QT[d, k, :], start=True, stop=True)
                last = pe.matmul(S_PS[:, h, SEQ:384], KTT[d, k, P:SEQ], QT[d, k, P:SEQ], start=True, stop=True)
            last.then_inc(sc_ps, 1)

        def suffix_sums(k):
            pe.wait_ge(sp_done, k + 1)
            if k:
                pe.wait_ge(loga_done, k)
            if k >= 2:
                pe.wait_ge(o_done, k - 1)
            for h in range(2):
                pe.matmul(C_PS[:, h, 0:384], FROM[:], by_head(SPL, k)[:, h, :], start=True, stop=False)
                last = pe.matmul(C_PS[:, h, P:SEQ], ONES[:], by_head(SPL, k)[:, h, SEQ:384], start=False, stop=True)
            last.then_inc(sum_ps, 1)

        def weighted_values(k):
            a = by_head(LOGA, k)
            pe.wait_ge(a_done, k + 1)
            if k:
                pe.wait_ge(o_done, k)
            for h in range(2):
                c = 2 * k + h
                o = [C_PS[:, h, 384 + tt * 64:448 + tt * 64] for tt in range(TT)]
                v = [V[:, c // 8, tt, c % 8 * 64:c % 8 * 64 + 64] for tt in range(TT)]
                pe.matmul(o[0], a[:, h, 0:P], v[0], start=True, stop=True)
                pe.matmul(o[1], a[:, h, P:SEQ], v[0], start=True, stop=False)
                last = pe.matmul(o[1], a[:, h, SEQ:384], v[1], start=False, stop=True)
            last.then_inc(o_ps, 1)

        for k in range(10):
            if k == 0:
                pe.wait_ge(evac_a, EVAC["w_in"] + 6)
                pe.wait_ge(evac_d, EVAC["w_in"] + 6)
            if k < 8:
                scores(k)
            if 1 <= k <= 8:
                suffix_sums(k - 1)
            if k >= 2:
                weighted_values(k - 2)
            n = 6 + k // 2
            if k % 2 == 0:
                pe.wait_ge(evac_a, EVAC["w_in"] + n - 1)
                pe.wait_ge(evac_d, EVAC["w_in"] + n - 1)
            (panel_tokens if n >= 9 else panel_features)(BASE["w_in"] + PB * n, PAIR[n % 2], None,
                                                        range(k % 2 * 2, k % 2 * 2 + 2))
        pe.wait_ge(wdt_ok, 1)
        pe.wait_ge(evac_a, EVAC["w_in"] + 10)
        pe.wait_ge(evac_d, EVAC["w_in"] + 10)
        for tt in range(TT):
            for kt in range(KT):
                t, w = slice(tt * P, (tt + 1) * P), slice(kt * 16, kt * 16 + 16)
                last = product(PS[:, 1024 + tt * 16:1040 + tt * 16], XTH[:, kt, t], XTL[:, kt, t],
                               WDTH[:, w], WDTL[:, w], kt == 0, kt == KT - 1)
        last.then_inc(dt_ps, 1)
        pe.wait_ge(dt_d, 3)
        pe.matmul(PS[:, 1088:1120], UPTO[:], SS[:, 12, :], start=True, stop=True)
        pe.matmul(PS[:, 1120:1136], ONES[:], SS[:, 12, 0:16], start=True, stop=True).then_inc(acs_ps, 1)

        def row_sums(tt):
            pe.wait_ge(au_ok, tt + 1)
            if tt:
                pe.wait_ge(lm_ok, tt)
            for q in range(4):
                o = PS[:, 2048 + q * 512:2560 + q * 512]
                pe.matmul(o, ONES[:], AU[:, 4 * q:4 * q + 4, :].rearrange("p h n -> p (h n)"),
                          start=True, stop=False)
                last = pe.matmul(o.rearrange("p (h n) -> p h n", h=4), IDENT[:],
                                 FUTURE[:].unsqueeze(1).to_broadcast([P, 4, P]), start=False, stop=True)
            last.then_inc(row_ps, 1)

        pe.wait_ge(o_done, 8)
        row_sums(0)
        def xs_tokens(tt):
            if tt:
                pe.wait_ge(xs_sb, 2 * tt)
            for ft in range(8):
                last = pe.transpose(PS[:, ft * P:(ft + 1) * P], CV[:, ft, tt * P:(tt + 1) * P], IDENT[:])
            last.then_inc(xs_ps, 1)

        pe.wait_ge(evac_a, EVAC["w_in"] + 11)
        pe.wait_ge(evac_d, EVAC["w_in"] + 11)
        pe.wait_ge(cv_done, 3)
        pe.wait_ge(acs_ok, 1)
        for g in range(2):
            pe.transpose(PS[:, 1152 + g * P:1280 + g * P], CV[:, 8 + g, 0:P], IDENT[:])
        for tt in range(TT):
            for g in range(2):
                o, t = 1536 + (2 * tt + g) * P, slice(tt * P, (tt + 1) * P)
                last = pe.matmul(PS[:, o:o + P], CV[:, 8 + g, t], CV[:, 10 + g, t], start=True, stop=True)
        last.then_inc(cb_ps, 1)
        xs_tokens(0)
        xs_tokens(1)
        pe.wait_ge(xd_ok, 2)
        pe.wait_ge(cb_ok, 2)
        for g in range(2):
            last = pe.matmul(PS[:, 1024 + g * 512:1536 + g * 512], BN[:, g, :], XDD[:, g * 512:(g + 1) * 512],
                             start=True, stop=True)
        last.then_inc(st_ps, 1)
        for tt in range(TT):
            pe.wait_ge(m_ok, tt + 1)
            pe.wait_ge(xd_ok, (1, 3)[tt])
            pe.wait_ge(xs_sb, 4)
            if tt:
                pe.wait_ge(y_done, 1)
            for h in range(16):
                last = pe.matmul(PS[:, h * 64:(h + 1) * 64], LM[:, h, :], XD[:, tt, h * 64:(h + 1) * 64],
                                 start=True, stop=True)
            if tt:
                pe.wait_ge(st_ok, 1)
                for g in range(2):
                    last = pe.matmul(PS[:, 1024 + g * 512:1536 + g * 512], CV[:, 10 + g, P:SEQ],
                                     ST[:, g * 512:(g + 1) * 512], start=True, stop=True)
            else:
                row_sums(1)
            last.then_inc(y_ps, 1)
        pe.wait_ge(y_done, 2)
        transpose_norm(3)
        transpose_norm(4)
        rows_product("w_out", 16)
        transpose_norm(5)
        plain("xa_q", "ff")
        pe.wait_ge(evac_a, EVAC["xa_q"] + 2)
        pe.wait_ge(evac_d, EVAC["xa_q"] + 2)
        for tt in range(TT):
            for h in range(4):
                for ft in (2 * h, 2 * h + 1):
                    last = pe.matmul(ACC[:, tt, h * SEQ:(h + 1) * SEQ], QT[:, ft, tt * P:(tt + 1) * P], XAK[:, ft, :],
                                     start=ft % 2 == 0, stop=ft % 2 == 1)
            last.then_inc(xs_sc, 1)
        for half in range(2):
            for h in (2 * half, 2 * half + 1):
                for tt in range(TT):
                    pe.wait_ge(xs_norm, tt + 1)
                    for mt in range(2):
                        last = pe.transpose(XT_PS[:, 2 * h + mt, tt * P:(tt + 1) * P],
                                            PE_[:, tt, h, mt * P:(mt + 1) * P], IDENT[:])
            last.then_inc(xp_ps, 1)
        pe.wait_ge(xp_sb, 2)
        for ft in range(8):
            for mt in range(2):
                last = pe.matmul(PS[:, 2048 + ft * SEQ:2048 + (ft + 1) * SEQ],
                                 XAV[:, ft // 4, mt, ft % 4 * P:ft % 4 * P + P], PT[:, ft // 2 * 2 + mt, :],
                                 start=mt == 0, stop=mt == 1)
            if ft % 2:
                last.then_inc(xo_ps, 1)
        pe.wait_ge(xo_low, 4)
        rows_product("xa_o", 8)
        transpose_norm(6)
        ffn_up("ffn2_up", 1)
        rows_product("ffn2_down", FFN_KT)
        transpose_norm(7)
        plain("w_in_2", "ffffftt")
        pe.wait_ge(evac_a, EVAC["w_in_2"] + 7)
        pe.wait_ge(evac_d, EVAC["w_in_2"] + 7)
        pe.wait_ge(hg_d, 6)
        for tt in range(TT):
            for h in range(4):
                last = pe.transpose(PS[:, (tt * 4 + h) * P:(tt * 4 + h + 1) * P], KEN[:, h, tt * P:(tt + 1) * P], IDENT[:])
        last.then_inc(hg_p, 1)
        for tt in range(TT):
            for h in range(4):
                o, t = 1024 + (tt * 4 + h) * P, slice(tt * P, (tt + 1) * P)
                last = pe.matmul(PS[:, o:o + P], KD[:, h, t], QD[:, h, t], start=True, stop=True)
        last.then_inc(hg_p, 1)

        def chunk_kv(tt):
            for j in range(4 - tt):
                rows = slice(HG_CHUNK * j, HG_CHUNK * (j + 1))
                for h in range(4):
                    last = pe.matmul(PS[:, 2048 + j * 512 + h * P:2048 + j * 512 + (h + 1) * P], KE[rows, tt, h, :],
                                     V2[rows, tt, h * P:(h + 1) * P], start=True, stop=True,
                                     tile_position=(HG_CHUNK * j, 0))
            last.then_inc(kv_ps, 1)

        pe.wait_ge(hg_a, 8)
        chunk_kv(0)
        pe.wait_ge(s_ok, 4)
        chunk_kv(1)
        pe.wait_ge(c2_a, 1)
        pe.wait_ge(hg_d, 7)
        for half in range(2):
            last = pe.matmul(PS[:, 1024 + half * 512:1536 + half * 512], GROUP64[:],
                             MS[:, 2 * half:2 * half + 2, :].rearrange("p f t -> p (f t)"), start=True, stop=True)
        last.then_inc(c2_p, 1)
        for tt in range(TT):
            for h in range(4):
                o = tt * 512 + h * P
                last = pe.matmul(PS[:, o:o + P], ABD[:, tt, h, :], V2[:, tt, h * P:(h + 1) * P],
                                 start=h == 0, stop=False, skip_group_check=True)
            if tt == 0:
                last.then_inc(hg_p, 1)
            else:
                pe.wait_ge(s_ok, 7)
            for n in range(max(1, 4 * tt), 4 * tt + 4):
                rows = slice(HG_CHUNK * (n % 4), HG_CHUNK * (n % 4 + 1))
                if n > 1:
                    pe.wait_ge(s_ok, n)
                for h in range(4):
                    o = tt * 512 + h * P
                    last = pe.matmul(PS[rows, o:o + P], QD[:, h, n * HG_CHUNK:(n + 1) * HG_CHUNK],
                                     ST2[:, n - 1, h, :], start=False, stop=True, skip_group_check=True)
        last.then_inc(hg_p, 1)
        pe.wait_ge(hg_d, 9)
        for tt in range(TT):
            o = U[:, 2 * tt:2 * tt + 2, :].rearrange("p a t -> p (a t)")
            for h in range(4):
                last = pe.transpose(XT_PS[:, 4 + h, tt * P:(tt + 1) * P], o[:, h * P:(h + 1) * P], IDENT[:])
        last.then_inc(hg_p, 1)
        pe.wait_ge(hg_d, 10)
        pe.wait_ge(c2_d, 4)
        rows_product("w_out_2", 8, XTH, XTL)
        transpose_norm(8)
        plain("peer_q", "ffff")
        for tt in range(TT):
            for half in range(2):
                w = slice(half * 512, half * 512 + 512)
                last = pe.matmul(ACC[:, tt, w], IDENT[:], H[:, tt, w], start=True, stop=False, skip_group_check=True)
        last.then_inc(injected, 1)
        pe.wait_ge(keys_in, 16)
        pe.wait_ge(evac_a, EVAC["peer_q"] + 4)
        pe.wait_ge(evac_d, EVAC["peer_q"] + 4)
        for tt in range(TT):
            if tt:
                pe.wait_ge(ks_sb, tt)
            for hp in range(16):
                last = pe.matmul(PS[:, hp * P:(hp + 1) * P], QP[:, hp, tt * P:(tt + 1) * P], KEYS[:, hp, :],
                                 start=True, stop=True)
            last.then_inc(ks_ps, 1)
        for tt in range(TT):
            pe.wait_ge(route_ok, tt + 1)
            pe.wait_ge(hot_used, tt + 1)
            pe.wait_ge(ks_sb, 2)
            if tt:
                pe.wait_ge(rt_ok, tt)
            for a in range(3):
                last = pe.transpose(PS[:, 1024 + a * P:1152 + a * P], ROUTE[:, tt, a, :], IDENT[:])
            last.then_inc(rt_ps, 1)

        def gates(q, group, dyn=None):
            pe.wait_ge(oa_ok, at(group + 1, dyn))
            pe.wait_ge(ob_ok, at(group + 1, dyn))
            if dyn is not None or group >= 2:
                pe.wait_ge(g_sb, at(group - 1, dyn))
            for j in range(4):
                last = pe.matmul(PS[:, 512 * q + j * P:512 * q + (j + 1) * P], OB[:, 4 * q + j, :], OA[:, 4 * q + j, :],
                                 start=True, stop=True)
            last.then_inc(g_ps, 1)

        gates(0, 0)
        gates(1, 1)
        with pe.Fori(1, 32) as i:
            gates(0, 0, i * 2)
            gates(1, 1, i * 2)

        def experts_down(n0, dyn=None):
            for k in range(4):
                s = (n0 + k) % SLOTS
                pe.wait_ge(w_split, at(n0 + k + 1, dyn))
                for tt in range(TT):
                    t = slice(tt * P, (tt + 1) * P)
                    for half in range(2):
                        w = slice(half * 512, half * 512 + 512)
                        last = product(ACC[:, tt, w], WTH[:, k, t], WTL[:, k, t], WH[:, s, w], WL[:, s, w],
                                       False, dyn is None and k == 3)
                last.then_inc(w_used, 1)

        def experts_turn(s, dyn=None):
            pe.wait_ge(gelu_ok, at(s + 1, dyn))
            for k in range(4):
                for tt in range(TT):
                    last = pe.transpose(PAIR[1][:, k * SEQ + tt * P:k * SEQ + (tt + 1) * P],
                                        GE[:, tt * 512 + k * P:tt * 512 + (k + 1) * P], IDENT[:])
            last.then_inc(et_ps, 1)

        b = BASE["peer"]
        pe.wait_ge(g_sb, 64)
        panel_tokens(b, PAIR[0])
        experts_turn(0)
        with pe.Fori(1, 32) as i:
            pe.wait_ge(gelu_ok, i * 1)
            panel_tokens(b - PB, PAIR[0], i * 8)
            pe.wait_ge(wt_low, i * 1)
            experts_down(b, i * 8)
            experts_turn(0, i)
        pe.wait_ge(wt_low, 32)
        experts_down(b + 252)

    ctx.close()


def panels(w):
    n = w.shape[1] // 512
    return w.reshape(PB, 2, P, n, 512).transpose(3, 0, 2, 1, 4).reshape(n * PB, P, BLK)


def row_blocks(w):
    return w.reshape(-1, P, BLK)


def gate_up(w):
    return w.reshape(D, 2, FFN_PANELS, 256).transpose(0, 2, 1, 3).reshape(D, 2 * D_FF)


def col(v):
    return v.reshape(-1, P).T


def kernel(**inputs):
    import concourse.bacc as bacc
    from concourse.bass_utils import run_bass_kernel_spmd

    a = {k: np.ascontiguousarray(v) for k, v in inputs.items()}
    g = {k: (v[0] if v.shape[0] == 1 and k not in ("hg_lb_logits_2", "norm_f_2") else v) for k, v in a.items()}
    u = g["peer_u_2"].reshape(32, 512, PB, 2, P).transpose(0, 2, 4, 3, 1).reshape(32, PB, P, BLK)
    v = g["peer_v_2"].reshape(32, PB, P, BLK)
    parts = [
        panels(g["xa_wkv"]), panels(gate_up(g["ffn1_w_gu"])), row_blocks(g["ffn1_w_down"]),
        panels(np.concatenate([g["w_in"][:, :3072], g["w_in"][:, 4096:5632], g["w_in"][:, 3072:4096]], axis=1)), row_blocks(g["w_out"]), panels(g["xa_wq"]), row_blocks(g["xa_wo"]),
        panels(gate_up(g["ffn2_w_gu"])), row_blocks(g["ffn2_w_down"]), panels(g["w_in_2"]),
        row_blocks(g["w_out_2"]), panels(g["peer_wq_2"]),
        u[0], np.stack([u[1:], v[:-1]], axis=1).reshape(248, P, BLK), v[31],
    ]
    cols = np.concatenate(
        [col(g[k]) for k in ("mem_g", "ffn1_pre_g", "mix_pre_g", "xa_pre_g", "ffn2_pre_g", "norm_mix_2",
                             "norm_ffn_2", "attn_norm_g", "ssd_norm_g", "conv_gain_2", "hg_gain_2", "conv_b")]
        + [g["conv_w"].reshape(4, 12, P).transpose(2, 1, 0).reshape(P, 48),
           g["conv_w_2"].reshape(3, 4, P).transpose(2, 1, 0).reshape(P, 12),
           g["hg_lb_logits_2"].reshape(2, 4, P).transpose(2, 0, 1).reshape(P, 8)], axis=1)
    arrays = {
        "stream": np.concatenate(parts, axis=0),
        "w_dt": g["w_in"][:, 5632:].reshape(KT, P, 16).transpose(1, 0, 2).reshape(P, KT * 16),
        "cols": cols,
        "small_row": np.concatenate([g["dt_bias"], g["a_log"], g["d_skip"]]).reshape(1, 48),
        "rows": np.stack([g["ffn1_post_g"], g["mix_post_g"], g["xa_post_g"], g["ffn2_post_g"], g["norm_f_2"]]),
        "x": a["x"].reshape(SEQ, D),
        "mem": a["mem"].reshape(SEQ, D),
        "keys": g["peer_keys_2"].reshape(16, P, P).transpose(2, 0, 1),
    }
    nc = bacc.Bacc("TRN2", target_bir_lowering=False, num_devices=1)
    ins = [nc.dram_tensor(f"in_{k}", v.shape, F32, kind="ExternalInput").ap() for k, v in arrays.items()]
    out = nc.dram_tensor("out", (SEQ, D), F32, kind="ExternalOutput").ap()
    build(nc, *ins, out)
    r = run_bass_kernel_spmd(nc, [{f"in_{k}": np.ascontiguousarray(v) for k, v in arrays.items()}], core_ids=[0])
    return r.results[0]["out"].reshape(1, SEQ, D)
```

```python
from contextlib import ExitStack

import numpy as np

import concourse.bass as bass
from concourse import mybir

F32 = mybir.dt.float32
F32R = mybir.dt.float32r
U32 = mybir.dt.uint32
ACT = mybir.ActivationFunctionType
ALU = mybir.AluOpType
AX_X = mybir.AxisListType.X

P = 128
SEQ = 256
TT = SEQ // P
D = 1024
KT = D // P
D_FF = 2816
FFN_PANELS = D_FF // 256
FFN_KT = D_FF // P
EPS = 1e-6
BLK = 1024
SLOTS = 4
PB = 4
KB = 1024

STREAM = [
    ("xa_kv", 16), ("ffn1_up", 44), ("ffn1_down", 22), ("w_in", 44), ("w_out", 16),
    ("xa_q", 8), ("xa_o", 8), ("ffn2_up", 44), ("ffn2_down", 22), ("w_in_2", 28),
    ("w_out_2", 8), ("peer_q", 16), ("peer", 256),
]
BASE, N_BLOCKS = {}, 0
for _name, _n in STREAM:
    BASE[_name] = N_BLOCKS
    N_BLOCKS += _n

EVAC, N_EVAC = {}, 0
for _name, _n in (("xa_kv", 4), ("w_in", 11), ("xa_q", 2), ("w_in_2", 7), ("peer_q", 4)):
    EVAC[_name] = N_EVAC
    N_EVAC += _n

GAIN_COL = {"mem": 0, "ffn1": 8, "mix": 16, "xa": 24, "ffn2": 32, "mix2": 40, "peer": 48,
            "attn": 56, "ssd": 64}
CONV_GAIN2, HG_GAIN, CONV_B, CONV_W, CONV_W2, LB = 72, 76, 77, 89, 137, 149
N_COLS = 157
EARLY = 64
SEARCH = 60
TURN = 12
TURNS = EARLY // 4
EARLY_OUT = [SEARCH // 4 + (EARLY - SEARCH) // 2] * 2 + [SEARCH // 4] * 2
GROUPS = SEQ // 4 // (EARLY - SEARCH)
HG_CHUNK = 32
SQUARES = [0, 2, 4, 6, 8, 12, 14, 16, 18, 20]



class Chain:

    def __init__(self, engine, semaphore):
        self.engine, self.semaphore, self.count = engine, semaphore, 0
        self.dyn, self.scale = None, 1

    def __call__(self, instruction):
        self.count += 1
        instruction.then_inc(self.semaphore, 1)
        self.engine.wait_ge(self.semaphore, at(self.count, self.dyn, self.scale))

    def enter(self, dyn, each):
        self.dyn, self.scale, self.began = dyn, each, self.count

    def leave(self, times):
        assert self.count - self.began == self.scale
        self.count, self.dyn, self.scale = self.began + times * self.scale, None, 1


def at(static, dyn=None, scale=1):
    return static if dyn is None else dyn * scale + static


def build(nc, stream, w_dt, cols, small_row, rows, x, mem, keys, early, out):
    ctx = ExitStack()
    B0 = 16512

    def sb(name, shape, kb, dt=F32):
        return nc.alloc_sbuf_tensor_at(name, shape, dt, offset=B0 + int(kb * KB))

    def sem(name):
        return ctx.enter_context(nc.semaphore(name))

    PS = ctx.enter_context(nc.psum_tensor("ps", [P, 4096], F32))
    PAIR = [PS[:, 0:1024], PS[:, 1024:2048]]
    ACC = PS[:, 2048:4096].rearrange("p (t n) -> p t n", t=TT)
    XT_PS = PS[:, 0:2048].rearrange("p (k t) -> p k t", k=KT)
    RING = sb("ring", [P, SLOTS, BLK], 0)
    WH = sb("w_high", [P, SLOTS, BLK], 16, F32R)
    WL = sb("w_low", [P, SLOTS, BLK], 32, F32R)
    XTH = sb("xT_high", [P, KT, SEQ], 48, F32R)
    XTL = sb("xT_low", [P, KT, SEQ], 56, F32R)
    IDENT = sb("ident", [P, P], 64)
    H = sb("h", [P, TT, D], 65)
    XN = sb("xn", [P, TT, D], 73)
    TMP = sb("tmp", [P, TT, D], 81)
    ROWG = sb("row_gain", [P, D], 89)
    COLS = sb("cols", [P, N_COLS], 93)
    STAT = sb("stat", [P, 64], 93.75)
    XAK = sb("xa_kT", [P, 8, SEQ], 97)
    XAV = sb("xa_v", [P, 2, TT, 512], 105)
    HTH = sb("hT_high", [P, FFN_KT, SEQ], 113, F32R)
    HTL = sb("hT_low", [P, FFN_KT, SEQ], 135, F32R)
    SG = sb("silu_gate", [P, 2, TT, 256], 157)
    HN = sb("hidden", [P, 2, TT, 256], 161)
    MEM = sb("mem_sb", [P, TT, D], 165)
    UPTO = sb("upto", [P, P], 94)
    FROM = sb("from", [P, P], 94.5)
    ONES = sb("ones", [P, P], 95)
    BEFORE = sb("before", [P, P], 95.5)
    CAP = sb("cap", [P, P], 96)
    SMALL = sb("small_row_sb", [P, 48], 96.5)
    R = sb("projections", [P, 11, 1024], 113)
    QT = R[:, 0:2, :].rearrange("p a (b t) -> p (a b) t", t=SEQ)
    KTT = R[:, 2:4, :].rearrange("p a (b t) -> p (a b) t", t=SEQ)
    V = R[:, 4:6, :].rearrange("p a (t n) -> p a t n", t=TT)
    XBC = R[:, 6:9, :].rearrange("p a (b t) -> p (a b) t", t=SEQ)
    Z = R[:, 9:11, :].rearrange("p a (t n) -> p a t n", t=TT)
    AO = sb("attention_out", [P, TT, D], 81)
    ZS = sb("scores", [P, 2, 768], 157)
    SPL = sb("softplus", [P, 2, 768], 163)
    LOGA = sb("log_attention", [P, 2, 768], 169)
    S_PS = PS[:, 2048:3072].rearrange("p (h n) -> p h n", h=2)
    C_PS = PS[:, 3072:4096].rearrange("p (h n) -> p h n", h=2)
    PE_ = sb("xa_probs", [P, TT, 4, SEQ], 157)
    PT = sb("xa_probsT", [P, 8, SEQ], 165)
    def r2(n):
        return R[:, n, :].rearrange("p (b t) -> p b t", t=SEQ)

    CG, HC, BG, Q2, F2 = (r2(n) for n in range(5))
    V2, G2 = (R[:, n, :].rearrange("p (t n) -> p t n", t=TT) for n in (5, 6))
    U = sb("conv_u", [P, 4, SEQ], 141)
    Y = sb("conv_y", [P, 4, SEQ], 145)
    MS = sb("conv_ms", [P, 4, SEQ], 149)
    FG = sb("forget", [P, 4, SEQ], 153)
    KH = sb("hg_k", [P, 4, SEQ], 157)
    GC = sb("log_decay", [P, 4, SEQ], 161)
    EG = sb("exp_decay", [P, 4, SEQ], 165)
    KD = sb("k_dec", [P, 4, SEQ], 169)
    QD = sb("q_dec", [P, 4, SEQ], 173)
    KEN = sb("k_end", [P, 4, SEQ], 177)
    KE = sb("k_end_tokens", [P, TT, 4, P], 181)
    ABD = sb("hg_scores", [P, TT, 4, P], 185)
    ST2 = sb("hg_states", [P, 7, 4, P], 189)
    GROUP64 = sb("group64", [P, P], 203)
    IN_CHUNK = sb("in_chunk", [P, P], 203.5)
    CHUNK_ON = sb("chunk_on", [P, 4 * SEQ], 85)
    LBS = sb("lower_bound", [P, 8, 4], 204)
    QP = R[:, 0:4, :].rearrange("p a (b t) -> p (a b) t", t=SEQ)
    SC = sb("key_scores", [P, TT, 16, P], 129)
    KEYS = sb("keys_sb", [P, 16, P], 145)
    TOP = sb("top", [P, TT, 16, 16], 153)
    TOP_AT = sb("top_at", [P, TT, 16, 16], 155, U32)
    TOP_ATF = sb("top_at_f", [P, TT, 16, 16], 157)
    CAND = sb("candidates", [P, TT, 8, 256], 159)
    CTOP = sb("cand_top", [P, TT, 8, 16], 175)
    CAT = sb("cand_at", [P, TT, 8, 16], 176, U32)
    CDIG = sb("cand_digits", [P, TT, 2, 128], 177, U32)
    CDIGF = sb("cand_digits_f", [P, TT, 2, 128], 179)
    HOT = sb("digit_hot", [P, 2, 128, 16], 181)
    ROUTE = sb("route", [P, TT, 3, 128], 197)
    GSUM = sb("gate_sum", [P, TT, 16], 200)
    ROUTE_T = sb("routeT", [P, 3, SEQ], 66.5)
    OA = sb("gate_at_key1", [P, 8, P], 69.5)
    OB = sb("one_at_key2", [P, 8, P], 73.5)
    IOTA = sb("iota", [P, P], 207)
    GE = sb("gelu_out", [P, 4, SEQ], 64.5)
    WTH = sb("expert_w_high", [P, 4, SEQ], 68.5, F32R)
    WTL = sb("expert_w_low", [P, 4, SEQ], 72.5, F32R)
    GATES = sb("gates", [P, P, SEQ], 79)
    WDT = sb("w_dt_sb", [P, KT * 16], 201)
    WDTH = sb("w_dt_high", [P, KT * 16], 201.5, F32R)
    WDTL = sb("w_dt_low", [P, KT * 16], 202, F32R)
    SS = sb("ssd_small", [P, 16, 32], 202.5)
    FUTURE = sb("future", [P, P], 204.5)
    CV = sb("conv_out", [P, 12, SEQ], 157)
    XSN = sb("xs_tokens", [P, TT, D], 169)
    AU = sb("adt_upto", [P, 16, P], 177)
    LM = sb("decay", [P, 16, P], 185)
    XD = sb("xs_dt", [P, TT, D], 193)
    XDD = sb("xs_dt_decay", [P, D], 73)
    ST = sb("state", [P, D], 77)
    YS = sb("ssd_out", [P, TT, D], 177)
    BN = sb("b_tokens", [P, 2, P], 145)
    CBM = sb("cb_masked", [P, TT, 2, P], 146)

    def mixer_dst(n, dyn):
        return R[:, n, :] if dyn is None else R[:, bass.ds(dyn + n, 1), :].rearrange("p a n -> p (a n)")

    def kv_dst(n, _):
        kv = XAK[:, 4 * n:4 * n + 4, :] if n < 2 else XAV[:, n - 2, :, :]
        return kv.rearrange("p a b -> p (a b)")

    def by_head(t, k):
        return t[:, k % 2, :].rearrange("p (h n) -> p h n", h=2)

    loaded = [sem(f"loaded{i}") for i in range(SLOTS)]
    w_high, w_split, w_used = sem("w_high_done"), sem("w_split_done"), sem("w_used")
    const_in, x_in, mem_in, row_in = sem("const_in"), sem("x_in"), sem("mem_in"), sem("row_in")
    out_done = sem("out_done")
    ident_zero, ident_ok = sem("ident_zero"), sem("ident_ok")
    act_chain, dve_chain = sem("act_chain"), sem("dve_chain")
    sq_done, inv_done, rs_done = sem("square_sum"), sem("inverse_ms"), sem("rms_scale")
    xn_act, xn_dve = sem("xn_tile0"), sem("xn_tile1")
    xt_ps, xt_high, xt_low = sem("xT_psum"), sem("xT_high_done"), sem("xT_low_done")
    evac_a, evac_d = sem("evac_act"), sem("evac_dve")
    silu_done, hidden_done, ht_ps = sem("silu_done"), sem("hidden_done"), sem("hT_psum")
    ht_high, ht_low = sem("hT_high_done"), sem("hT_low_done")
    psq_done, pinv_done, prs_done = sem("post_square_sum"), sem("post_inverse"), sem("post_scale")
    h_done = sem("h_done")
    masks_one, masks_ok = sem("masks_one"), sem("masks_ok")
    sc_ps, sc_sb, abs_done, ln_done, sp_done = (sem("scores_psum"), sem("scores_copied"), sem("abs_done"),
                                                sem("ln_done"), sem("softplus_done"))
    sum_ps, loga_done, a_done, o_ps, o_done = (sem("suffix_psum"), sem("log_a_done"), sem("a_done"),
                                               sem("o_psum"), sem("o_copied"))
    wdt_high, wdt_ok, dt_ps = sem("w_dt_high_done"), sem("w_dt_split"), sem("dt_psum")
    dt_a, dt_d, conv_done, cv_done = sem("dt_act"), sem("dt_dve"), sem("conv_done"), sem("conv_silu")
    xs_ps, xs_sb, cb_ps, cb_ok = sem("xs_psum"), sem("xs_copied"), sem("cb_psum"), sem("cb_masked_done")
    acs_ps, acs_ok, au_ok, row_ps, lm_ok = (sem("a_cumsum_psum"), sem("a_cumsum_ok"), sem("adt_upto_ok"),
                                            sem("a_rows_psum"), sem("decay_exp"))
    m_ok, xd_ok, st_ps, st_ok, y_ps, y_used = (sem("m_ok"), sem("xs_dt_ok"), sem("state_psum"), sem("state_ok"),
                                       sem("y_psum"), sem("y_used"))
    hg_one, hg_ok = sem("hg_masks_one"), sem("hg_masks_ok")
    xs_sc, xs_max, xs_exp, xs_norm = sem("xa_scores"), sem("xa_max"), sem("xa_exp"), sem("xa_norm")
    xp_ps, xp_sb, xo_ps, xo_high, xo_low = (sem("xa_probsT_psum"), sem("xa_probsT_ok"), sem("xa_o_psum"),
                                            sem("xa_o_high"), sem("xa_o_low"))
    c2_d, c2_a, c2_p = sem("conv2_dve"), sem("conv2_act"), sem("conv2_pe")
    hg_d, hg_a, hg_p = sem("hg_dve"), sem("hg_act"), sem("hg_pe")
    kv_ps, s_ok = sem("kv_psum"), sem("states_ok")
    keys_in, iota_ok, injected = sem("keys_in"), sem("iota_ok"), sem("residual_in_psum")
    ks_ps, ks_sb, hot_one, hot_ok, hot_used = (
        sem("key_scores_psum"), sem("key_scores_copied"), sem("hot_one"), sem("hot_ok"), sem("hot_used"))
    gd_ok, gexp_ok, route_ok, rt_ps, rt_ok = (sem("gate_diff"), sem("gate_exp"), sem("route_ok"), sem("routeT_psum"),
                                              sem("routeT_ok"))
    key1_ok, key2_ok, hot4_ok, g_ps, g_sb = sem("ones_at_key1"), sem("ones_at_key2"), sem("gate_at_key1_ok"), sem("gates_psum"), sem("gates_copied")
    gelu_ok, prod_ok, wt_high, wt_low = (sem("gelu_done"), sem("weighted"), sem("weighted_high"),
                                         sem("weighted_low"))
    early_out = [sem(f"early_out{i}") for i in range(4)]
    early_in = [sem(f"early_in{i}") for i in range(4)]
    final_ok = sem("final_ok")
    yz_ok, z_silu, y_done = sem("yz_ok"), sem("z_silu"), sem("y_done")

    block = ctx.enter_context(nc.Block())

    @block.sync
    def _(sp):
        sp.dma_start(MEM[:], mem.rearrange("(t p) d -> p t d", p=P)).then_inc(mem_in, 16)
        sp.dma_start(COLS[:], cols).then_inc(const_in, 16)
        sp.dma_start(WDT[:], w_dt).then_inc(const_in, 16)
        sp.dma_start(SMALL[:], small_row[0].partition_broadcast(P)).then_inc(const_in, 16)
        for n in range(SLOTS):
            sp.dma_start(RING[:, n, :], stream[n]).then_inc(loaded[n], 16)
        sp.dma_start(H[:], x.rearrange("(t p) d -> p t d", p=P)).then_inc(x_in, 16)

        def load(n, dyn=None):
            sp.wait_ge(w_split, at(n - SLOTS + 1, dyn))
            src = stream[n] if dyn is None else stream[bass.ds(dyn + n, 1)].rearrange("a p c -> (a p) c")
            sp.dma_start(RING[:, n % SLOTS, :], src).then_inc(loaded[n % SLOTS], 16)

        b = BASE["peer"]
        with sp.Fori(0, (b + 8) // SLOTS - 1) as i:
            for n in range(SLOTS, 2 * SLOTS):
                load(n, i * SLOTS)
        with sp.Fori(0, SEARCH // SLOTS) as i:
            for n in range(SLOTS):
                load(b + 8 + n, i * SLOTS)
                sp.wait_ge(gelu_ok, i * SLOTS + (n + 1))
                sp.dma_start(early[bass.ds(i * SLOTS + n, 1)].rearrange("a p t -> (a p) t"), GE[:, n, :]
                             ).then_inc(early_out[n], 16)
        for n in range(SEARCH, EARLY):
            load(b + 8 + n)
            sp.wait_ge(gelu_ok, n + 1)
            sp.dma_start(early[n], GE[:, n % 2, :]).then_inc(early_out[n % 2], 16)

        def load_early(turn, k, dyn=None):
            n = 4 * turn + k
            src = early[n] if dyn is None else early[bass.ds(dyn * 4 + n, 1)].rearrange("a p t -> (a p) t")
            sp.dma_start(GE[:, k, :], src).then_inc(early_in[k], 16)

        for n in range(4):
            sp.wait_ge(early_out[n], 16 * EARLY_OUT[n])
        sp.wait_ge(g_sb, 64)
        for k in range(4):
            load_early(0, k)
        with sp.Fori(0, TURNS - 1) as i:
            for j in range(TURN):
                load(b + EARLY + 8 + j, i * TURN)
                if 5 <= j < 9:
                    sp.wait_ge(wt_low, i * 8 + j)
                    load_early(1, j - 5, i)
        for n in range(N_BLOCKS - 4, N_BLOCKS):
            load(n)
        sp.wait_ge(final_ok, 2)
        sp.dma_start(out.rearrange("(t p) d -> p t d", p=P), TMP[:]).then_inc(out_done, 16)
        sp.wait_ge(out_done, 16)

    @block.gpsimd
    def _(pool):
        pool.memset(IDENT[:], 0.0).then_inc(ident_zero, 1)
        pool.wait_ge(ident_zero, 1)
        pool.affine_select(out=IDENT[:], in_=IDENT[:], compare_op=ALU.not_equal, fill=1.0, base=0,
                           pattern=[[-1, P]], channel_multiplier=1).then_inc(ident_ok, 1)
        pool.dma_start(ROWG[:], rows[0].partition_broadcast(P)).then_inc(row_in, 16)
        for mask in (UPTO, FROM, BEFORE, CAP, ONES):
            pool.memset(mask[:], 1.0).then_inc(masks_one, 1)
        pool.memset(FUTURE[:], 0.0).then_inc(masks_one, 1)
        pool.wait_ge(masks_one, 6)
        for mask, sign, compare, fill in ((UPTO, 1, ALU.is_ge, 0.0), (FROM, -1, ALU.is_ge, 0.0),
                                          (BEFORE, 1, ALU.is_gt, 0.0), (CAP, 1, ALU.is_gt, -1e30),
                                          (FUTURE, 1, ALU.is_ge, -1e30)):
            pool.affine_select(out=mask[:], in_=mask[:], compare_op=compare, fill=fill, base=0,
                               pattern=[[sign, P]], channel_multiplier=-sign).then_inc(masks_ok, 1)

        def row_gain(k):
            pool.wait_ge(h_done, 2 * k)
            pool.dma_start(ROWG[:], rows[k].partition_broadcast(P)).then_inc(row_in, 16)

        def per_head(dst, src, heads):
            return pool.tensor_tensor(dst.rearrange("p (h d) -> p h d", d=64), src.rearrange("p (h d) -> p h d", d=64),
                                      heads.unsqueeze(2).to_broadcast([P, 16, 64]), ALU.mult)

        def ssd():
            pool.wait_ge(dt_d, 3)
            for tt in range(TT):
                if tt:
                    pool.wait_ge(row_ps, 1)
                pool.tensor_tensor(AU[:], SS[:, 12, tt * 16:tt * 16 + 16].unsqueeze(2).to_broadcast([P, 16, P]),
                                   UPTO[:].unsqueeze(1).to_broadcast([P, 16, P]), ALU.mult).then_inc(au_ok, 1)
                pool.wait_ge(xs_sb, 2 * (tt + 1))
                per_head(XD[:, tt, :], XSN[:, tt, :], SS[:, 10, tt * 16:tt * 16 + 16]).then_inc(xd_ok, 1)
                if tt == 0:
                    pool.wait_ge(dt_a, 4)
                    pool.wait_ge(xd_ok, 1)
                    per_head(XDD[:], XD[:, 0, :], SS[:, 15, 0:16]).then_inc(xd_ok, 1)
            pool.wait_ge(row_ps, 2)
            for tt in range(TT):
                per_head(YS[:, tt, :], XSN[:, tt, :], SMALL[:, 32:48]).then_inc(yz_ok, 1)

        row_gain(1)
        ssd()
        row_gain(2)
        row_gain(3)
        pool.wait_ge(h_done, 8)
        pool.memset(CHUNK_ON[:], 1.0).then_inc(hg_one, 1)
        pool.memset(ABD[:], 0.0).then_inc(hg_one, 1)
        pool.memset(GROUP64[:], 1.0 / 64).then_inc(hg_one, 1)
        pool.tensor_copy(IN_CHUNK[:], UPTO[:]).then_inc(hg_one, 1)
        pool.wait_ge(hg_one, 4)
        pool.memset(CHUNK_ON[:].rearrange("p (n c) -> p n c", c=HG_CHUNK)[:, :, 0:1], 0.0).then_inc(hg_ok, 1)
        pool.affine_select(out=IN_CHUNK[:], in_=IN_CHUNK[:], compare_op=ALU.is_ge, fill=0.0, base=0,
                           pattern=[[-HG_CHUNK, 4], [0, HG_CHUNK]], channel_multiplier=1).then_inc(hg_ok, 1)
        pool.affine_select(out=GROUP64[:], in_=GROUP64[:], compare_op=ALU.is_ge, fill=0.0, base=0,
                           pattern=[[-64, 2], [0, 64]], channel_multiplier=1).then_inc(hg_ok, 1)
        pool.wait_ge(hg_ok, 3)
        pool.affine_select(out=GROUP64[:], in_=GROUP64[:], compare_op=ALU.is_ge, fill=0.0, base=63,
                           pattern=[[64, 2], [0, 64]], channel_multiplier=-1).then_inc(hg_ok, 1)
        pool.wait_ge(h_done, 10)
        pool.dma_start(KEYS[:], keys).then_inc(keys_in, 16)
        pool.iota(IOTA[:], pattern=[[1, P]], base=0, channel_multiplier=0,
                  allow_small_or_imprecise_dtypes=True).then_inc(iota_ok, 1)
        pool.wait_ge(iota_ok, 1)
        for tt in range(TT):
            for p in range(2):
                pool.wait_ge(hot_one, 2 * tt + p + 1)
                hot = HOT[:, p, :, :].rearrange("p (h k) j -> p h k j", h=8)
                pool.tensor_tensor(hot, hot, TOP_ATF[:, tt, p:16:2, :].unsqueeze(2).to_broadcast([P, 8, 16, 16]),
                                   ALU.mult).then_inc(hot_ok, 1)

        with pool.Fori(0, SEQ // 8) as i:
            for q in range(2):
                pool.wait_ge(key1_ok, i * 2 + (q + 1))
                hot = OA[:, 4 * q:4 * q + 4, :]
                gate = ROUTE_T[:, 2, bass.ds(i * 8 + 4 * q, 4)].unsqueeze(2).to_broadcast([P, 4, P])
                pool.tensor_tensor(hot, hot, gate, ALU.mult).then_inc(hot4_ok, 1)

        def product(v, k, tile, dyn=None):
            g = GATES[:, tile, :] if dyn is None else GATES[:, bass.ds(dyn * 4 + tile, 1), :]
            if dyn is not None:
                g = g.rearrange("p a t -> p (a t)")
            pool.tensor_tensor(GE[:, k, :], GE[:, k, :], g, ALU.mult).then_inc(prod_ok, 1)

        pool.wait_ge(g_sb, 64)
        for k in range(4):
            pool.wait_ge(early_in[k], 16)
            product(k, k, k)
        with pool.Fori(0, TURNS - 1) as i:
            for k in range(4):
                pool.wait_ge(gelu_ok, i * 4 + (EARLY + k + 1))
                product(4 + k, k, EARLY + k, i)
            for k in range(4):
                pool.wait_ge(early_in[k], i * 16 + 32)
                product(8 + k, k, 4 + k, i)
        for k in range(4):
            pool.wait_ge(gelu_ok, 2 * EARLY - 4 + k + 1)
            product(2 * EARLY - 4 + k, k, 2 * EARLY - 4 + k)
        pool.wait_ge(prod_ok, 2 * EARLY)
        pool.dma_start(ROWG[:], rows[4].partition_broadcast(P)).then_inc(row_in, 16)

    @block.scalar
    def _(act):
        chain = Chain(act, act_chain)

        def split(n0, count, dyn=None):
            for n in range(n0, n0 + count):
                act.wait_ge(loaded[n % SLOTS], at(16 * (n // SLOTS + 1), dyn, 16 // SLOTS))
                if dyn is not None or n >= SLOTS:
                    act.wait_ge(w_used, at(n - SLOTS + 1, dyn))
                act.activation(WH[:, n % SLOTS, :], RING[:, n % SLOTS, :], ACT.Copy).then_inc(w_high, 1)

        def split_run(n0, count):
            groups = count // SLOTS
            if groups > 1:
                with act.Fori(0, groups) as i:
                    split(n0, SLOTS, i * SLOTS)
            else:
                groups = 0
            split(n0 + groups * SLOTS, count - groups * SLOTS)

        def prenorm(k, src, gain, high=XTH, k0=0, groups=1, updates=None):
            w = D // groups
            for tt in range(TT):
                if updates is not None:
                    act.wait_ge(h_done, updates + tt + 1)
                for g in range(groups):
                    n = tt * groups + g
                    act.activation(XN[:, tt, g * w:g * w + w], src[:, tt, g * w:g * w + w], ACT.Square,
                                   accum_out=STAT[:, n:n + 1]).then_inc(sq_done, 1)
            act.wait_ge(inv_done, k + 1)
            n = TT * groups
            chain(act.activation(STAT[:, 8:8 + n], STAT[:, 4:4 + n], ACT.Sqrt))
            act.activation(STAT[:, 12:12 + n], STAT[:, 8:8 + n], ACT.Copy).then_inc(rs_done, 1)
            for g in range(groups):
                last = act.activation(XN[:, 0, g * w:g * w + w], src[:, 0, g * w:g * w + w], ACT.Copy,
                                      scale=STAT[:, 8 + g:9 + g])
            last.then_inc(xn_act, 1)
            for kt in range(KT):
                act.wait_ge(xt_ps, k * KT // 2 + kt // 2 + 1)
                act.activation(high[:, k0 + kt, :], XT_PS[:, kt, :], ACT.Copy,
                               scale=COLS[:, GAIN_COL[gain] + kt:GAIN_COL[gain] + kt + 1]).then_inc(xt_high, 1)

        def evac(stage, dst, n, parity, dyn=None):
            act.wait_ge(w_used, at(BASE[stage] + PB * (n + 1), dyn, PB))
            act.activation(dst(n, dyn)[:, 0:512], PAIR[parity][:, 0:512], ACT.Copy).then_inc(evac_a, 1)

        def ffn_up(stage, f):
            b, e = BASE[stage], f * FFN_PANELS

            def silu(p, parity, dyn=None):
                act.wait_ge(w_used, at(b + PB * (p + 1), dyn, PB))
                if dyn is not None or e + p >= 2:
                    act.wait_ge(hidden_done, at(e + p - 1, dyn))
                act.activation(SG[:, parity, :, :],
                               PAIR[parity].rearrange("p (t n) -> p t n", t=TT)[:, :, 0:256],
                               ACT.Silu).then_inc(silu_done, 1)

            def high(p, parity, dyn=None):
                act.wait_ge(ht_ps, at(e + p + 1, dyn))
                act.activation(HTH[:, bass.ds(at(2 * p, dyn, 2), 2), :] if dyn is not None
                               else HTH[:, 2 * p:2 * p + 2, :],
                               ACC[:, 0, 512 * parity:512 * parity + 512].rearrange("p (k t) -> p k t", k=2),
                               ACT.Copy).then_inc(ht_high, 1)

            split(b + PB, PB)
            silu(0, 0)
            with act.Fori(0, (FFN_PANELS - 3) // 2) as i:
                for p in (2, 3):
                    split(b + PB * p, PB, i * (2 * PB))
                    silu(p - 1, (p - 1) % 2, i * 2)
                    high(p - 2, p % 2, i * 2)
            p = FFN_PANELS - 1
            split(b + PB * p, PB)
            silu(p - 1, (p - 1) % 2)
            high(p - 2, p % 2)
            split(b + PB * FFN_PANELS, PB)
            silu(p, p % 2)
            high(p - 1, (p - 1) % 2)
            high(p, p % 2)

        def post_square(k):
            for tt in range(TT):
                act.activation(XN[:, tt, :], ACC[:, tt, :], ACT.Square,
                               accum_out=STAT[:, 16 + tt:17 + tt]).then_inc(psq_done, 1)
            act.wait_ge(pinv_done, k + 1)
            act.activation(STAT[:, 20:22], STAT[:, 18:20], ACT.Sqrt).then_inc(prs_done, 1)

        def plain(stage, panels, dst):
            b = BASE[stage]
            for n in range(1, panels):
                split(b + PB * n, PB)
                evac(stage, dst, n - 1, (n - 1) % 2)
            split(b + PB * panels, PB)
            evac(stage, dst, panels - 1, (panels - 1) % 2)

        split(0, PB)
        act.wait_ge(const_in, 48)
        act.activation(WDTH[:], WDT[:], ACT.Copy).then_inc(wdt_high, 1)
        act.wait_ge(mem_in, 16)
        prenorm(0, MEM, "mem")
        plain("xa_kv", 4, kv_dst)
        act.wait_ge(x_in, 16)
        prenorm(1, H, "ffn1")
        ffn_up("ffn1_up", 0)
        split_run(BASE["ffn1_down"] + PB, FFN_KT)
        act.wait_ge(w_used, BASE["w_in"])
        post_square(0)

        def attention_half(k):
            if k < 8:
                act.wait_ge(sc_ps, k + 1)
                if k >= 2:
                    act.wait_ge(sp_done, k - 1)
                    act.wait_ge(loga_done, k - 1)
                act.activation(by_head(ZS, k), S_PS[:, :, 0:384], ACT.Copy, scale=0.125).then_inc(sc_sb, 1)
                act.wait_ge(abs_done, k + 1)
                if k >= 2:
                    act.wait_ge(sum_ps, k - 1)
                chain(act.activation(SPL[:, k % 2, :], SPL[:, k % 2, :], ACT.Exp))
                act.activation(SPL[:, k % 2, :], SPL[:, k % 2, :], ACT.Ln, bias=1.0).then_inc(ln_done, 1)
            if 1 <= k <= 8:
                act.wait_ge(loga_done, k)
                act.activation(LOGA[:, (k - 1) % 2, :], LOGA[:, (k - 1) % 2, :], ACT.Exp).then_inc(a_done, 1)
            if k >= 2:
                act.wait_ge(o_ps, k - 1)
                act.activation(AO[:, :, (k - 2) * P:(k - 1) * P].rearrange("p t (h n) -> p h t n", h=2),
                               C_PS[:, :, 384:512].rearrange("p h (t n) -> p h t n", t=TT), ACT.Copy).then_inc(o_done, 1)

        prenorm(2, H, "mix", updates=0)
        b = BASE["w_in"]
        with act.Fori(0, 3) as i:
            for p in (0, 1):
                split(b + PB * (p + 1), PB, i * (2 * PB))
                evac("w_in", mixer_dst, p, p, i * 2)
        act.preload_act_table_set("natural_log_exp_and_others")
        for k in range(10):
            attention_half(k)
            split(b + PB * 7 + 2 * k, 2)
            if k % 2:
                evac("w_in", mixer_dst, 6 + k // 2, (k // 2) % 2)
        act.activation(SS[:, 11, 0:16], SMALL[:, 16:32], ACT.Exp).then_inc(dt_a, 1)
        act.wait_ge(dt_d, 1)
        act.activation(SS[:, 2, :], SS[:, 1, :], ACT.Exp).then_inc(dt_a, 1)
        act.wait_ge(dt_d, 2)
        act.activation(SS[:, 4, :], SS[:, 3, :], ACT.Ln).then_inc(dt_a, 1)
        act.wait_ge(acs_ok, 1)
        act.activation(SS[:, 15, 0:16], SS[:, 14, 0:16], ACT.Exp)
        act.activation(SS[:, 15, 16:32], SS[:, 13, 16:32], ACT.Exp, scale=-1.0).then_inc(dt_a, 1)
        for b3 in range(3):
            act.wait_ge(conv_done, 4 * (b3 + 1))
            act.activation(CV[:, 4 * b3:4 * b3 + 4, :], CV[:, 4 * b3:4 * b3 + 4, :], ACT.Silu).then_inc(cv_done, 1)
        act.wait_ge(evac_d, EVAC["w_in"] + 11)
        act.wait_ge(evac_a, EVAC["w_in"] + 11)
        act.activation(Z, Z, ACT.Silu).then_inc(z_silu, 1)
        for tt in range(TT):
            act.wait_ge(xs_ps, tt + 1)
            act.activation(XSN[:, tt, 0:512], PS[:, 0:512], ACT.Copy).then_inc(xs_sb, 1)
            act.wait_ge(row_ps, tt + 1)
            if tt:
                act.wait_ge(y_ps, 1)
            for h in range(16):
                last = act.activation(LM[:, h, :], PS[:, 2048 + h * P:2048 + (h + 1) * P], ACT.Exp,
                                      bias=SS[:, 13, tt * 16 + h:tt * 16 + h + 1])
            last.then_inc(lm_ok, 1)
            if tt == 0:
                act.wait_ge(st_ps, 1)
                act.activation(ST[:], PS[:, 1024:2048], ACT.Copy).then_inc(st_ok, 1)
        act.wait_ge(y_done, 2)
        prenorm(3, AO, "attn", HTH)
        prenorm(4, YS, "ssd", HTH, 8, groups=2)
        split_run(BASE["w_out"] + PB, 16)
        act.wait_ge(w_used, BASE["xa_q"])
        post_square(1)
        prenorm(5, H, "xa", updates=2)
        plain("xa_q", 2, mixer_dst)
        for tt in range(TT):
            act.wait_ge(xs_max, tt + 1)
            for h in range(4):
                n = tt * 4 + h
                last = act.activation(PE_[:, tt, h, :], ACC[:, tt, h * SEQ:(h + 1) * SEQ], ACT.Exp, scale=1.0 / 16,
                                      bias=STAT[:, 32 + n:33 + n], accum_out=STAT[:, 40 + n:41 + n])
            last.then_inc(xs_exp, 1)
        act.wait_ge(xp_ps, 1)
        act.activation(PT[:, 0:4, :], XT_PS[:, 0:4, :], ACT.Copy).then_inc(xp_sb, 1)
        for bank in range(4):
            act.wait_ge(xo_ps, bank + 1)
            act.activation(HTH[:, 2 * bank:2 * bank + 2, :],
                           PS[:, 2048 + bank * 512:2560 + bank * 512].rearrange("p (k t) -> p k t", k=2),
                           ACT.Copy).then_inc(xo_high, 1)
        split_run(BASE["xa_o"] + PB, 8)
        act.wait_ge(w_used, BASE["ffn2_up"])
        post_square(2)
        prenorm(6, H, "ffn2", updates=4)
        ffn_up("ffn2_up", 1)
        split_run(BASE["ffn2_down"] + PB, FFN_KT)
        act.wait_ge(w_used, BASE["w_in_2"])
        post_square(3)
        prenorm(7, H, "mix2", updates=6)
        plain("w_in_2", 7, mixer_dst)
        act.wait_ge(evac_a, EVAC["w_in_2"] + 7)
        act.wait_ge(evac_d, EVAC["w_in_2"] + 7)
        act.wait_ge(hg_d, 1)
        act.activation(LBS[:, 2:4, :], LBS[:, 0:2, :], ACT.Exp).then_inc(hg_a, 1)
        act.activation(FG[:], F2, ACT.Sigmoid).then_inc(hg_a, 1)
        act.activation(Q2, Q2, ACT.Silu)
        act.activation(G2, G2, ACT.Silu).then_inc(hg_a, 1)
        act.preload_act_table_set("natural_log_exp_and_others")
        act.wait_ge(hg_d, 2)
        act.activation(GC[:], FG[:], ACT.Ln).then_inc(hg_a, 1)
        act.wait_ge(hg_d, 3)
        act.activation(EG[:], GC[:], ACT.Exp).then_inc(hg_a, 1)
        act.activation(KD[:], GC[:], ACT.Exp, scale=-1.0).then_inc(hg_a, 1)
        act.wait_ge(hg_d, 4)
        act.activation(KEN[:], KEN[:], ACT.Exp).then_inc(hg_a, 1)
        act.wait_ge(c2_d, 1)
        act.activation(MS[:], Y[:], ACT.Square).then_inc(c2_a, 1)
        act.wait_ge(hg_p, 1)
        act.activation(KE[:].rearrange("p t h n -> p (t h n)"), PS[:, 0:1024], ACT.Copy).then_inc(hg_a, 1)
        act.wait_ge(kv_ps, 1)
        act.activation(ST2[:, 0, :, :].rearrange("p h n -> p (h n)"), PS[:, 2048:2560], ACT.Copy).then_inc(s_ok, 1)
        act.wait_ge(c2_d, 2)
        act.activation(MS[:], MS[:], ACT.Sqrt).then_inc(c2_a, 1)
        act.wait_ge(c2_d, 3)
        act.activation(XTH[:, 0:4, :], Y[:], ACT.Copy).then_inc(c2_a, 1)
        act.wait_ge(hg_p, 4)
        for n in range(8):
            last = act.activation(U[:, n // 2, n % 2 * P:n % 2 * P + P], PS[:, n * P:(n + 1) * P], ACT.Square, accum_out=STAT[:, 32 + n:33 + n])
        last.then_inc(hg_a, 1)
        act.wait_ge(hg_d, 8)
        act.activation(STAT[:, 48:56], STAT[:, 40:48], ACT.Sqrt).then_inc(hg_a, 1)
        act.wait_ge(hg_p, 5)
        act.activation(XTH[:, 4:8, :], XT_PS[:, 4:8, :], ACT.Copy, scale=COLS[:, HG_GAIN:HG_GAIN + 1]).then_inc(hg_a, 1)
        split_run(BASE["w_out_2"] + PB, 8)

        prenorm(8, H, "peer", updates=8)
        plain("peer_q", 4, mixer_dst)
        for tt in range(TT):
            act.wait_ge(ks_ps, tt + 1)
            act.activation(SC[:, tt, :, :].rearrange("p a n -> p (a n)"), PS[:, 2048:4096], ACT.Copy).then_inc(ks_sb, 1)
        act.wait_ge(injected, 1)
        b = BASE["peer"]

        def early_tile(n, buf, written, dyn=None):
            act.wait_ge(w_used, at(b + n + 1, dyn, 4))
            if dyn is not None or written:
                act.wait_ge(early_out[buf], at(16 * written, dyn, 16))
            act.activation(GE[:, buf, :], PS[:, n % 2 * 512:n % 2 * 512 + SEQ], ACT.Gelu).then_inc(gelu_ok, 1)
            split(b + n + 4, 1, None if dyn is None else dyn * 4)

        for n in range(4):
            early_tile(n, n, 0)
        with act.Fori(1, SEARCH // 4) as i:
            for n in range(4):
                early_tile(n, n, 0, i)
        for tt in range(TT):
            act.wait_ge(gd_ok, tt + 1)
            act.activation(CTOP[:, tt, :, :], CTOP[:, tt, :, :], ACT.Exp).then_inc(gexp_ok, 1)

        def route_copy(tt):
            act.wait_ge(rt_ps, tt + 1)
            act.activation(ROUTE_T[:, :, tt * P:(tt + 1) * P], PS[:, 1024:1408].rearrange("p (a n) -> p a n", a=3),
                           ACT.Copy).then_inc(rt_ok, 1)

        def gates_copy(group, dyn=None):
            act.wait_ge(g_ps, at(group + 1, dyn))
            t = bass.ds(at(4 * group, dyn, 4), 4)
            o = 1024 + 512 * (group % 2)
            act.activation(GATES[:, :, t], PS[:, o:o + 512].rearrange("p (t n) -> p n t", t=4),
                           ACT.Copy).then_inc(g_sb, 1)

        act.wait_ge(early_out[2], 16 * EARLY_OUT[2])
        act.wait_ge(early_out[3], 16 * EARLY_OUT[3])
        route_copy(0)
        route_copy(1)
        for n in range(EARLY - SEARCH):
            early_tile(SEARCH + n, n % 2, SEARCH // 4 + n // 2)
            with act.Fori(0, GROUPS // 2) as i:
                for g in range(2):
                    gates_copy(GROUPS * n + g, i * 2)

        def high(v, dyn=None, last_use=None):
            act.wait_ge(prod_ok, at(v + 1, dyn, 8))
            if last_use is not None:
                act.wait_ge(w_used, at(last_use + 1, dyn, TURN))
            act.activation(WTH[:, v % 4, :], GE[:, v % 4, :], ACT.Copy).then_inc(wt_high, 1)

        def u_tile(k, dyn=None):
            act.wait_ge(w_used, at(b + EARLY + k + 1, dyn, TURN))
            act.wait_ge(wt_low, at(k + 1, dyn, 8))
            act.activation(GE[:, k, :], PS[:, k * 512:k * 512 + SEQ], ACT.Gelu).then_inc(gelu_ok, 1)

        m = b + EARLY
        for k in range(4):
            high(k)
        with act.Fori(0, TURNS - 1) as i:
            for k in range(4):
                u_tile(k, i)
                split(m + k + 4, 1, i * TURN)
            for k in range(4):
                high(4 + k, i, m + 4 + k)
                split(m + k + 8, 1, i * TURN)
            for k in range(4):
                high(8 + k, i, m + 8 + k)
                split(m + k + 12, 1, i * TURN)
        m, v, t = m + (TURNS - 1) * TURN, (TURNS - 1) * 8, TURNS - 1
        for k in range(4):
            act.wait_ge(w_used, m + k + 1)
            act.wait_ge(wt_low, v + k + 1)
            act.activation(GE[:, k, :], PS[:, k * 512:k * 512 + SEQ], ACT.Gelu).then_inc(gelu_ok, 1)
            split(m + k + 4, 1)
        for k in range(4):
            high(v + 4 + k, None, m + 4 + k)
            split(m + k + 8, 1)
        act.wait_ge(w_used, N_BLOCKS)
        post_square(4)

    @block.vector
    def _(dve):
        chain = Chain(dve, dve_chain)

        def split(n0, count, dyn=None):
            for n in range(n0, n0 + count):
                dve.wait_ge(w_high, at(n + 1, dyn))
                dve.tensor_tensor(WL[:, n % SLOTS, :], RING[:, n % SLOTS, :],
                                  WH[:, n % SLOTS, :].bitcast(F32), ALU.subtract).then_inc(w_split, 1)

        def split_run(n0, count):
            groups = count // SLOTS
            if groups > 1:
                with dve.Fori(0, groups) as i:
                    split(n0, SLOTS, i * SLOTS)
            else:
                groups = 0
            split(n0 + groups * SLOTS, count - groups * SLOTS)

        def inverse(src, dst, width=D):
            chain(dve.tensor_scalar(dst, src, 1.0 / width, EPS, ALU.mult, ALU.add))
            return dve.reciprocal(dst, dst)

        def prenorm(k, src, gain, high=XTH, low=XTL, k0=0, groups=1):
            n, w = TT * groups, D // groups
            dve.wait_ge(sq_done, SQUARES[k + 1])
            inverse(STAT[:, 0:n], STAT[:, 4:4 + n], w).then_inc(inv_done, 1)
            dve.wait_ge(rs_done, k + 1)
            for g in range(groups):
                last = dve.tensor_scalar(XN[:, 1, g * w:g * w + w], src[:, 1, g * w:g * w + w],
                                         STAT[:, 12 + groups + g:13 + groups + g], None, ALU.mult)
            last.then_inc(xn_dve, 1)
            for kt in range(KT):
                dve.wait_ge(xt_high, k * KT + (kt | 1) + 1)
                dve.scalar_tensor_tensor(low[:, k0 + kt, :], XT_PS[:, kt, :],
                                         COLS[:, GAIN_COL[gain] + kt:GAIN_COL[gain] + kt + 1],
                                         high[:, k0 + kt, :].bitcast(F32), ALU.mult, ALU.subtract).then_inc(xt_low, 1)

        def evac(stage, dst, n, parity, dyn=None):
            dve.wait_ge(w_used, at(BASE[stage] + PB * (n + 1), dyn, PB))
            dve.tensor_copy(dst(n, dyn)[:, 512:1024], PAIR[parity][:, 512:1024]).then_inc(evac_d, 1)

        def ffn_up(stage, f):
            b, e = BASE[stage], f * FFN_PANELS

            def hidden(p, parity, dyn=None):
                dve.wait_ge(silu_done, at(e + p + 1, dyn))
                if dyn is not None or e + p >= 2:
                    dve.wait_ge(ht_ps, at(e + p - 1, dyn))
                dve.tensor_tensor(HN[:, parity, :, :], SG[:, parity, :, :],
                                  PAIR[parity].rearrange("p (t n) -> p t n", t=TT)[:, :, 256:512],
                                  ALU.mult).then_inc(hidden_done, 1)

            def low(p, parity, dyn=None):
                dve.wait_ge(ht_high, at(e + p + 1, dyn))
                w = bass.ds(at(2 * p, dyn, 2), 2) if dyn is not None else slice(2 * p, 2 * p + 2)
                dve.tensor_tensor(HTL[:, w, :],
                                  ACC[:, 0, 512 * parity:512 * parity + 512].rearrange("p (k t) -> p k t", k=2),
                                  HTH[:, w, :].bitcast(F32), ALU.subtract).then_inc(ht_low, 1)

            split(b + PB, PB)
            hidden(0, 0)
            with dve.Fori(0, (FFN_PANELS - 3) // 2) as i:
                for p in (2, 3):
                    split(b + PB * p, PB, i * (2 * PB))
                    hidden(p - 1, (p - 1) % 2, i * 2)
                    low(p - 2, p % 2, i * 2)
            p = FFN_PANELS - 1
            split(b + PB * p, PB)
            hidden(p - 1, (p - 1) % 2)
            low(p - 2, p % 2)
            split(b + PB * FFN_PANELS, PB)
            hidden(p, p % 2)
            low(p - 1, (p - 1) % 2)
            low(p, p % 2)

        def post_add(k, factor):
            dve.wait_ge(psq_done, 2 * (k + 1))
            inverse(STAT[:, 16:18], STAT[:, 18:20]).then_inc(pinv_done, 1)
            dve.wait_ge(prs_done, k + 1)
            dve.wait_ge(row_in, 16 * (k + 1))
            for tt in range(TT):
                chain(dve.scalar_tensor_tensor(TMP[:, tt, :], ACC[:, tt, :], STAT[:, 20 + tt:21 + tt],
                                               ROWG[:], ALU.mult, ALU.mult))
                dve.scalar_tensor_tensor(H[:, tt, :], TMP[:, tt, :], factor, H[:, tt, :],
                                         ALU.mult, ALU.add).then_inc(h_done, 1)

        def plain(stage, panels, dst):
            b = BASE[stage]
            for n in range(1, panels):
                split(b + PB * n, PB)
                evac(stage, dst, n - 1, (n - 1) % 2)
            split(b + PB * panels, PB)
            evac(stage, dst, panels - 1, (panels - 1) % 2)

        split(0, PB)
        dve.wait_ge(const_in, 48)
        dve.wait_ge(wdt_high, 1)
        dve.tensor_tensor(WDTL[:], WDT[:], WDTH[:].bitcast(F32), ALU.subtract).then_inc(wdt_ok, 1)
        dve.wait_ge(mem_in, 16)
        prenorm(0, MEM, "mem")
        plain("xa_kv", 4, kv_dst)
        dve.wait_ge(x_in, 16)
        prenorm(1, H, "ffn1")
        ffn_up("ffn1_up", 0)
        split_run(BASE["ffn1_down"] + PB, FFN_KT)
        post_add(0, 0.5)

        def diagonals(t, k):
            return t[:, k % 2, :].rearrange("p (h x n) -> p h x n", h=2, x=3)[:, :, 0:3:2, :]

        def over_diagonals(mask):
            return mask[:].unsqueeze(1).unsqueeze(1).to_broadcast([P, 2, 2, P])

        def attention_half(k):
            if k < 8:
                dve.wait_ge(sc_sb, k + 1)
                if k >= 2:
                    dve.wait_ge(sum_ps, k - 1)
                dve.scalar_tensor_tensor(SPL[:, k % 2, :], ZS[:, k % 2, :], -1.0, ZS[:, k % 2, :],
                                         ALU.mult, ALU.min).then_inc(abs_done, 1)
                dve.wait_ge(ln_done, k + 1)
                chain(dve.scalar_tensor_tensor(SPL[:, k % 2, :], ZS[:, k % 2, :], 0.0, SPL[:, k % 2, :],
                                               ALU.max, ALU.add))
                dve.tensor_tensor(diagonals(SPL, k), diagonals(SPL, k), over_diagonals(BEFORE),
                                  ALU.mult).then_inc(sp_done, 1)
            if 1 <= k <= 8:
                j = k - 1
                dve.wait_ge(sum_ps, k)
                if j >= 1:
                    dve.wait_ge(o_ps, j)
                if j >= 2:
                    dve.wait_ge(o_ps, j - 1)
                chain(dve.tensor_tensor(by_head(LOGA, j), by_head(ZS, j), C_PS[:, :, 0:384], ALU.subtract))
                dve.tensor_tensor(diagonals(LOGA, j), diagonals(LOGA, j), over_diagonals(CAP),
                                  ALU.min).then_inc(loga_done, 1)

        dve.wait_ge(h_done, 2)
        prenorm(2, H, "mix")
        b = BASE["w_in"]
        with dve.Fori(0, 3) as i:
            for p in (0, 1):
                split(b + PB * (p + 1), PB, i * (2 * PB))
                evac("w_in", mixer_dst, p, p, i * 2)
        dve.wait_ge(masks_ok, 5)
        for k in range(10):
            attention_half(k)
            split(b + PB * 7 + 2 * k, 2)
            if k % 2:
                evac("w_in", mixer_dst, 6 + k // 2, (k // 2) % 2)

        def both(heads):
            return heads.unsqueeze(1).to_broadcast([P, TT, 16])

        def two(row):
            return SS[:, row, :].rearrange("p (t h) -> p t h", t=TT)

        dve.wait_ge(dt_ps, 1)
        chain(dve.tensor_tensor(two(0), PS[:, 1024:1056].rearrange("p (t h) -> p t h", t=TT),
                                both(SMALL[:, 0:16]), ALU.add))
        dve.scalar_tensor_tensor(SS[:, 1, :], SS[:, 0, :], -1.0, SS[:, 0, :], ALU.mult, ALU.min).then_inc(dt_d, 1)
        dve.wait_ge(dt_a, 2)
        chain(dve.tensor_scalar(SS[:, 3, :], SS[:, 2, :], 1.0, None, ALU.add))
        dve.tensor_scalar(SS[:, 6, :], SS[:, 3, :], -1.0, 1e-30, ALU.add, ALU.add).then_inc(dt_d, 1)
        dve.wait_ge(dt_d, 2)
        chain(dve.reciprocal(SS[:, 7, :], SS[:, 6, :]))
        dve.wait_ge(dt_a, 3)
        chain(dve.scalar_tensor_tensor(SS[:, 8, :], SS[:, 4, :], 1e-30, SS[:, 7, :], ALU.add, ALU.mult))
        chain(dve.tensor_tensor(SS[:, 9, :], SS[:, 8, :], SS[:, 2, :], ALU.mult))
        chain(dve.scalar_tensor_tensor(SS[:, 10, :], SS[:, 0, :], 0.0, SS[:, 9, :], ALU.max, ALU.add))
        dve.scalar_tensor_tensor(two(12), two(10), -1.0, both(SS[:, 11, 0:16]), ALU.mult, ALU.mult
                                 ).then_inc(dt_d, 1)
        dve.wait_ge(acs_ps, 1)
        chain(dve.tensor_scalar(SS[:, 13, :], PS[:, 1088:1120], -1.0, None, ALU.mult))
        dve.tensor_tensor(SS[:, 14, 0:16], PS[:, 1120:1136], SS[:, 13, 0:16], ALU.add).then_inc(acs_ok, 1)
        dve.wait_ge(evac_a, EVAC["w_in"] + 9)
        with dve.Fori(0, 12) as i:
            tile, x = CV[:, bass.ds(i, 1), :], XBC[:, bass.ds(i, 1), :]
            tile, x = tile.rearrange("p a t -> p (a t)"), x.rearrange("p a t -> p (a t)")
            tap = [COLS[:, bass.ds(i * 4 + (CONV_W + j), 1)] for j in range(4)]
            chain.enter(i, 3)
            chain(dve.tensor_scalar(tile, x, tap[3], COLS[:, bass.ds(i + CONV_B, 1)], ALU.mult, ALU.add))
            for back in (1, 2):
                chain(dve.scalar_tensor_tensor(tile[:, back:], x[:, :SEQ - back], tap[3 - back], tile[:, back:],
                                               ALU.mult, ALU.add))
            dve.scalar_tensor_tensor(tile[:, 3:], x[:, :SEQ - 3], tap[0], tile[:, 3:],
                                     ALU.mult, ALU.add).then_inc(conv_done, 1)
            chain.leave(12)
        dve.wait_ge(cb_ps, 1)
        dve.tensor_copy(BN[:], PS[:, 1152:1408].rearrange("p (g n) -> p g n", g=2)).then_inc(cb_ok, 1)
        dve.tensor_tensor(CBM[:].rearrange("p t g n -> p (t g) n"), PS[:, 1536:2048].rearrange("p (a n) -> p a n", a=4),
                          UPTO[:].unsqueeze(1).to_broadcast([P, 4, P]), ALU.mult).then_inc(cb_ok, 1)
        dve.wait_ge(cb_ok, 2)
        for tt in range(TT):
            dve.wait_ge(xs_ps, tt + 1)
            dve.tensor_copy(XSN[:, tt, 512:1024], PS[:, 512:1024]).then_inc(xs_sb, 1)
        for tt in range(TT):
            dve.wait_ge(lm_ok, tt + 1)
            for g in range(2):
                m = LM[:, 8 * g:8 * g + 8, :]
                last = dve.tensor_tensor(m, m, CBM[:, tt, g, :].unsqueeze(1).to_broadcast([P, 8, P]), ALU.mult)
            last.then_inc(m_ok, 1)
            dve.wait_ge(y_ps, tt + 1)
            dve.wait_ge(yz_ok, tt + 1)
            y = YS[:, tt, :]
            chain(dve.tensor_tensor(y, y, PS[:, 0:1024], ALU.add))
            if tt:
                chain(dve.tensor_tensor(XDD[:].rearrange("p (h d) -> p h d", d=64),
                                        PS[:, 1024:2048].rearrange("p (h d) -> p h d", d=64),
                                        SS[:, 15, 16:32].unsqueeze(2).to_broadcast([P, 16, 64]), ALU.mult))
                chain(dve.tensor_tensor(y, y, XDD[:], ALU.add))
            dve.wait_ge(z_silu, 1)
            dve.tensor_tensor(y.rearrange("p (a n) -> p a n", a=2), y.rearrange("p (a n) -> p a n", a=2),
                              Z[:, :, tt, :], ALU.mult).then_inc(y_done, 1)
        dve.wait_ge(y_done, 2)
        prenorm(3, AO, "attn", HTH, HTL)
        prenorm(4, YS, "ssd", HTH, HTL, 8, groups=2)
        split_run(BASE["w_out"] + PB, 16)
        post_add(1, 1.0)
        prenorm(5, H, "xa")
        plain("xa_q", 2, mixer_dst)
        for tt in range(TT):
            dve.wait_ge(xs_sc, tt + 1)
            s = slice(tt * 4, tt * 4 + 4)
            chain(dve.reduce_max(STAT[:, 24:32][:, s], ACC[:, tt, :].rearrange("p (h m) -> p h m", h=4), AX_X))
            dve.tensor_scalar(STAT[:, 32:40][:, s], STAT[:, 24:32][:, s], -1.0 / 16, None, ALU.mult).then_inc(xs_max, 1)
        for tt in range(TT):
            dve.wait_ge(xs_exp, tt + 1)
            s = slice(tt * 4, tt * 4 + 4)
            chain(dve.reciprocal(STAT[:, 48:56][:, s], STAT[:, 40:48][:, s]))
            dve.tensor_tensor(PE_[:, tt, :, :], PE_[:, tt, :, :],
                              STAT[:, 48:56][:, s].unsqueeze(2).to_broadcast([P, 4, SEQ]), ALU.mult).then_inc(xs_norm, 1)
        dve.wait_ge(xp_ps, 2)
        dve.tensor_copy(PT[:, 4:8, :], XT_PS[:, 4:8, :]).then_inc(xp_sb, 1)
        for bank in range(4):
            dve.wait_ge(xo_high, bank + 1)
            k2 = slice(2 * bank, 2 * bank + 2)
            dve.tensor_tensor(HTL[:, k2, :], PS[:, 2048 + bank * 512:2560 + bank * 512].rearrange("p (k t) -> p k t", k=2),
                              HTH[:, k2, :].bitcast(F32), ALU.subtract).then_inc(xo_low, 1)
        split_run(BASE["xa_o"] + PB, 8)
        post_add(2, 1.0)
        prenorm(6, H, "ffn2")
        ffn_up("ffn2_up", 1)
        split_run(BASE["ffn2_down"] + PB, FFN_KT)
        post_add(3, 0.5)
        prenorm(7, H, "mix2")
        lb = COLS[:, LB:LB + 8].rearrange("p (r f) -> p r f", r=2)
        chain(dve.tensor_tensor(LBS[:, 4, :], lb[:, 0, :], lb[:, 1, :], ALU.max))
        dve.tensor_tensor(LBS[:, 0:2, :], lb, LBS[:, 4, :].unsqueeze(1).to_broadcast([P, 2, 4]),
                          ALU.subtract).then_inc(hg_d, 1)
        plain("w_in_2", 7, mixer_dst)
        dve.wait_ge(evac_a, EVAC["w_in_2"] + 7)
        dve.wait_ge(evac_d, EVAC["w_in_2"] + 7)
        dve.wait_ge(hg_a, 1)
        chain(dve.tensor_tensor(LBS[:, 4, :], LBS[:, 2, :], LBS[:, 3, :], ALU.add))
        chain(dve.reciprocal(LBS[:, 5, :], LBS[:, 4, :]))
        chain(dve.tensor_tensor(LBS[:, 6, :], LBS[:, 2, :], LBS[:, 5, :], ALU.mult))
        chain(dve.tensor_scalar(LBS[:, 7, :], LBS[:, 6, :], -1.0, 1.0, ALU.mult, ALU.add))
        dve.wait_ge(hg_a, 2)
        for ft in range(4):
            last = dve.tensor_scalar(FG[:, ft, :], FG[:, ft, :], LBS[:, 7, ft:ft + 1], LBS[:, 6, ft:ft + 1],
                                     ALU.mult, ALU.add)
        last.then_inc(hg_d, 1)
        dve.wait_ge(hg_d, 2)
        chain(dve.tensor_scalar(KH[:], FG[:], -1.0, 1.0, ALU.mult, ALU.add))
        dve.wait_ge(hg_a, 4)
        dve.wait_ge(hg_ok, 4)
        flat = GC[:].rearrange("p h t -> p (h t)")
        dve.tensor_tensor_scan(flat, CHUNK_ON[:], flat, 0.0, ALU.mult, ALU.add).then_inc(hg_d, 1)
        dve.wait_ge(hg_d, 3)

        def chunks(t):
            return t[:].rearrange("p h (n c) -> p (h n) c", c=HG_CHUNK)

        dve.tensor_tensor(chunks(KEN), chunks(GC)[:, :, HG_CHUNK - 1:].to_broadcast([P, 32, HG_CHUNK]), chunks(GC),
                          ALU.subtract).then_inc(hg_d, 1)
        dve.wait_ge(hg_a, 6)
        dve.scalar_tensor_tensor(QD[:], Q2, P ** -0.5, EG[:], ALU.mult, ALU.mult)
        dve.tensor_tensor(KD[:], KD[:], KH[:], ALU.mult).then_inc(hg_d, 1)
        dve.wait_ge(hg_a, 7)
        dve.tensor_tensor(KEN[:], KEN[:], KH[:], ALU.mult).then_inc(hg_d, 1)
        chain(dve.tensor_tensor(U[:], CG, HC, ALU.mult))
        for ft in range(4):
            w = [COLS[:, CONV_W2 + 3 * ft + j:CONV_W2 + 3 * ft + j + 1] for j in range(3)]
            chain(dve.tensor_scalar(Y[:, ft, :], U[:, ft, :], w[2], None, ALU.mult))
            for back in (1, 2):
                chain(dve.scalar_tensor_tensor(Y[:, ft, back:], U[:, ft, :SEQ - back], w[2 - back], Y[:, ft, back:],
                                               ALU.mult, ALU.add))
        dve.tensor_tensor(Y[:], Y[:], BG, ALU.mult).then_inc(c2_d, 1)
        dve.wait_ge(hg_p, 2)
        for tt in range(TT):
            last = dve.copy_predicated(ABD[:, tt, :, :], IN_CHUNK[:].bitcast(U32).unsqueeze(1).to_broadcast([P, 4, P]),
                                       PS[:, 1024 + tt * 512:1536 + tt * 512].rearrange("p (h n) -> p h n", h=4))
        last.then_inc(hg_d, 1)
        dve.wait_ge(s_ok, 1)
        for n in range(1, 7):
            if n == 4:
                dve.wait_ge(kv_ps, 2)
            if n > 1:
                dve.wait_ge(s_ok, n)
            for h in range(4):
                last = dve.scalar_tensor_tensor(
                    ST2[:, n, h, :], ST2[:, n - 1, h, :], EG[:, h, (n + 1) * HG_CHUNK - 1:(n + 1) * HG_CHUNK],
                    PS[:, 2048 + n % 4 * 512 + h * P:2048 + n % 4 * 512 + (h + 1) * P], ALU.mult, ALU.add)
            last.then_inc(s_ok, 1)
        dve.wait_ge(c2_p, 1)
        chain(dve.tensor_scalar(MS[:].rearrange("p f t -> p (f t)"), PS[:, 1024:2048], EPS, None, ALU.add))
        dve.reciprocal(MS[:], MS[:]).then_inc(c2_d, 1)
        dve.wait_ge(c2_a, 2)
        for ft in range(4):
            last = dve.scalar_tensor_tensor(Y[:, ft, :], Y[:, ft, :], COLS[:, CONV_GAIN2 + ft:CONV_GAIN2 + ft + 1],
                                            MS[:, ft, :], ALU.mult, ALU.mult)
        last.then_inc(c2_d, 1)
        dve.wait_ge(c2_a, 3)
        dve.tensor_tensor(XTL[:, 0:4, :], Y[:], XTH[:, 0:4, :].bitcast(F32), ALU.subtract).then_inc(c2_d, 1)
        dve.wait_ge(hg_a, 9)
        chain(dve.tensor_scalar(STAT[:, 40:48], STAT[:, 32:40], 1.0 / P, EPS, ALU.mult, ALU.add))
        dve.reciprocal(STAT[:, 40:48], STAT[:, 40:48]).then_inc(hg_d, 1)
        dve.wait_ge(hg_a, 10)
        for tt in range(TT):
            o = U[:, 2 * tt:2 * tt + 2, :].rearrange("p a t -> p (a t)").rearrange("p (h n) -> p h n", h=4)
            chain(dve.tensor_tensor(o, PS[:, tt * 512:tt * 512 + 512].rearrange("p (h n) -> p h n", h=4),
                                    STAT[:, 48 + tt * 4:52 + tt * 4].unsqueeze(2).to_broadcast([P, 4, P]), ALU.mult))
            last = dve.tensor_tensor(o, o, G2[:, tt, :].rearrange("p (h n) -> p h n", h=4), ALU.mult)
        last.then_inc(hg_d, 1)
        dve.wait_ge(hg_a, 11)
        dve.scalar_tensor_tensor(XTL[:, 4:8, :], XT_PS[:, 4:8, :], COLS[:, HG_GAIN:HG_GAIN + 1],
                                 XTH[:, 4:8, :].bitcast(F32), ALU.mult, ALU.subtract).then_inc(hg_d, 1)
        split_run(BASE["w_out_2"] + PB, 8)
        dve.wait_ge(w_used, BASE["peer_q"])
        for tt in range(TT):
            dve.tensor_tensor(H[:, tt, :], H[:, tt, :], ACC[:, tt, :], ALU.add).then_inc(h_done, 1)
        prenorm(8, H, "peer")
        plain("peer_q", 4, mixer_dst)

        b = BASE["peer"]
        ticks = [0, 0]

        def tick(long=False):
            ticks[0] += not long
            if (long or ticks[0] % 5 == 0) and ticks[1] < SEARCH:
                split(b + PB + ticks[1], 1)
                ticks[1] += 1

        def best16(values, rows, top, places):
            def each(instruction):
                for r in range(rows):
                    last = instruction(r)
                    if r < rows - 1:
                        tick()
                chain(last)
                tick()

            each(lambda r: dve.max(top[:, r, 0:8], values[:, r, :]))
            each(lambda r: dve.max_index(places[:, r, 0:8], top[:, r, 0:8], values[:, r, :]))
            each(lambda r: dve.match_replace(values[:, r, :], top[:, r, 0:8], values[:, r, :], -3.0e38))
            each(lambda r: dve.max(top[:, r, 8:16], values[:, r, :]))
            each(lambda r: dve.max_index(places[:, r, 8:16], top[:, r, 8:16], values[:, r, :]))

        def keys_of(tt):
            dve.wait_ge(hot_ok, 2 * tt + 2)
            for p in range(2):
                dve.reduce_sum(ROUTE[:, tt, p, :], HOT[:, p, :, :], AX_X).then_inc(hot_used, 1)
                tick(long=True)

        dve.wait_ge(iota_ok, 1)
        for tt in range(TT):
            dve.wait_ge(ks_sb, tt + 1)
            best16(SC[:, tt, :, :], 16, TOP[:, tt, :, :], TOP_AT[:, tt, :, :])
            dve.tensor_copy(TOP_ATF[:, tt, :, :], TOP_AT[:, tt, :, :])
            chain(dve.tensor_tensor(CAND[:, tt, :, :].rearrange("p h (a b) -> p h a b", a=16),
                                    TOP[:, tt, 0:16:2, :].unsqueeze(3).to_broadcast([P, 8, 16, 16]),
                                    TOP[:, tt, 1:16:2, :].unsqueeze(2).to_broadcast([P, 8, 16, 16]), ALU.add))
            tick(long=True)
            if tt:
                keys_of(0)
            best16(CAND[:, tt, :, :], 8, CTOP[:, tt, :, :], CAT[:, tt, :, :])
            at_ = CAT[:, tt, :, :].rearrange("p h k -> p (h k)")
            dve.tensor_scalar(CDIG[:, tt, 0, :], at_, 4, None, ALU.logical_shift_right)
            chain(dve.tensor_scalar(CDIG[:, tt, 1, :], at_, 15, None, ALU.bitwise_and))
            chain(dve.tensor_copy(CDIGF[:, tt, :, :], CDIG[:, tt, :, :]))
            if tt:
                dve.wait_ge(hot_used, 2 * tt)
            for p in range(2):
                dve.tensor_tensor(HOT[:, p, :, :], CDIGF[:, tt, p, :].unsqueeze(2).to_broadcast([P, 128, 16]),
                                  IOTA[:, 0:16].unsqueeze(1).to_broadcast([P, 128, 16]),
                                  ALU.is_equal).then_inc(hot_one, 1)
                tick(long=True)
            chain(dve.tensor_copy(GSUM[:, tt, 8:16].unsqueeze(2), CTOP[:, tt, :, 0:1]))
            dve.tensor_tensor(CTOP[:, tt, :, :], CTOP[:, tt, :, :],
                              GSUM[:, tt, 8:16].unsqueeze(2).to_broadcast([P, 8, 16]), ALU.subtract).then_inc(gd_ok, 1)
        split(b + PB + ticks[1], SEARCH - 2 - ticks[1])
        ticks[1] = SEARCH - 2
        keys_of(1)
        for tt in range(TT):
            dve.wait_ge(gexp_ok, tt + 1)
            chain(dve.reduce_sum(GSUM[:, tt, 0:8], CTOP[:, tt, :, :], AX_X))
            chain(dve.reciprocal(GSUM[:, tt, 0:8], GSUM[:, tt, 0:8]))
            dve.tensor_tensor(ROUTE[:, tt, 2, :].rearrange("p (h k) -> p h k", h=8), CTOP[:, tt, :, :],
                              GSUM[:, tt, 0:8].unsqueeze(2).to_broadcast([P, 8, 16]), ALU.mult).then_inc(route_ok, 1)

        def gate_hot(group, dyn=None, late=True):
            if late:
                dve.wait_ge(g_ps, at(group - 1, dyn))
            t, q = bass.ds(at(4 * group, dyn, 4), 4), 4 * (group % 2)
            for p, hot, done in ((0, OA, key1_ok), (1, OB, key2_ok)):
                dve.tensor_tensor(hot[:, q:q + 4, :], IOTA[:].unsqueeze(1).to_broadcast([P, 4, P]),
                                  ROUTE_T[:, p, t].unsqueeze(2).to_broadcast([P, 4, P]), ALU.is_equal).then_inc(done, 1)

        dve.wait_ge(rt_ok, 2)
        for g in range(GROUPS):
            gate_hot(g, late=g >= 2)
        split(b + SEARCH + 4, 1)
        for n in range(1, EARLY - SEARCH):
            with dve.Fori(0, GROUPS // 2) as i:
                for g in range(2):
                    gate_hot(GROUPS * n + g, i * 2)
            split(b + SEARCH + 4 + n, 1)

        def low(v, dyn=None):
            dve.wait_ge(wt_high, at(v + 1, dyn, 8))
            dve.tensor_tensor(WTL[:, v % 4, :], GE[:, v % 4, :], WTH[:, v % 4, :].bitcast(F32),
                              ALU.subtract).then_inc(wt_low, 1)

        m = b + EARLY
        for k in range(4):
            low(k)
        with dve.Fori(0, TURNS - 1) as i:
            for j in range(TURN):
                if j >= 4:
                    low(j, i)
                split(m + 4 + j, 1, i * TURN)
        m, v = m + (TURNS - 1) * TURN, (TURNS - 1) * 8
        for j in range(8):
            if j >= 4:
                low(v + j)
            split(m + 4 + j, 1)
        dve.wait_ge(psq_done, 10)
        inverse(STAT[:, 16:18], STAT[:, 18:20]).then_inc(pinv_done, 1)
        dve.wait_ge(prs_done, 5)
        dve.wait_ge(row_in, 16 * 5)
        for tt in range(TT):
            dve.scalar_tensor_tensor(TMP[:, tt, :], ACC[:, tt, :], STAT[:, 20 + tt:21 + tt],
                                     ROWG[:], ALU.mult, ALU.mult).then_inc(final_ok, 1)

    @block.tensor
    def _(pe):
        def product(out, high, low, w_hi, w_lo, start, stop):
            pe.matmul(out, high, w_hi, start=start, stop=False, skip_group_check=True)
            pe.matmul(out, low, w_hi, start=False, stop=False, skip_group_check=True)
            return pe.matmul(out, high, w_lo, start=False, stop=stop, skip_group_check=True)

        def transpose_norm(k):
            for tt, ready in enumerate((xn_act, xn_dve)):
                pe.wait_ge(ready, k + 1)
                for kt in range(KT):
                    last = pe.transpose(XT_PS[:, kt, tt * P:(tt + 1) * P], XN[:, tt, kt * P:(kt + 1) * P], IDENT[:])
                    if tt == TT - 1 and kt % 2:
                        last.then_inc(xt_ps, 1)
            pe.wait_ge(xt_low, (k + 1) * KT)

        def panel_tokens(n0, pair, dyn=None, blocks=range(PB)):
            for b in blocks:
                s = (n0 + b) % SLOTS
                pe.wait_ge(w_split, at(n0 + b + 1, dyn))
                for kt in (2 * b, 2 * b + 1):
                    w = slice((kt % 2) * 512, (kt % 2) * 512 + 512)
                    for tt in range(TT):
                        t = slice(tt * P, (tt + 1) * P)
                        last = product(pair[:, tt * 512:(tt + 1) * 512], XTH[:, kt, t], XTL[:, kt, t],
                                       WH[:, s, w], WL[:, s, w], kt == 0, kt == KT - 1)
                last.then_inc(w_used, 1)

        def panel_features(n0, pair, dyn=None, blocks=range(PB)):
            for b in blocks:
                s = (n0 + b) % SLOTS
                pe.wait_ge(w_split, at(n0 + b + 1, dyn))
                for kt in (2 * b, 2 * b + 1):
                    for ft in range(4):
                        w = slice((kt % 2) * 512 + ft * P, (kt % 2) * 512 + (ft + 1) * P)
                        last = product(pair[:, ft * SEQ:(ft + 1) * SEQ], WH[:, s, w], WL[:, s, w],
                                       XTH[:, kt, :], XTL[:, kt, :], kt == 0 and ft % 2 == 0, kt == KT - 1)
                last.then_inc(w_used, 1)

        def plain(stage, kinds):
            for n, kind in enumerate(kinds):
                if n >= 2:
                    pe.wait_ge(evac_a, EVAC[stage] + n - 1)
                    pe.wait_ge(evac_d, EVAC[stage] + n - 1)
                (panel_tokens if kind == "t" else panel_features)(BASE[stage] + PB * n, PAIR[n % 2])

        def ffn_up(stage, f):
            b, e = BASE[stage], f * FFN_PANELS

            def up(p, parity, dyn=None):
                if dyn is not None or e + p >= 2:
                    pe.wait_ge(hidden_done, at(e + p - 1, dyn))
                panel_tokens(b + PB * p, PAIR[parity], None if dyn is None else dyn * PB)

            def turn(p, parity, dyn=None):
                pe.wait_ge(hidden_done, at(e + p + 1, dyn))
                if dyn is not None or e + p >= 2:
                    pe.wait_ge(ht_low, at(e + p - 1, dyn))
                for ft in range(2):
                    for tt in range(TT):
                        o = 512 * parity + ft * SEQ + tt * P
                        last = pe.transpose(ACC[:, 0, o:o + P], HN[:, parity, tt, ft * P:(ft + 1) * P], IDENT[:])
                last.then_inc(ht_ps, 1)

            up(0, 0)
            up(1, 1)
            turn(0, 0)
            with pe.Fori(0, (FFN_PANELS - 3) // 2) as i:
                for p in (2, 3):
                    up(p, p % 2, i * 2)
                    turn(p - 1, (p - 1) % 2, i * 2)
            p = FFN_PANELS - 1
            up(p, p % 2)
            turn(p - 1, (p - 1) % 2)
            turn(p, p % 2)
            pe.wait_ge(ht_low, e + FFN_PANELS)

        def rows_product(stage, kts, high=HTH, low=HTL):
            for kt in range(kts):
                n = BASE[stage] + kt
                pe.wait_ge(w_split, n + 1)
                for tt in range(TT):
                    t = slice(tt * P, (tt + 1) * P)
                    for half in range(2):
                        w = slice(half * 512, half * 512 + 512)
                        last = product(ACC[:, tt, w], high[:, kt, t], low[:, kt, t],
                                       WH[:, n % SLOTS, w], WL[:, n % SLOTS, w], kt == 0, kt == kts - 1)
                last.then_inc(w_used, 1)

        pe.wait_ge(ident_ok, 1)
        transpose_norm(0)
        plain("xa_kv", "fftt")
        pe.wait_ge(evac_a, EVAC["w_in"])
        pe.wait_ge(evac_d, EVAC["w_in"])
        transpose_norm(1)
        ffn_up("ffn1_up", 0)
        rows_product("ffn1_down", FFN_KT)
        transpose_norm(2)
        plain("w_in", "fffftt")
        pe.wait_ge(masks_ok, 5)
        pe.wait_ge(evac_a, EVAC["w_in"] + 4)
        pe.wait_ge(evac_d, EVAC["w_in"] + 4)

        def scores(k):
            if k:
                pe.wait_ge(sc_sb, k)
            for h in range(2):
                d = slice(64 * h, 64 * h + 64)
                pe.matmul(S_PS[:, h, 0:SEQ], KTT[d, k, 0:P], QT[d, k, :], start=True, stop=True)
                last = pe.matmul(S_PS[:, h, SEQ:384], KTT[d, k, P:SEQ], QT[d, k, P:SEQ], start=True, stop=True)
            last.then_inc(sc_ps, 1)

        def suffix_sums(k):
            pe.wait_ge(sp_done, k + 1)
            if k:
                pe.wait_ge(loga_done, k)
            if k >= 2:
                pe.wait_ge(o_done, k - 1)
            for h in range(2):
                pe.matmul(C_PS[:, h, 0:384], FROM[:], by_head(SPL, k)[:, h, :], start=True, stop=False)
                last = pe.matmul(C_PS[:, h, P:SEQ], ONES[:], by_head(SPL, k)[:, h, SEQ:384], start=False, stop=True)
            last.then_inc(sum_ps, 1)

        def weighted_values(k):
            a = by_head(LOGA, k)
            pe.wait_ge(a_done, k + 1)
            if k:
                pe.wait_ge(o_done, k)
            for h in range(2):
                c = 2 * k + h
                o = [C_PS[:, h, 384 + tt * 64:448 + tt * 64] for tt in range(TT)]
                v = [V[:, c // 8, tt, c % 8 * 64:c % 8 * 64 + 64] for tt in range(TT)]
                pe.matmul(o[0], a[:, h, 0:P], v[0], start=True, stop=True)
                pe.matmul(o[1], a[:, h, P:SEQ], v[0], start=True, stop=False)
                last = pe.matmul(o[1], a[:, h, SEQ:384], v[1], start=False, stop=True)
            last.then_inc(o_ps, 1)

        for k in range(10):
            if k == 0:
                pe.wait_ge(evac_a, EVAC["w_in"] + 6)
                pe.wait_ge(evac_d, EVAC["w_in"] + 6)
            if k < 8:
                scores(k)
            if 1 <= k <= 8:
                suffix_sums(k - 1)
            if k >= 2:
                weighted_values(k - 2)
            n = 6 + k // 2
            if k % 2 == 0:
                pe.wait_ge(evac_a, EVAC["w_in"] + n - 1)
                pe.wait_ge(evac_d, EVAC["w_in"] + n - 1)
            (panel_tokens if n >= 9 else panel_features)(BASE["w_in"] + PB * n, PAIR[n % 2], None,
                                                        range(k % 2 * 2, k % 2 * 2 + 2))
        pe.wait_ge(wdt_ok, 1)
        pe.wait_ge(evac_a, EVAC["w_in"] + 10)
        pe.wait_ge(evac_d, EVAC["w_in"] + 10)
        for tt in range(TT):
            for kt in range(KT):
                t, w = slice(tt * P, (tt + 1) * P), slice(kt * 16, kt * 16 + 16)
                last = product(PS[:, 1024 + tt * 16:1040 + tt * 16], XTH[:, kt, t], XTL[:, kt, t],
                               WDTH[:, w], WDTL[:, w], kt == 0, kt == KT - 1)
        last.then_inc(dt_ps, 1)
        pe.wait_ge(dt_d, 3)
        pe.matmul(PS[:, 1088:1120], UPTO[:], SS[:, 12, :], start=True, stop=True)
        pe.matmul(PS[:, 1120:1136], ONES[:], SS[:, 12, 0:16], start=True, stop=True).then_inc(acs_ps, 1)

        def row_sums(tt):
            pe.wait_ge(au_ok, tt + 1)
            if tt:
                pe.wait_ge(lm_ok, tt)
            for q in range(4):
                o = PS[:, 2048 + q * 512:2560 + q * 512]
                pe.matmul(o, ONES[:], AU[:, 4 * q:4 * q + 4, :].rearrange("p h n -> p (h n)"),
                          start=True, stop=False)
                last = pe.matmul(o.rearrange("p (h n) -> p h n", h=4), IDENT[:],
                                 FUTURE[:].unsqueeze(1).to_broadcast([P, 4, P]), start=False, stop=True)
            last.then_inc(row_ps, 1)

        pe.wait_ge(o_done, 8)
        row_sums(0)
        def xs_tokens(tt):
            if tt:
                pe.wait_ge(xs_sb, 2 * tt)
            for ft in range(8):
                last = pe.transpose(PS[:, ft * P:(ft + 1) * P], CV[:, ft, tt * P:(tt + 1) * P], IDENT[:])
            last.then_inc(xs_ps, 1)

        pe.wait_ge(evac_a, EVAC["w_in"] + 11)
        pe.wait_ge(evac_d, EVAC["w_in"] + 11)
        pe.wait_ge(cv_done, 3)
        pe.wait_ge(acs_ok, 1)
        for g in range(2):
            pe.transpose(PS[:, 1152 + g * P:1280 + g * P], CV[:, 8 + g, 0:P], IDENT[:])
        for tt in range(TT):
            for g in range(2):
                o, t = 1536 + (2 * tt + g) * P, slice(tt * P, (tt + 1) * P)
                last = pe.matmul(PS[:, o:o + P], CV[:, 8 + g, t], CV[:, 10 + g, t], start=True, stop=True)
        last.then_inc(cb_ps, 1)
        xs_tokens(0)
        xs_tokens(1)
        pe.wait_ge(xd_ok, 2)
        pe.wait_ge(cb_ok, 2)
        for g in range(2):
            last = pe.matmul(PS[:, 1024 + g * 512:1536 + g * 512], BN[:, g, :], XDD[:, g * 512:(g + 1) * 512],
                             start=True, stop=True)
        last.then_inc(st_ps, 1)
        for tt in range(TT):
            pe.wait_ge(m_ok, tt + 1)
            pe.wait_ge(xd_ok, (1, 3)[tt])
            pe.wait_ge(xs_sb, 4)
            if tt:
                pe.wait_ge(y_done, 1)
            for h in range(16):
                last = pe.matmul(PS[:, h * 64:(h + 1) * 64], LM[:, h, :], XD[:, tt, h * 64:(h + 1) * 64],
                                 start=True, stop=True)
            if tt:
                pe.wait_ge(st_ok, 1)
                for g in range(2):
                    last = pe.matmul(PS[:, 1024 + g * 512:1536 + g * 512], CV[:, 10 + g, P:SEQ],
                                     ST[:, g * 512:(g + 1) * 512], start=True, stop=True)
            else:
                row_sums(1)
            last.then_inc(y_ps, 1)
        pe.wait_ge(y_done, 2)
        transpose_norm(3)
        transpose_norm(4)
        rows_product("w_out", 16)
        transpose_norm(5)
        plain("xa_q", "ff")
        pe.wait_ge(evac_a, EVAC["xa_q"] + 2)
        pe.wait_ge(evac_d, EVAC["xa_q"] + 2)
        for tt in range(TT):
            for h in range(4):
                for ft in (2 * h, 2 * h + 1):
                    last = pe.matmul(ACC[:, tt, h * SEQ:(h + 1) * SEQ], QT[:, ft, tt * P:(tt + 1) * P], XAK[:, ft, :],
                                     start=ft % 2 == 0, stop=ft % 2 == 1)
            last.then_inc(xs_sc, 1)
        for half in range(2):
            for h in (2 * half, 2 * half + 1):
                for tt in range(TT):
                    pe.wait_ge(xs_norm, tt + 1)
                    for mt in range(2):
                        last = pe.transpose(XT_PS[:, 2 * h + mt, tt * P:(tt + 1) * P],
                                            PE_[:, tt, h, mt * P:(mt + 1) * P], IDENT[:])
            last.then_inc(xp_ps, 1)
        pe.wait_ge(xp_sb, 2)
        for ft in range(8):
            for mt in range(2):
                last = pe.matmul(PS[:, 2048 + ft * SEQ:2048 + (ft + 1) * SEQ],
                                 XAV[:, ft // 4, mt, ft % 4 * P:ft % 4 * P + P], PT[:, ft // 2 * 2 + mt, :],
                                 start=mt == 0, stop=mt == 1)
            if ft % 2:
                last.then_inc(xo_ps, 1)
        pe.wait_ge(xo_low, 4)
        rows_product("xa_o", 8)
        transpose_norm(6)
        ffn_up("ffn2_up", 1)
        rows_product("ffn2_down", FFN_KT)
        transpose_norm(7)
        plain("w_in_2", "ffffftt")
        pe.wait_ge(evac_a, EVAC["w_in_2"] + 7)
        pe.wait_ge(evac_d, EVAC["w_in_2"] + 7)
        pe.wait_ge(hg_d, 6)
        for tt in range(TT):
            for h in range(4):
                last = pe.transpose(PS[:, (tt * 4 + h) * P:(tt * 4 + h + 1) * P], KEN[:, h, tt * P:(tt + 1) * P], IDENT[:])
        last.then_inc(hg_p, 1)
        for tt in range(TT):
            for h in range(4):
                o, t = 1024 + (tt * 4 + h) * P, slice(tt * P, (tt + 1) * P)
                last = pe.matmul(PS[:, o:o + P], KD[:, h, t], QD[:, h, t], start=True, stop=True)
        last.then_inc(hg_p, 1)

        def chunk_kv(tt):
            for j in range(4 - tt):
                rows = slice(HG_CHUNK * j, HG_CHUNK * (j + 1))
                for h in range(4):
                    last = pe.matmul(PS[:, 2048 + j * 512 + h * P:2048 + j * 512 + (h + 1) * P], KE[rows, tt, h, :],
                                     V2[rows, tt, h * P:(h + 1) * P], start=True, stop=True,
                                     tile_position=(HG_CHUNK * j, 0))
            last.then_inc(kv_ps, 1)

        pe.wait_ge(hg_a, 8)
        chunk_kv(0)
        pe.wait_ge(s_ok, 4)
        chunk_kv(1)
        pe.wait_ge(c2_a, 1)
        pe.wait_ge(hg_d, 7)
        for half in range(2):
            last = pe.matmul(PS[:, 1024 + half * 512:1536 + half * 512], GROUP64[:],
                             MS[:, 2 * half:2 * half + 2, :].rearrange("p f t -> p (f t)"), start=True, stop=True)
        last.then_inc(c2_p, 1)
        for tt in range(TT):
            for h in range(4):
                o = tt * 512 + h * P
                last = pe.matmul(PS[:, o:o + P], ABD[:, tt, h, :], V2[:, tt, h * P:(h + 1) * P],
                                 start=h == 0, stop=False, skip_group_check=True)
            if tt == 0:
                last.then_inc(hg_p, 1)
            else:
                pe.wait_ge(s_ok, 7)
            for n in range(max(1, 4 * tt), 4 * tt + 4):
                rows = slice(HG_CHUNK * (n % 4), HG_CHUNK * (n % 4 + 1))
                if n > 1:
                    pe.wait_ge(s_ok, n)
                for h in range(4):
                    o = tt * 512 + h * P
                    last = pe.matmul(PS[rows, o:o + P], QD[:, h, n * HG_CHUNK:(n + 1) * HG_CHUNK],
                                     ST2[:, n - 1, h, :], start=False, stop=True, skip_group_check=True)
        last.then_inc(hg_p, 1)
        pe.wait_ge(hg_d, 9)
        for tt in range(TT):
            o = U[:, 2 * tt:2 * tt + 2, :].rearrange("p a t -> p (a t)")
            for h in range(4):
                last = pe.transpose(XT_PS[:, 4 + h, tt * P:(tt + 1) * P], o[:, h * P:(h + 1) * P], IDENT[:])
        last.then_inc(hg_p, 1)
        pe.wait_ge(hg_d, 10)
        pe.wait_ge(c2_d, 4)
        rows_product("w_out_2", 8, XTH, XTL)
        transpose_norm(8)
        plain("peer_q", "ffff")
        pe.wait_ge(keys_in, 16)
        pe.wait_ge(evac_a, EVAC["peer_q"] + 4)
        pe.wait_ge(evac_d, EVAC["peer_q"] + 4)
        b = BASE["peer"]

        def u_block(n, bank, dyn=None):
            s = n % SLOTS
            pe.wait_ge(w_split, at(n + 1, dyn))
            o = PS[:, bank * 512:bank * 512 + SEQ]
            for kt in range(KT):
                w = slice(kt * P, (kt + 1) * P)
                last = product(o, WH[:, s, w], WL[:, s, w], XTH[:, kt, :], XTL[:, kt, :], kt == 0, kt == KT - 1)
            last.then_inc(w_used, 1)

        def early_tile(n, dyn=None, late=True):
            if late:
                pe.wait_ge(gelu_ok, at(n - 1, dyn))
            u_block(b + n, n % 2, dyn)

        for tt in range(TT):
            if tt:
                pe.wait_ge(ks_sb, tt)
            for hp in range(16):
                last = pe.matmul(PS[:, 2048 + hp * P:2048 + (hp + 1) * P], QP[:, hp, tt * P:(tt + 1) * P], KEYS[:, hp, :],
                                 start=True, stop=True)
            last.then_inc(ks_ps, 1)
            early_tile(tt, late=False)
        pe.wait_ge(ks_sb, 2)
        for tt in range(TT):
            for half in range(2):
                w = slice(half * 512, half * 512 + 512)
                last = pe.matmul(ACC[:, tt, w], IDENT[:], H[:, tt, w], start=True, stop=False, skip_group_check=True)
        last.then_inc(injected, 1)
        early_tile(2)
        early_tile(3)
        with pe.Fori(1, SEARCH // 4) as i:
            for n in range(4):
                early_tile(n, i * 4)
        for tt in range(TT):
            pe.wait_ge(route_ok, tt + 1)
            pe.wait_ge(hot_used, 2 * tt + 2)
            if tt:
                pe.wait_ge(rt_ok, tt)
            for a in range(3):
                last = pe.transpose(PS[:, 1024 + a * P:1152 + a * P], ROUTE[:, tt, a, :], IDENT[:])
            last.then_inc(rt_ps, 1)

        def gates(group, dyn=None, late=True):
            pe.wait_ge(hot4_ok, at(group + 1, dyn))
            pe.wait_ge(key2_ok, at(group + 1, dyn))
            if late:
                pe.wait_ge(g_sb, at(group - 1, dyn))
            q = group % 2
            for j in range(4):
                o = 1024 + 512 * q + j * P
                last = pe.matmul(PS[:, o:o + P], OB[:, 4 * q + j, :], OA[:, 4 * q + j, :], start=True, stop=True)
            last.then_inc(g_ps, 1)

        for n in range(EARLY - SEARCH):
            early_tile(SEARCH + n)
            if n == 0:
                pe.wait_ge(rt_ok, 2)
                gates(0, late=False)
                gates(1, late=False)
            first = 1 if n == 0 else 0
            with pe.Fori(first, GROUPS // 2) as i:
                for g in range(2):
                    gates(GROUPS * n + g, i * 2)

        def v_block(n, v, dyn=None):
            s = n % SLOTS
            pe.wait_ge(w_split, at(n + 1, dyn, TURN))
            pe.wait_ge(wt_low, at(v + 1, dyn, 8))
            for tt in range(TT):
                t = slice(tt * P, (tt + 1) * P)
                for half in range(2):
                    w = slice(half * 512, half * 512 + 512)
                    last = product(ACC[:, tt, w], WTH[:, v % 4, t], WTL[:, v % 4, t], WH[:, s, w], WL[:, s, w],
                                   False, dyn is None and v == 2 * EARLY - 1)
            last.then_inc(w_used, 1)

        m = b + EARLY
        pe.wait_ge(g_sb, 64)
        pe.wait_ge(gelu_ok, EARLY)
        with pe.Fori(0, TURNS - 1) as i:
            for k in range(4):
                pe.wait_ge(gelu_ok, i * 4 + (EARLY - 3 + k))
                u_block(m + k, k, i * TURN)
            for j in range(8):
                v_block(m + 4 + j, j, i)
        m, v = m + (TURNS - 1) * TURN, (TURNS - 1) * 8
        for k in range(4):
            pe.wait_ge(gelu_ok, 2 * EARLY - 7 + k)
            u_block(m + k, k)
        for j in range(8):
            v_block(m + 4 + j, v + j)

    ctx.close()


def panels(w):
    n = w.shape[1] // 512
    return w.reshape(PB, 2, P, n, 512).transpose(3, 0, 2, 1, 4).reshape(n * PB, P, BLK)


def row_blocks(w):
    return w.reshape(-1, P, BLK)


def gate_up(w):
    return w.reshape(D, 2, FFN_PANELS, 256).transpose(0, 2, 1, 3).reshape(D, 2 * D_FF)


def col(v):
    return v.reshape(-1, P).T


def kernel(**inputs):
    import concourse.bacc as bacc
    from concourse.bass_utils import run_bass_kernel_spmd

    a = {k: np.ascontiguousarray(v) for k, v in inputs.items()}
    g = {k: (v[0] if v.shape[0] == 1 and k not in ("hg_lb_logits_2", "norm_f_2") else v) for k, v in a.items()}
    u = g["peer_u_2"].reshape(P, P, KT, P).transpose(0, 3, 2, 1).reshape(P, P, BLK)
    v = g["peer_v_2"].reshape(P, P, BLK)
    turns = [part.reshape(TURNS, 4, P, BLK) for part in (u[EARLY:], v[:EARLY], v[EARLY:])]
    parts = [
        panels(g["xa_wkv"]), panels(gate_up(g["ffn1_w_gu"])), row_blocks(g["ffn1_w_down"]),
        panels(np.concatenate([g["w_in"][:, :3072], g["w_in"][:, 4096:5632], g["w_in"][:, 3072:4096]], axis=1)), row_blocks(g["w_out"]), panels(g["xa_wq"]), row_blocks(g["xa_wo"]),
        panels(gate_up(g["ffn2_w_gu"])), row_blocks(g["ffn2_w_down"]), panels(g["w_in_2"]),
        row_blocks(g["w_out_2"]), panels(g["peer_wq_2"]),
        u[:EARLY], np.stack(turns, axis=1).reshape(-1, P, BLK),
    ]
    cols = np.concatenate(
        [col(g[k]) for k in ("mem_g", "ffn1_pre_g", "mix_pre_g", "xa_pre_g", "ffn2_pre_g", "norm_mix_2",
                             "norm_ffn_2", "attn_norm_g", "ssd_norm_g", "conv_gain_2", "hg_gain_2", "conv_b")]
        + [g["conv_w"].reshape(4, 12, P).transpose(2, 1, 0).reshape(P, 48),
           g["conv_w_2"].reshape(3, 4, P).transpose(2, 1, 0).reshape(P, 12),
           g["hg_lb_logits_2"].reshape(2, 4, P).transpose(2, 0, 1).reshape(P, 8)], axis=1)
    arrays = {
        "stream": np.concatenate(parts, axis=0),
        "w_dt": g["w_in"][:, 5632:].reshape(KT, P, 16).transpose(1, 0, 2).reshape(P, KT * 16),
        "cols": cols,
        "small_row": np.concatenate([g["dt_bias"], g["a_log"], g["d_skip"]]).reshape(1, 48),
        "rows": np.stack([g["ffn1_post_g"], g["mix_post_g"], g["xa_post_g"], g["ffn2_post_g"], g["norm_f_2"]]),
        "x": a["x"].reshape(SEQ, D),
        "mem": a["mem"].reshape(SEQ, D),
        "keys": g["peer_keys_2"].reshape(16, P, P).transpose(2, 0, 1),
    }
    nc = bacc.Bacc("TRN2", target_bir_lowering=False, num_devices=1)
    ins = [nc.dram_tensor(f"in_{k}", v.shape, F32, kind="ExternalInput").ap() for k, v in arrays.items()]
    out = nc.dram_tensor("out", (SEQ, D), F32, kind="ExternalOutput").ap()
    early = nc.dram_tensor("early_gelu", (EARLY, P, SEQ), F32, kind="Internal").ap()
    build(nc, *ins, early, out)
    r = run_bass_kernel_spmd(nc, [{f"in_{k}": np.ascontiguousarray(v) for k, v in arrays.items()}], core_ids=[0])
    return r.results[0]["out"].reshape(1, SEQ, D)
```

```python
from contextlib import ExitStack

import numpy as np

import concourse.bass as bass
from concourse import mybir

F32 = mybir.dt.float32
F32R = mybir.dt.float32r
U32 = mybir.dt.uint32
ACT = mybir.ActivationFunctionType
ALU = mybir.AluOpType
AX_X = mybir.AxisListType.X

P = 128
SEQ = 256
TT = SEQ // P
D = 1024
KT = D // P
D_FF = 2816
FFN_PANELS = D_FF // 256
FFN_KT = D_FF // P
EPS = 1e-6
BLK = 1024
SLOTS = 4
PB = 4
KB = 1024

STREAM = [
    ("ffn1_up", 44), ("ffn1_down", 22), ("kv0", 4), ("w_in", 44), ("kv1", 4), ("kv2", 4), ("w_out", 16),
    ("kv3", 4), ("xa_q", 8), ("xa_o", 8), ("ffn2_up", 44), ("ffn2_down", 22), ("w_in_2", 28),
    ("w_out_2", 8), ("peer_q", 16), ("peer", 256),
]
BASE, N_BLOCKS = {}, 0
for _name, _n in STREAM:
    BASE[_name] = N_BLOCKS
    N_BLOCKS += _n

EVAC, N_EVAC = {}, 0
for _name, _n in (("kv0", 1), ("w_in", 11), ("kv1", 1), ("kv2", 1), ("kv3", 1), ("xa_q", 2), ("w_in_2", 7), ("peer_q", 4)):
    EVAC[_name] = N_EVAC
    N_EVAC += _n

POST_AT = [BASE["kv0"], BASE["kv3"], BASE["ffn2_up"], BASE["w_in_2"], N_BLOCKS]

GAIN_COL = {"mem": 0, "ffn1": 8, "mix": 16, "xa": 24, "ffn2": 32, "mix2": 40, "peer": 48,
            "attn": 56, "ssd": 64}
CONV_GAIN2, HG_GAIN, CONV_B, CONV_W, CONV_W2, LB = 72, 76, 77, 89, 137, 149
N_COLS = 157
EARLY = 64
SEARCH = 60
TURN = 12
TURNS = EARLY // 4
EARLY_OUT = [SEARCH // 4 + (EARLY - SEARCH) // 2] * 2 + [SEARCH // 4] * 2
GROUPS = SEQ // 4 // (EARLY - SEARCH)
HG_CHUNK = 32
SQUARES = [0, 2, 4, 6, 8, 12, 14, 16, 18, 20]



class Chain:

    def __init__(self, engine, semaphore):
        self.engine, self.semaphore, self.count = engine, semaphore, 0
        self.dyn, self.scale = None, 1

    def __call__(self, instruction):
        self.count += 1
        instruction.then_inc(self.semaphore, 1)
        self.engine.wait_ge(self.semaphore, at(self.count, self.dyn, self.scale))

    def enter(self, dyn, each):
        self.dyn, self.scale, self.began = dyn, each, self.count

    def leave(self, times):
        assert self.count - self.began == self.scale
        self.count, self.dyn, self.scale = self.began + times * self.scale, None, 1


def at(static, dyn=None, scale=1):
    return static if dyn is None else dyn * scale + static


def build(nc, stream, w_dt, cols, small_row, rows, x, mem, keys, early, out):
    ctx = ExitStack()
    B0 = 16512

    def sb(name, shape, kb, dt=F32):
        return nc.alloc_sbuf_tensor_at(name, shape, dt, offset=B0 + int(kb * KB))

    def sem(name):
        return ctx.enter_context(nc.semaphore(name))

    PS = ctx.enter_context(nc.psum_tensor("ps", [P, 4096], F32))
    PAIR = [PS[:, 0:1024], PS[:, 1024:2048]]
    ACC = PS[:, 2048:4096].rearrange("p (t n) -> p t n", t=TT)
    XT_PS = PS[:, 0:2048].rearrange("p (k t) -> p k t", k=KT)
    RING = sb("ring", [P, SLOTS, BLK], 0)
    WH = sb("w_high", [P, SLOTS, BLK], 16, F32R)
    WL = sb("w_low", [P, SLOTS, BLK], 32, F32R)
    XTH = sb("xT_high", [P, KT, SEQ], 48, F32R)
    XTL = sb("xT_low", [P, KT, SEQ], 56, F32R)
    IDENT = sb("ident", [P, P], 64)
    H = sb("h", [P, TT, D], 65)
    XN = sb("xn", [P, TT, D], 73)
    TMP = sb("tmp", [P, TT, D], 81)
    ROWG = sb("row_gain", [P, D], 89)
    COLS = sb("cols", [P, N_COLS], 93)
    STAT = sb("stat", [P, 64], 93.75)
    XAK = sb("xa_kT", [P, 8, SEQ], 97)
    XAV = sb("xa_v", [P, 2, TT, 512], 105)
    HTH = sb("hT_high", [P, FFN_KT, SEQ], 113, F32R)
    HTL = sb("hT_low", [P, FFN_KT, SEQ], 135, F32R)
    SG = sb("silu_gate", [P, 2, TT, 256], 157)
    HN = sb("hidden", [P, 2, TT, 256], 161)
    MEM = sb("mem_sb", [P, TT, D], 165)
    MTH = sb("memT_high", [P, KT, SEQ], 177, F32R)
    MTL = sb("memT_low", [P, KT, SEQ], 185, F32R)
    UPTO = sb("upto", [P, P], 94)
    FROM = sb("from", [P, P], 94.5)
    ONES = sb("ones", [P, P], 95)
    BEFORE = sb("before", [P, P], 95.5)
    CAP = sb("cap", [P, P], 96)
    SMALL = sb("small_row_sb", [P, 48], 96.5)
    R = sb("projections", [P, 11, 1024], 113)
    QT = R[:, 0:2, :].rearrange("p a (b t) -> p (a b) t", t=SEQ)
    KTT = R[:, 2:4, :].rearrange("p a (b t) -> p (a b) t", t=SEQ)
    V = R[:, 4:6, :].rearrange("p a (t n) -> p a t n", t=TT)
    XBC = R[:, 6:9, :].rearrange("p a (b t) -> p (a b) t", t=SEQ)
    Z = R[:, 9:11, :].rearrange("p a (t n) -> p a t n", t=TT)
    AO = sb("attention_out", [P, TT, D], 81)
    ZS = sb("scores", [P, 2, 768], 157)
    SPL = sb("softplus", [P, 2, 768], 163)
    LOGA = sb("log_attention", [P, 2, 768], 169)
    S_PS = PS[:, 2048:3072].rearrange("p (h n) -> p h n", h=2)
    C_PS = PS[:, 3072:4096].rearrange("p (h n) -> p h n", h=2)
    PE_ = sb("xa_probs", [P, TT, 4, SEQ], 157)
    PT = sb("xa_probsT", [P, 8, SEQ], 165)
    def r2(n):
        return R[:, n, :].rearrange("p (b t) -> p b t", t=SEQ)

    F2, Q2, CG, HC, BG = (r2(n) for n in (0, 1, 4, 5, 6))
    G2, V2 = (R[:, n, :].rearrange("p (t n) -> p t n", t=TT) for n in (2, 3))
    U = sb("conv_u", [P, 4, SEQ], 141)
    Y = sb("conv_y", [P, 4, SEQ], 145)
    MS = sb("conv_ms", [P, 4, SEQ], 149)
    FG = sb("forget", [P, 4, SEQ], 153)
    KH = sb("hg_k", [P, 4, SEQ], 157)
    GC = sb("log_decay", [P, 4, SEQ], 161)
    EG = sb("exp_decay", [P, 4, SEQ], 165)
    KD = sb("k_dec", [P, 4, SEQ], 169)
    QD = sb("q_dec", [P, 4, SEQ], 173)
    KEN = sb("k_end", [P, 4, SEQ], 177)
    KE = sb("k_end_tokens", [P, TT, 4, P], 181)
    ABD = sb("hg_scores", [P, TT, 4, P], 185)
    ST2 = sb("hg_states", [P, 7, 4, P], 189)
    GROUP64 = sb("group64", [P, P], 203)
    IN_CHUNK = sb("in_chunk", [P, P], 203.5)
    CHUNK_ON = sb("chunk_on", [P, 4 * SEQ], 85)
    LBS = sb("lower_bound", [P, 8, 4], 204)
    QP = R[:, 0:4, :].rearrange("p a (b t) -> p (a b) t", t=SEQ)
    SC = sb("key_scores", [P, TT, 16, P], 129)
    KEYS = sb("keys_sb", [P, 16, P], 145)
    TOP = sb("top", [P, TT, 16, 16], 153)
    TOP_AT = sb("top_at", [P, TT, 16, 16], 155, U32)
    TOP_ATF = sb("top_at_f", [P, TT, 16, 16], 157)
    CAND = sb("candidates", [P, TT, 8, 256], 159)
    CTOP = sb("cand_top", [P, TT, 8, 16], 175)
    CAT = sb("cand_at", [P, TT, 8, 16], 176, U32)
    CDIG = sb("cand_digits", [P, TT, 2, 128], 177, U32)
    CDIGF = sb("cand_digits_f", [P, TT, 2, 128], 179)
    HOT = sb("digit_hot", [P, 2, 128, 16], 181)
    ROUTE = sb("route", [P, TT, 3, 128], 197)
    GSUM = sb("gate_sum", [P, TT, 16], 200)
    ROUTE_T = sb("routeT", [P, 3, SEQ], 66.5)
    OA = sb("gate_at_key1", [P, 8, P], 69.5)
    OB = sb("one_at_key2", [P, 8, P], 73.5)
    IOTA = sb("iota", [P, P], 207)
    GE = sb("gelu_out", [P, 4, SEQ], 64.5)
    WTH = sb("expert_w_high", [P, 4, SEQ], 68.5, F32R)
    WTL = sb("expert_w_low", [P, 4, SEQ], 72.5, F32R)
    GATES = sb("gates", [P, P, SEQ], 79)
    WDT = sb("w_dt_sb", [P, KT * 16], 201)
    WDTH = sb("w_dt_high", [P, KT * 16], 201.5, F32R)
    WDTL = sb("w_dt_low", [P, KT * 16], 202, F32R)
    SS = sb("ssd_small", [P, 16, 32], 202.5)
    FUTURE = sb("future", [P, P], 204.5)
    CV = sb("conv_out", [P, 12, SEQ], 157)
    XSN = sb("xs_tokens", [P, TT, D], 169)
    AU = sb("adt_upto", [P, 16, P], 113)
    LM = sb("decay", [P, 16, P], 121)
    XD = sb("xs_dt", [P, TT, D], 193)
    XDD = sb("xs_dt_decay", [P, D], 73)
    ST = sb("state", [P, D], 77)
    YS = sb("ssd_out", [P, TT, D], 157)
    BN = sb("b_tokens", [P, 2, P], 145)
    CBM = sb("cb_masked", [P, TT, 2, P], 146)

    def mixer_dst(n, dyn):
        return R[:, n, :] if dyn is None else R[:, bass.ds(dyn + n, 1), :].rearrange("p a n -> p (a n)")

    def kv_dst(n):
        kv = XAK[:, 4 * n:4 * n + 4, :] if n < 2 else XAV[:, n - 2, :, :]
        return kv.rearrange("p a b -> p (a b)")

    def by_head(t, k):
        return t[:, k % 2, :].rearrange("p (h n) -> p h n", h=2)

    loaded = [sem(f"loaded{i}") for i in range(SLOTS)]
    w_high, w_split, w_used = sem("w_high_done"), sem("w_split_done"), sem("w_used")
    const_in, x_in, mem_in, row_in = sem("const_in"), sem("x_in"), sem("mem_in"), sem("row_in")
    out_done = sem("out_done")
    ident_zero, ident_ok = sem("ident_zero"), sem("ident_ok")
    act_chain, dve_chain = sem("act_chain"), sem("dve_chain")
    sq_done, inv_done, rs_done = sem("square_sum"), sem("inverse_ms"), sem("rms_scale")
    xn_act, xn_dve = sem("xn_tile0"), sem("xn_tile1")
    xt_ps, xt_high, xt_low = sem("xT_psum"), sem("xT_high_done"), sem("xT_low_done")
    evac_a, evac_d = sem("evac_act"), sem("evac_dve")
    silu_done, hidden_done, ht_ps = sem("silu_done"), sem("hidden_done"), sem("hT_psum")
    ht_high, ht_low = sem("hT_high_done"), sem("hT_low_done")
    psq_done, pinv_done, prs_done, acc0_done = (sem("post_square_sum"), sem("post_inverse"), sem("post_scale"),
                                               sem("result_tile0_done"))
    h_done = sem("h_done")
    masks_one, masks_ok, small_in = sem("masks_one"), sem("masks_ok"), sem("small_in")
    sc_ps, sc_sb, abs_done, ln_done, sp_done = (sem("scores_psum"), sem("scores_copied"), sem("abs_done"),
                                                sem("ln_done"), sem("softplus_done"))
    sum_ps, loga_done, a_done, o_ps, o_done = (sem("suffix_psum"), sem("log_a_done"), sem("a_done"),
                                               sem("o_psum"), sem("o_copied"))
    wdt_high, wdt_ok, dt_ps = sem("w_dt_high_done"), sem("w_dt_split"), sem("dt_psum")
    dt_a, dt_d, conv_done, cv_done = sem("dt_act"), sem("dt_dve"), sem("conv_done"), sem("conv_silu")
    xs_ps, xs_sb, cb_ps, cb_ok = sem("xs_psum"), sem("xs_copied"), sem("cb_psum"), sem("cb_masked_done")
    acs_ps, acs_ok, au_ok, row_ps, lm_ok = (sem("a_cumsum_psum"), sem("a_cumsum_ok"), sem("adt_upto_ok"),
                                            sem("a_rows_psum"), sem("decay_exp"))
    m_ok, xd_ok, st_ps, st_ok, y_ps, y_used = (sem("m_ok"), sem("xs_dt_ok"), sem("state_psum"), sem("state_ok"),
                                       sem("y_psum"), sem("y_used"))
    hg_one, hg_ok = sem("hg_masks_one"), sem("hg_masks_ok")
    xs_sc, xs_max, xs_exp, xs_norm = sem("xa_scores"), sem("xa_max"), sem("xa_exp"), sem("xa_norm")
    xp_ps, xp_sb, xo_ps, xo_high, xo_low = (sem("xa_probsT_psum"), sem("xa_probsT_ok"), sem("xa_o_psum"),
                                            sem("xa_o_high"), sem("xa_o_low"))
    c2_d, c2_a, c2_p = sem("conv2_dve"), sem("conv2_act"), sem("conv2_pe")
    hg_d, hg_a, hg_p = sem("hg_dve"), sem("hg_act"), sem("hg_pe")
    kv_ps, s_ok = sem("kv_psum"), sem("states_ok")
    keys_in, iota_ok, injected = sem("keys_in"), sem("iota_ok"), sem("residual_in_psum")
    ks_ps, ks_sb, hot_one, hot_ok, hot_used = (
        sem("key_scores_psum"), sem("key_scores_copied"), sem("hot_one"), sem("hot_ok"), sem("hot_used"))
    gd_ok, gexp_ok, route_ok, rt_ps, rt_ok = (sem("gate_diff"), sem("gate_exp"), sem("route_ok"), sem("routeT_psum"),
                                              sem("routeT_ok"))
    key1_ok, key2_ok, hot4_ok, g_ps, g_sb = sem("ones_at_key1"), sem("ones_at_key2"), sem("gate_at_key1_ok"), sem("gates_psum"), sem("gates_copied")
    gelu_ok, prod_ok, wt_high, wt_low = (sem("gelu_done"), sem("weighted"), sem("weighted_high"),
                                         sem("weighted_low"))
    early_out = [sem(f"early_out{i}") for i in range(4)]
    early_in = [sem(f"early_in{i}") for i in range(4)]
    final_ok = sem("final_ok")
    yz_ok, z_silu, y_done = sem("yz_ok"), sem("z_silu"), sem("y_done")

    block = ctx.enter_context(nc.Block())

    @block.sync
    def _(sp):
        sp.dma_start(H[:], x.rearrange("(t p) d -> p t d", p=P)).then_inc(x_in, 16)
        sp.dma_start(COLS[:], cols).then_inc(const_in, 16)
        sp.dma_start(RING[:, 0, :], stream[0]).then_inc(loaded[0], 16)
        sp.dma_start(MEM[:], mem.rearrange("(t p) d -> p t d", p=P)).then_inc(mem_in, 16)
        for n in range(1, SLOTS):
            sp.dma_start(RING[:, n, :], stream[n]).then_inc(loaded[n], 16)
        sp.dma_start(WDT[:], w_dt).then_inc(small_in, 16)
        sp.dma_start(SMALL[:], small_row[0].partition_broadcast(P)).then_inc(small_in, 16)

        def load(n, dyn=None):
            sp.wait_ge(w_split, at(n - SLOTS + 1, dyn))
            src = stream[n] if dyn is None else stream[bass.ds(dyn + n, 1)].rearrange("a p c -> (a p) c")
            sp.dma_start(RING[:, n % SLOTS, :], src).then_inc(loaded[n % SLOTS], 16)

        b = BASE["peer"]
        with sp.Fori(0, (b + 8) // SLOTS - 1) as i:
            for n in range(SLOTS, 2 * SLOTS):
                load(n, i * SLOTS)
        with sp.Fori(0, SEARCH // SLOTS) as i:
            for n in range(SLOTS):
                load(b + 8 + n, i * SLOTS)
                sp.wait_ge(gelu_ok, i * SLOTS + (n + 1))
                sp.dma_start(early[bass.ds(i * SLOTS + n, 1)].rearrange("a p t -> (a p) t"), GE[:, n, :]
                             ).then_inc(early_out[n], 16)
        for n in range(SEARCH, EARLY):
            load(b + 8 + n)
            sp.wait_ge(gelu_ok, n + 1)
            sp.dma_start(early[n], GE[:, n % 2, :]).then_inc(early_out[n % 2], 16)

        def load_early(turn, k, dyn=None):
            n = 4 * turn + k
            src = early[n] if dyn is None else early[bass.ds(dyn * 4 + n, 1)].rearrange("a p t -> (a p) t")
            sp.dma_start(GE[:, k, :], src).then_inc(early_in[k], 16)

        for n in range(4):
            sp.wait_ge(early_out[n], 16 * EARLY_OUT[n])
        sp.wait_ge(g_sb, 64)
        for k in range(4):
            load_early(0, k)
        with sp.Fori(0, TURNS - 1) as i:
            for j in range(TURN):
                load(b + EARLY + 8 + j, i * TURN)
                if 5 <= j < 9:
                    sp.wait_ge(wt_low, i * 8 + j)
                    load_early(1, j - 5, i)
        for n in range(N_BLOCKS - 4, N_BLOCKS):
            load(n)
        for tt in range(TT):
            sp.wait_ge(final_ok, tt + 1)
            sp.dma_start(out[tt * P:(tt + 1) * P, :], TMP[:, tt, :]).then_inc(out_done, 16)
        sp.wait_ge(out_done, 32)

    @block.gpsimd
    def _(pool):
        pool.memset(IDENT[:], 0.0).then_inc(ident_zero, 1)
        pool.wait_ge(ident_zero, 1)
        pool.affine_select(out=IDENT[:], in_=IDENT[:], compare_op=ALU.not_equal, fill=1.0, base=0,
                           pattern=[[-1, P]], channel_multiplier=1).then_inc(ident_ok, 1)
        pool.dma_start(ROWG[:], rows[0].partition_broadcast(P)).then_inc(row_in, 16)
        for mask in (UPTO, FROM, BEFORE, CAP, ONES):
            pool.memset(mask[:], 1.0).then_inc(masks_one, 1)
        pool.memset(FUTURE[:], 0.0).then_inc(masks_one, 1)
        pool.wait_ge(masks_one, 6)
        for mask, sign, compare, fill in ((UPTO, 1, ALU.is_ge, 0.0), (FROM, -1, ALU.is_ge, 0.0),
                                          (BEFORE, 1, ALU.is_gt, 0.0), (CAP, 1, ALU.is_gt, -1e30),
                                          (FUTURE, 1, ALU.is_ge, -1e30)):
            pool.affine_select(out=mask[:], in_=mask[:], compare_op=compare, fill=fill, base=0,
                               pattern=[[sign, P]], channel_multiplier=-sign).then_inc(masks_ok, 1)

        def row_gain(k):
            pool.wait_ge(h_done, 2 * k)
            pool.dma_start(ROWG[:], rows[k].partition_broadcast(P)).then_inc(row_in, 16)

        def per_head(dst, src, heads):
            return pool.tensor_tensor(dst.rearrange("p (h d) -> p h d", d=64), src.rearrange("p (h d) -> p h d", d=64),
                                      heads.unsqueeze(2).to_broadcast([P, 16, 64]), ALU.mult)

        def ssd():
            pool.wait_ge(dt_d, 3)
            for tt in range(TT):
                if tt:
                    pool.wait_ge(row_ps, 1)
                else:
                    pool.wait_ge(o_done, 8)
                pool.tensor_tensor(AU[:], SS[:, 12, tt * 16:tt * 16 + 16].unsqueeze(2).to_broadcast([P, 16, P]),
                                   UPTO[:].unsqueeze(1).to_broadcast([P, 16, P]), ALU.mult).then_inc(au_ok, 1)
                pool.wait_ge(xs_sb, 2 * (tt + 1))
                per_head(XD[:, tt, :], XSN[:, tt, :], SS[:, 10, tt * 16:tt * 16 + 16]).then_inc(xd_ok, 1)
                if tt == 0:
                    pool.wait_ge(dt_a, 4)
                    pool.wait_ge(xd_ok, 1)
                    per_head(XDD[:], XD[:, 0, :], SS[:, 15, 0:16]).then_inc(xd_ok, 1)
            for tt in range(TT):
                per_head(YS[:, tt, :], XSN[:, tt, :], SMALL[:, 32:48]).then_inc(yz_ok, 1)

        row_gain(1)
        ssd()
        row_gain(2)
        row_gain(3)
        pool.wait_ge(h_done, 8)
        pool.memset(CHUNK_ON[:], 1.0).then_inc(hg_one, 1)
        pool.memset(ABD[:], 0.0).then_inc(hg_one, 1)
        pool.memset(GROUP64[:], 1.0 / 64).then_inc(hg_one, 1)
        pool.tensor_copy(IN_CHUNK[:], UPTO[:]).then_inc(hg_one, 1)
        pool.wait_ge(hg_one, 4)
        pool.memset(CHUNK_ON[:].rearrange("p (n c) -> p n c", c=HG_CHUNK)[:, :, 0:1], 0.0).then_inc(hg_ok, 1)
        pool.affine_select(out=IN_CHUNK[:], in_=IN_CHUNK[:], compare_op=ALU.is_ge, fill=0.0, base=0,
                           pattern=[[-HG_CHUNK, 4], [0, HG_CHUNK]], channel_multiplier=1).then_inc(hg_ok, 1)
        pool.affine_select(out=GROUP64[:], in_=GROUP64[:], compare_op=ALU.is_ge, fill=0.0, base=0,
                           pattern=[[-64, 2], [0, 64]], channel_multiplier=1).then_inc(hg_ok, 1)
        pool.wait_ge(hg_ok, 3)
        pool.affine_select(out=GROUP64[:], in_=GROUP64[:], compare_op=ALU.is_ge, fill=0.0, base=63,
                           pattern=[[64, 2], [0, 64]], channel_multiplier=-1).then_inc(hg_ok, 1)
        pool.wait_ge(h_done, 10)
        pool.dma_start(KEYS[:], keys).then_inc(keys_in, 16)
        pool.iota(IOTA[:], pattern=[[1, P]], base=0, channel_multiplier=0,
                  allow_small_or_imprecise_dtypes=True).then_inc(iota_ok, 1)
        pool.wait_ge(iota_ok, 1)
        for tt in range(TT):
            for p in range(2):
                pool.wait_ge(hot_one, 2 * tt + p + 1)
                hot = HOT[:, p, :, :].rearrange("p (h k) j -> p h k j", h=8)
                pool.tensor_tensor(hot, hot, TOP_ATF[:, tt, p:16:2, :].unsqueeze(2).to_broadcast([P, 8, 16, 16]),
                                   ALU.mult).then_inc(hot_ok, 1)

        with pool.Fori(0, SEQ // 8) as i:
            for q in range(2):
                pool.wait_ge(key1_ok, i * 2 + (q + 1))
                hot = OA[:, 4 * q:4 * q + 4, :]
                gate = ROUTE_T[:, 2, bass.ds(i * 8 + 4 * q, 4)].unsqueeze(2).to_broadcast([P, 4, P])
                pool.tensor_tensor(hot, hot, gate, ALU.mult).then_inc(hot4_ok, 1)

        def product(v, k, tile, dyn=None):
            g = GATES[:, tile, :] if dyn is None else GATES[:, bass.ds(dyn * 4 + tile, 1), :]
            if dyn is not None:
                g = g.rearrange("p a t -> p (a t)")
            pool.tensor_tensor(GE[:, k, :], GE[:, k, :], g, ALU.mult).then_inc(prod_ok, 1)

        pool.wait_ge(g_sb, 64)
        for k in range(4):
            pool.wait_ge(early_in[k], 16)
            product(k, k, k)
        with pool.Fori(0, TURNS - 1) as i:
            for k in range(4):
                pool.wait_ge(gelu_ok, i * 4 + (EARLY + k + 1))
                product(4 + k, k, EARLY + k, i)
            for k in range(4):
                pool.wait_ge(early_in[k], i * 16 + 32)
                product(8 + k, k, 4 + k, i)
        for k in range(4):
            pool.wait_ge(gelu_ok, 2 * EARLY - 4 + k + 1)
            product(2 * EARLY - 4 + k, k, 2 * EARLY - 4 + k)
        pool.wait_ge(prod_ok, 2 * EARLY)
        pool.dma_start(ROWG[:], rows[4].partition_broadcast(P)).then_inc(row_in, 16)

    @block.scalar
    def _(act):
        chain = Chain(act, act_chain)

        def split(n0, count, dyn=None):
            for n in range(n0, n0 + count):
                act.wait_ge(loaded[n % SLOTS], at(16 * (n // SLOTS + 1), dyn, 16 // SLOTS))
                if dyn is not None or n >= SLOTS:
                    act.wait_ge(w_used, at(n - SLOTS + 1, dyn))
                act.activation(WH[:, n % SLOTS, :], RING[:, n % SLOTS, :], ACT.Copy).then_inc(w_high, 1)

        def split_run(n0, count):
            groups = count // SLOTS
            if groups > 1:
                with act.Fori(0, groups) as i:
                    split(n0, SLOTS, i * SLOTS)
            else:
                groups = 0
            split(n0 + groups * SLOTS, count - groups * SLOTS)

        def prenorm(k, src, gain, high=XTH, k0=0, groups=1, updates=None, between=None):
            w = D // groups

            def squares(tt):
                if updates is not None:
                    act.wait_ge(h_done, updates + tt + 1)
                for g in range(groups):
                    n = tt * groups + g
                    act.activation(XN[:, tt, g * w:g * w + w], src[:, tt, g * w:g * w + w], ACT.Square,
                                   accum_out=STAT[:, n:n + 1]).then_inc(sq_done, 1)

            squares(0)
            act.wait_ge(inv_done, 2 * k + 1)
            chain(act.activation(STAT[:, 8:8 + groups], STAT[:, 4:4 + groups], ACT.Sqrt))
            for g in range(groups):
                last = act.activation(XN[:, 0, g * w:g * w + w], src[:, 0, g * w:g * w + w], ACT.Copy,
                                      scale=STAT[:, 8 + g:9 + g])
            last.then_inc(xn_act, 1)
            squares(1)
            act.wait_ge(inv_done, 2 * k + 2)
            act.activation(STAT[:, 12 + groups:12 + 2 * groups], STAT[:, 4 + groups:4 + 2 * groups],
                           ACT.Sqrt).then_inc(rs_done, 1)
            if between:
                between()
            for kt in range(KT):
                act.wait_ge(xt_ps, k * KT // 2 + kt // 2 + 1)
                act.activation(high[:, k0 + kt, :], XT_PS[:, kt, :], ACT.Copy,
                               scale=COLS[:, GAIN_COL[gain] + kt:GAIN_COL[gain] + kt + 1]).then_inc(xt_high, 1)

        def evac(stage, dst, n, parity, dyn=None):
            act.wait_ge(w_used, at(BASE[stage] + PB * (n + 1), dyn, PB))
            act.activation(dst(n, dyn)[:, 0:512], PAIR[parity][:, 0:512], ACT.Copy).then_inc(evac_a, 1)

        def ffn_up(stage, f):
            b, e = BASE[stage], f * FFN_PANELS

            def silu(p, parity, dyn=None):
                act.wait_ge(w_used, at(b + PB * (p + 1), dyn, PB))
                if dyn is not None or e + p >= 2:
                    act.wait_ge(hidden_done, at(e + p - 1, dyn))
                act.activation(SG[:, parity, :, :],
                               PAIR[parity].rearrange("p (t n) -> p t n", t=TT)[:, :, 0:256],
                               ACT.Silu).then_inc(silu_done, 1)

            def high(p, parity, dyn=None):
                act.wait_ge(ht_ps, at(e + p + 1, dyn))
                act.activation(HTH[:, bass.ds(at(2 * p, dyn, 2), 2), :] if dyn is not None
                               else HTH[:, 2 * p:2 * p + 2, :],
                               ACC[:, 0, 512 * parity:512 * parity + 512].rearrange("p (k t) -> p k t", k=2),
                               ACT.Copy).then_inc(ht_high, 1)

            split(b + PB, PB)
            silu(0, 0)
            with act.Fori(0, (FFN_PANELS - 3) // 2) as i:
                for p in (2, 3):
                    split(b + PB * p, PB, i * (2 * PB))
                    silu(p - 1, (p - 1) % 2, i * 2)
                    high(p - 2, p % 2, i * 2)
            p = FFN_PANELS - 1
            split(b + PB * p, PB)
            silu(p - 1, (p - 1) % 2)
            high(p - 2, p % 2)
            split(b + PB * FFN_PANELS, PB)
            silu(p, p % 2)
            high(p - 1, (p - 1) % 2)
            high(p, p % 2)

        def post_square(k, scratch=XN):
            for tt in range(TT):
                if tt:
                    act.wait_ge(w_used, POST_AT[k])
                else:
                    act.wait_ge(acc0_done, k + 1 + (k > 3))
                act.activation(scratch[:, tt, :], ACC[:, tt, :], ACT.Square,
                               accum_out=STAT[:, 16 + tt:17 + tt]).then_inc(psq_done, 1)
                act.wait_ge(pinv_done, 2 * k + tt + 1)
                act.activation(STAT[:, 20 + tt:21 + tt], STAT[:, 18 + tt:19 + tt], ACT.Sqrt).then_inc(prs_done, 1)

        def plain(stage, panels, dst, after=()):
            b = BASE[stage]
            for n in range(panels):
                split(b + PB * (n + 1), PB)
                evac(stage, dst, n, n % 2)
                if n < len(after):
                    after[n]()

        def kv_evac(n):
            evac(f"kv{n}", lambda *_: kv_dst(n), 0, 0)

        def junction(k, gain, kv, updates):
            b = BASE[f"kv{kv}"] + PB
            split(b, 1)

            def between():
                kv_evac(kv)
                split(b + 1, 2)

            prenorm(k, H, gain, updates=updates, between=between)
            split(b + 3, 1)

        act.preload_act_table_set("sqrt_and_others")
        act.wait_ge(const_in, 16)
        act.wait_ge(x_in, 16)
        prenorm(0, H, "ffn1")
        split(0, 1)
        act.wait_ge(mem_in, 16)
        prenorm(1, MEM, "mem", MTH, between=lambda: split(1, 3))
        act.wait_ge(small_in, 32)
        act.activation(WDTH[:], WDT[:], ACT.Copy).then_inc(wdt_high, 1)
        ffn_up("ffn1_up", 0)
        act.preload_act_table_set("sqrt_and_others")
        split_run(BASE["ffn1_down"] + PB, FFN_KT - 1)
        post_square(0)
        split(BASE["ffn1_down"] + PB + FFN_KT - 1, 1)

        def attention_half(k):
            if k < 8:
                act.wait_ge(sc_ps, k + 1)
                if k >= 2:
                    act.wait_ge(sp_done, k - 1)
                    act.wait_ge(loga_done, k - 1)
                act.activation(by_head(ZS, k), S_PS[:, :, 0:384], ACT.Copy, scale=0.125).then_inc(sc_sb, 1)
                act.wait_ge(abs_done, k + 1)
                if k >= 2:
                    act.wait_ge(sum_ps, k - 1)
                chain(act.activation(SPL[:, k % 2, :], SPL[:, k % 2, :], ACT.Exp))
                act.activation(SPL[:, k % 2, :], SPL[:, k % 2, :], ACT.Ln, bias=1.0).then_inc(ln_done, 1)
            if 1 <= k <= 8:
                act.wait_ge(loga_done, k)
                act.activation(LOGA[:, (k - 1) % 2, :], LOGA[:, (k - 1) % 2, :], ACT.Exp).then_inc(a_done, 1)
            if k >= 2:
                act.wait_ge(o_ps, k - 1)
                act.activation(AO[:, :, (k - 2) * P:(k - 1) * P].rearrange("p t (h n) -> p h t n", h=2),
                               C_PS[:, :, 384:512].rearrange("p h (t n) -> p h t n", t=TT), ACT.Copy).then_inc(o_done, 1)

        junction(2, "mix", 0, 0)
        b = BASE["w_in"]
        with act.Fori(0, 3) as i:
            for p in (0, 1):
                split(b + PB * (p + 1), PB, i * (2 * PB))
                evac("w_in", mixer_dst, p, p, i * 2)
        act.preload_act_table_set("natural_log_exp_and_others")
        for k in range(10):
            attention_half(k)
            split(b + PB * 7 + 2 * k, 2)
            if k % 2:
                evac("w_in", mixer_dst, 6 + k // 2, (k // 2) % 2)
        act.activation(SS[:, 11, 0:16], SMALL[:, 16:32], ACT.Exp).then_inc(dt_a, 1)
        act.wait_ge(dt_d, 1)
        act.activation(SS[:, 2, :], SS[:, 1, :], ACT.Exp).then_inc(dt_a, 1)
        act.wait_ge(dt_d, 2)
        act.activation(SS[:, 4, :], SS[:, 3, :], ACT.Ln).then_inc(dt_a, 1)
        act.wait_ge(acs_ok, 1)
        act.activation(SS[:, 15, 0:16], SS[:, 14, 0:16], ACT.Exp)
        act.activation(SS[:, 15, 16:32], SS[:, 13, 16:32], ACT.Exp, scale=-1.0).then_inc(dt_a, 1)
        split(BASE["kv1"] + PB, PB)
        kv_evac(1)
        for b3 in range(3):
            if b3 == 2:
                split(BASE["kv2"] + PB, PB)
                kv_evac(2)
            act.wait_ge(conv_done, 4 * (b3 + 1))
            act.activation(CV[:, 4 * b3:4 * b3 + 4, :], CV[:, 4 * b3:4 * b3 + 4, :], ACT.Silu).then_inc(cv_done, 1)
        act.wait_ge(evac_d, EVAC["w_in"] + 11)
        act.wait_ge(evac_a, EVAC["w_in"] + 11)
        act.activation(Z, Z, ACT.Silu).then_inc(z_silu, 1)
        for tt in range(TT):
            act.wait_ge(xs_ps, tt + 1)
            act.activation(XSN[:, tt, 0:512], PS[:, 0:512], ACT.Copy).then_inc(xs_sb, 1)
            act.wait_ge(row_ps, tt + 1)
            if tt:
                act.wait_ge(y_ps, 1)
            for h in range(16):
                last = act.activation(LM[:, h, :], PS[:, 2048 + h * P:2048 + (h + 1) * P], ACT.Exp,
                                      bias=SS[:, 13, tt * 16 + h:tt * 16 + h + 1])
            last.then_inc(lm_ok, 1)
            if tt == 0:
                act.wait_ge(st_ps, 1)
                act.activation(ST[:], PS[:, 1024:2048], ACT.Copy).then_inc(st_ok, 1)
        act.wait_ge(y_done, 2)
        prenorm(3, AO, "attn", HTH)
        prenorm(4, YS, "ssd", HTH, 8, groups=2)
        act.preload_act_table_set("sqrt_and_others")
        split_run(BASE["w_out"] + PB, 16 - 1)
        post_square(1)
        split(BASE["w_out"] + PB + 16 - 1, 1)
        junction(5, "xa", 3, 2)
        plain("xa_q", 2, mixer_dst)
        for tt in range(TT):
            act.wait_ge(xs_max, tt + 1)
            for h in range(4):
                n = tt * 4 + h
                last = act.activation(PE_[:, tt, h, :], ACC[:, tt, h * SEQ:(h + 1) * SEQ], ACT.Exp, scale=1.0 / 16,
                                      bias=STAT[:, 32 + n:33 + n], accum_out=STAT[:, 40 + n:41 + n])
            last.then_inc(xs_exp, 1)
        act.wait_ge(xp_ps, 1)
        act.activation(PT[:, 0:4, :], XT_PS[:, 0:4, :], ACT.Copy).then_inc(xp_sb, 1)
        for bank in range(4):
            act.wait_ge(xo_ps, bank + 1)
            act.activation(HTH[:, 2 * bank:2 * bank + 2, :],
                           PS[:, 2048 + bank * 512:2560 + bank * 512].rearrange("p (k t) -> p k t", k=2),
                           ACT.Copy).then_inc(xo_high, 1)
        act.preload_act_table_set("sqrt_and_others")
        split_run(BASE["xa_o"] + PB, 8 - 1)
        post_square(2)
        split(BASE["xa_o"] + PB + 8 - 1, 1)
        prenorm(6, H, "ffn2", updates=4)
        ffn_up("ffn2_up", 1)
        act.preload_act_table_set("sqrt_and_others")
        split_run(BASE["ffn2_down"] + PB, FFN_KT - 1)
        post_square(3)
        split(BASE["ffn2_down"] + PB + FFN_KT - 1, 1)
        prenorm(7, H, "mix2", updates=6)

        e = EVAC["w_in_2"]

        def after_f():
            act.wait_ge(hg_d, 1)
            act.activation(LBS[:, 2:4, :], LBS[:, 0:2, :], ACT.Exp).then_inc(hg_a, 1)
            act.wait_ge(evac_a, e + 1)
            act.wait_ge(evac_d, e + 1)
            act.activation(FG[:], F2, ACT.Sigmoid).then_inc(hg_a, 1)

        def after_q():
            act.wait_ge(evac_a, e + 2)
            act.wait_ge(evac_d, e + 2)
            act.activation(Q2, Q2, ACT.Silu)

        def after_g():
            act.wait_ge(evac_a, e + 3)
            act.wait_ge(evac_d, e + 3)
            act.activation(G2, G2, ACT.Silu).then_inc(hg_a, 1)
            act.preload_act_table_set("natural_log_exp_and_others")
            act.wait_ge(hg_d, 2)
            act.activation(GC[:], FG[:], ACT.Ln).then_inc(hg_a, 1)

        def after_v():
            act.wait_ge(hg_d, 3)
            act.activation(EG[:], GC[:], ACT.Exp).then_inc(hg_a, 1)
            act.activation(KD[:], GC[:], ACT.Exp, scale=-1.0).then_inc(hg_a, 1)

        def after_c():
            act.wait_ge(hg_d, 4)
            act.activation(KEN[:], KEN[:], ACT.Exp).then_inc(hg_a, 1)

        plain("w_in_2", 7, mixer_dst, (after_f, after_q, after_g, after_v, after_c))
        act.wait_ge(hg_p, 1)
        act.activation(KE[:].rearrange("p t h n -> p (t h n)"), PS[:, 0:1024], ACT.Copy).then_inc(hg_a, 1)
        act.wait_ge(c2_d, 1)
        act.activation(MS[:], Y[:], ACT.Square).then_inc(c2_a, 1)
        act.wait_ge(kv_ps, 1)
        act.activation(ST2[:, 0, :, :].rearrange("p h n -> p (h n)"), PS[:, 2048:2560], ACT.Copy).then_inc(s_ok, 1)
        act.wait_ge(c2_d, 2)
        act.activation(MS[:], MS[:], ACT.Sqrt).then_inc(c2_a, 1)
        act.wait_ge(c2_d, 3)
        act.activation(XTH[:, 0:4, :], Y[:], ACT.Copy).then_inc(c2_a, 1)
        act.wait_ge(hg_p, 4)
        for n in range(8):
            last = act.activation(U[:, n // 2, n % 2 * P:n % 2 * P + P], PS[:, n * P:(n + 1) * P], ACT.Square, accum_out=STAT[:, 32 + n:33 + n])
        last.then_inc(hg_a, 1)
        act.wait_ge(hg_d, 8)
        act.activation(STAT[:, 48:56], STAT[:, 40:48], ACT.Sqrt).then_inc(hg_a, 1)
        act.wait_ge(hg_p, 5)
        act.activation(XTH[:, 4:8, :], XT_PS[:, 4:8, :], ACT.Copy, scale=COLS[:, HG_GAIN:HG_GAIN + 1]).then_inc(hg_a, 1)
        act.preload_act_table_set("sqrt_and_others")
        split_run(BASE["w_out_2"] + PB, 8)

        prenorm(8, H, "peer", updates=8)
        plain("peer_q", 4, mixer_dst)
        for tt in range(TT):
            act.wait_ge(ks_ps, tt + 1)
            act.activation(SC[:, tt, :, :].rearrange("p a n -> p (a n)"), PS[:, 2048:4096], ACT.Copy).then_inc(ks_sb, 1)
        act.wait_ge(injected, 1)
        b = BASE["peer"]

        def early_tile(n, buf, written, dyn=None):
            act.wait_ge(w_used, at(b + n + 1, dyn, 4))
            if dyn is not None or written:
                act.wait_ge(early_out[buf], at(16 * written, dyn, 16))
            act.activation(GE[:, buf, :], PS[:, n % 2 * 512:n % 2 * 512 + SEQ], ACT.Gelu).then_inc(gelu_ok, 1)
            split(b + n + 4, 1, None if dyn is None else dyn * 4)

        for n in range(4):
            early_tile(n, n, 0)
        with act.Fori(1, SEARCH // 4) as i:
            for n in range(4):
                early_tile(n, n, 0, i)
        for tt in range(TT):
            act.wait_ge(gd_ok, tt + 1)
            act.activation(CTOP[:, tt, :, :], CTOP[:, tt, :, :], ACT.Exp).then_inc(gexp_ok, 1)

        def route_copy(tt):
            act.wait_ge(rt_ps, tt + 1)
            act.activation(ROUTE_T[:, :, tt * P:(tt + 1) * P], PS[:, 1024:1408].rearrange("p (a n) -> p a n", a=3),
                           ACT.Copy).then_inc(rt_ok, 1)

        def gates_copy(group, dyn=None):
            act.wait_ge(g_ps, at(group + 1, dyn))
            t = bass.ds(at(4 * group, dyn, 4), 4)
            o = 1024 + 512 * (group % 2)
            act.activation(GATES[:, :, t], PS[:, o:o + 512].rearrange("p (t n) -> p n t", t=4),
                           ACT.Copy).then_inc(g_sb, 1)

        act.wait_ge(early_out[2], 16 * EARLY_OUT[2])
        act.wait_ge(early_out[3], 16 * EARLY_OUT[3])
        route_copy(0)
        route_copy(1)
        for n in range(EARLY - SEARCH):
            early_tile(SEARCH + n, n % 2, SEARCH // 4 + n // 2)
            with act.Fori(0, GROUPS // 2) as i:
                for g in range(2):
                    gates_copy(GROUPS * n + g, i * 2)

        def high(v, dyn=None, last_use=None):
            act.wait_ge(prod_ok, at(v + 1, dyn, 8))
            if last_use is not None:
                act.wait_ge(w_used, at(last_use + 1, dyn, TURN))
            act.activation(WTH[:, v % 4, :], GE[:, v % 4, :], ACT.Copy).then_inc(wt_high, 1)

        def u_tile(k, dyn=None):
            act.wait_ge(w_used, at(b + EARLY + k + 1, dyn, TURN))
            act.wait_ge(wt_low, at(k + 1, dyn, 8))
            act.activation(GE[:, k, :], PS[:, k * 512:k * 512 + SEQ], ACT.Gelu).then_inc(gelu_ok, 1)

        m = b + EARLY
        for k in range(4):
            high(k)
        with act.Fori(0, TURNS - 1) as i:
            for k in range(4):
                u_tile(k, i)
                split(m + k + 4, 1, i * TURN)
            for k in range(4):
                high(4 + k, i, m + 4 + k)
                split(m + k + 8, 1, i * TURN)
            for k in range(4):
                high(8 + k, i, m + 8 + k)
                split(m + k + 12, 1, i * TURN)
        m, v = m + (TURNS - 1) * TURN, (TURNS - 1) * 8
        for k in range(4):
            act.wait_ge(w_used, m + k + 1)
            act.wait_ge(wt_low, v + k + 1)
            act.activation(GE[:, k, :], PS[:, k * 512:k * 512 + SEQ], ACT.Gelu).then_inc(gelu_ok, 1)
            split(m + k + 4, 1)
        act.preload_act_table_set("sqrt_and_others")
        for k in range(4):
            high(v + 4 + k, None, m + 4 + k)
            split(m + k + 8, 1)
        post_square(4, MEM)

    @block.vector
    def _(dve):
        chain = Chain(dve, dve_chain)

        def split(n0, count, dyn=None):
            for n in range(n0, n0 + count):
                dve.wait_ge(w_high, at(n + 1, dyn))
                dve.tensor_tensor(WL[:, n % SLOTS, :], RING[:, n % SLOTS, :],
                                  WH[:, n % SLOTS, :].bitcast(F32), ALU.subtract).then_inc(w_split, 1)

        def split_run(n0, count):
            groups = count // SLOTS
            if groups > 1:
                with dve.Fori(0, groups) as i:
                    split(n0, SLOTS, i * SLOTS)
            else:
                groups = 0
            split(n0 + groups * SLOTS, count - groups * SLOTS)

        def inverse(src, dst, width=D):
            chain(dve.tensor_scalar(dst, src, 1.0 / width, EPS, ALU.mult, ALU.add))
            return dve.reciprocal(dst, dst)

        def first_inverse(k, groups=1):
            dve.wait_ge(sq_done, SQUARES[k] + groups)
            inverse(STAT[:, 0:groups], STAT[:, 4:4 + groups], D // groups).then_inc(inv_done, 1)

        def prenorm(k, src, gain, high=XTH, low=XTL, k0=0, groups=1, between=None, begun=False):
            n, w = TT * groups, D // groups
            if not begun:
                first_inverse(k, groups)
            dve.wait_ge(sq_done, SQUARES[k + 1])
            inverse(STAT[:, groups:n], STAT[:, 4 + groups:4 + n], w).then_inc(inv_done, 1)
            dve.wait_ge(rs_done, k + 1)
            for g in range(groups):
                last = dve.tensor_scalar(XN[:, 1, g * w:g * w + w], src[:, 1, g * w:g * w + w],
                                         STAT[:, 12 + groups + g:13 + groups + g], None, ALU.mult)
            last.then_inc(xn_dve, 1)
            if between:
                between()
            for kt in range(KT):
                dve.wait_ge(xt_high, k * KT + (kt | 1) + 1)
                dve.scalar_tensor_tensor(low[:, k0 + kt, :], XT_PS[:, kt, :],
                                         COLS[:, GAIN_COL[gain] + kt:GAIN_COL[gain] + kt + 1],
                                         high[:, k0 + kt, :].bitcast(F32), ALU.mult, ALU.subtract).then_inc(xt_low, 1)

        def evac(stage, dst, n, parity, dyn=None):
            dve.wait_ge(w_used, at(BASE[stage] + PB * (n + 1), dyn, PB))
            dve.tensor_copy(dst(n, dyn)[:, 512:1024], PAIR[parity][:, 512:1024]).then_inc(evac_d, 1)

        def ffn_up(stage, f):
            b, e = BASE[stage], f * FFN_PANELS

            def hidden(p, parity, dyn=None):
                dve.wait_ge(silu_done, at(e + p + 1, dyn))
                if dyn is not None or e + p >= 2:
                    dve.wait_ge(ht_ps, at(e + p - 1, dyn))
                dve.tensor_tensor(HN[:, parity, :, :], SG[:, parity, :, :],
                                  PAIR[parity].rearrange("p (t n) -> p t n", t=TT)[:, :, 256:512],
                                  ALU.mult).then_inc(hidden_done, 1)

            def low(p, parity, dyn=None):
                dve.wait_ge(ht_high, at(e + p + 1, dyn))
                w = bass.ds(at(2 * p, dyn, 2), 2) if dyn is not None else slice(2 * p, 2 * p + 2)
                dve.tensor_tensor(HTL[:, w, :],
                                  ACC[:, 0, 512 * parity:512 * parity + 512].rearrange("p (k t) -> p k t", k=2),
                                  HTH[:, w, :].bitcast(F32), ALU.subtract).then_inc(ht_low, 1)

            split(b + PB, PB)
            hidden(0, 0)
            with dve.Fori(0, (FFN_PANELS - 3) // 2) as i:
                for p in (2, 3):
                    split(b + PB * p, PB, i * (2 * PB))
                    hidden(p - 1, (p - 1) % 2, i * 2)
                    low(p - 2, p % 2, i * 2)
            p = FFN_PANELS - 1
            split(b + PB * p, PB)
            hidden(p - 1, (p - 1) % 2)
            low(p - 2, p % 2)
            split(b + PB * FFN_PANELS, PB)
            hidden(p, p % 2)
            low(p - 1, (p - 1) % 2)
            low(p, p % 2)

        def post_add(k, factor, norm, block):
            dve.wait_ge(row_in, 16 * (k + 1))
            for tt in range(TT):
                dve.wait_ge(psq_done, 2 * k + tt + 1)
                inverse(STAT[:, 16 + tt:17 + tt], STAT[:, 18 + tt:19 + tt]).then_inc(pinv_done, 1)
                dve.wait_ge(prs_done, 2 * k + tt + 1)
                dve.scalar_tensor_tensor(TMP[:, tt, :], ACC[:, tt, :], STAT[:, 20 + tt:21 + tt],
                                         ROWG[:], ALU.mult, ALU.mult).then_inc(dve_chain, 1)
                chain.count += 1
                product_at = chain.count
                if tt:
                    split(block, 1)
                    first_inverse(norm)
                dve.wait_ge(dve_chain, product_at)
                dve.scalar_tensor_tensor(H[:, tt, :], TMP[:, tt, :], factor, H[:, tt, :],
                                         ALU.mult, ALU.add).then_inc(h_done, 1)

        def plain(stage, panels, dst, after=()):
            b = BASE[stage]
            for n in range(panels):
                split(b + PB * (n + 1), PB)
                evac(stage, dst, n, n % 2)
                if n < len(after):
                    after[n]()

        def kv_evac(n):
            evac(f"kv{n}", lambda *_: kv_dst(n), 0, 0)

        def junction(k, gain, kv):
            b = BASE[f"kv{kv}"] + PB

            def between():
                kv_evac(kv)
                split(b, 3)

            prenorm(k, H, gain, between=between, begun=True)
            split(b + 3, 1)

        dve.wait_ge(const_in, 16)
        dve.wait_ge(x_in, 16)
        prenorm(0, H, "ffn1")
        split(0, 1)
        dve.wait_ge(mem_in, 16)
        prenorm(1, MEM, "mem", MTH, MTL, between=lambda: split(1, 3))
        dve.wait_ge(small_in, 32)
        dve.wait_ge(wdt_high, 1)
        dve.tensor_tensor(WDTL[:], WDT[:], WDTH[:].bitcast(F32), ALU.subtract).then_inc(wdt_ok, 1)
        ffn_up("ffn1_up", 0)
        split_run(BASE["ffn1_down"] + PB, FFN_KT - 1)
        post_add(0, 0.5, 2, BASE["ffn1_down"] + PB + FFN_KT - 1)

        def diagonals(t, k):
            return t[:, k % 2, :].rearrange("p (h x n) -> p h x n", h=2, x=3)[:, :, 0:3:2, :]

        def over_diagonals(mask):
            return mask[:].unsqueeze(1).unsqueeze(1).to_broadcast([P, 2, 2, P])

        def attention_half(k):
            if k < 8:
                dve.wait_ge(sc_sb, k + 1)
                if k >= 2:
                    dve.wait_ge(sum_ps, k - 1)
                dve.scalar_tensor_tensor(SPL[:, k % 2, :], ZS[:, k % 2, :], -1.0, ZS[:, k % 2, :],
                                         ALU.mult, ALU.min).then_inc(abs_done, 1)
                dve.wait_ge(ln_done, k + 1)
                chain(dve.scalar_tensor_tensor(SPL[:, k % 2, :], ZS[:, k % 2, :], 0.0, SPL[:, k % 2, :],
                                               ALU.max, ALU.add))
                dve.tensor_tensor(diagonals(SPL, k), diagonals(SPL, k), over_diagonals(BEFORE),
                                  ALU.mult).then_inc(sp_done, 1)
            if 1 <= k <= 8:
                j = k - 1
                dve.wait_ge(sum_ps, k)
                if j >= 1:
                    dve.wait_ge(o_ps, j)
                if j >= 2:
                    dve.wait_ge(o_ps, j - 1)
                chain(dve.tensor_tensor(by_head(LOGA, j), by_head(ZS, j), C_PS[:, :, 0:384], ALU.subtract))
                dve.tensor_tensor(diagonals(LOGA, j), diagonals(LOGA, j), over_diagonals(CAP),
                                  ALU.min).then_inc(loga_done, 1)

        dve.wait_ge(h_done, 2)
        junction(2, "mix", 0)
        b = BASE["w_in"]
        with dve.Fori(0, 3) as i:
            for p in (0, 1):
                split(b + PB * (p + 1), PB, i * (2 * PB))
                evac("w_in", mixer_dst, p, p, i * 2)
        dve.wait_ge(masks_ok, 5)
        for k in range(10):
            attention_half(k)
            split(b + PB * 7 + 2 * k, 2)
            if k % 2:
                evac("w_in", mixer_dst, 6 + k // 2, (k // 2) % 2)

        def both(heads):
            return heads.unsqueeze(1).to_broadcast([P, TT, 16])

        def two(row):
            return SS[:, row, :].rearrange("p (t h) -> p t h", t=TT)

        dve.wait_ge(dt_ps, 1)
        chain(dve.tensor_tensor(two(0), PS[:, 1024:1056].rearrange("p (t h) -> p t h", t=TT),
                                both(SMALL[:, 0:16]), ALU.add))
        dve.scalar_tensor_tensor(SS[:, 1, :], SS[:, 0, :], -1.0, SS[:, 0, :], ALU.mult, ALU.min).then_inc(dt_d, 1)
        dve.wait_ge(dt_a, 2)
        chain(dve.tensor_scalar(SS[:, 3, :], SS[:, 2, :], 1.0, None, ALU.add))
        dve.tensor_scalar(SS[:, 6, :], SS[:, 3, :], -1.0, 1e-30, ALU.add, ALU.add).then_inc(dt_d, 1)
        dve.wait_ge(dt_d, 2)
        chain(dve.reciprocal(SS[:, 7, :], SS[:, 6, :]))
        dve.wait_ge(dt_a, 3)
        chain(dve.scalar_tensor_tensor(SS[:, 8, :], SS[:, 4, :], 1e-30, SS[:, 7, :], ALU.add, ALU.mult))
        chain(dve.tensor_tensor(SS[:, 9, :], SS[:, 8, :], SS[:, 2, :], ALU.mult))
        chain(dve.scalar_tensor_tensor(SS[:, 10, :], SS[:, 0, :], 0.0, SS[:, 9, :], ALU.max, ALU.add))
        dve.scalar_tensor_tensor(two(12), two(10), -1.0, both(SS[:, 11, 0:16]), ALU.mult, ALU.mult
                                 ).then_inc(dt_d, 1)
        dve.wait_ge(acs_ps, 1)
        chain(dve.tensor_scalar(SS[:, 13, :], PS[:, 1088:1120], -1.0, None, ALU.mult))
        dve.tensor_tensor(SS[:, 14, 0:16], PS[:, 1120:1136], SS[:, 13, 0:16], ALU.add).then_inc(acs_ok, 1)
        dve.wait_ge(evac_a, EVAC["w_in"] + 9)
        for half in range(2):
            with dve.Fori(2 * half, 2 * half + 2) as i:
                for step in range(4):
                    for a in range(3):
                        tile, x = (t[:, bass.ds(i * 3 + a, 1), :].rearrange("p a t -> p (a t)") for t in (CV, XBC))
                        tap = COLS[:, bass.ds(i * 12 + (4 * a + CONV_W + 3 - step), 1)]
                        if step:
                            dve.wait_ge(dve_chain, i * 9 + (chain.count + 3 * (step - 1) + a + 1))
                            last = dve.scalar_tensor_tensor(tile[:, step:], x[:, :SEQ - step], tap, tile[:, step:],
                                                            ALU.mult, ALU.add)
                        else:
                            last = dve.tensor_scalar(tile, x, tap, COLS[:, bass.ds(i * 3 + (a + CONV_B), 1)],
                                                     ALU.mult, ALU.add)
                        last.then_inc(conv_done if step == 3 else dve_chain, 1)
            split(BASE[f"kv{half + 1}"] + PB, PB)
            kv_evac(half + 1)
        chain.count += 4 * 9
        dve.wait_ge(cb_ps, 1)
        dve.tensor_copy(BN[:], PS[:, 1152:1408].rearrange("p (g n) -> p g n", g=2)).then_inc(cb_ok, 1)
        dve.tensor_tensor(CBM[:].rearrange("p t g n -> p (t g) n"), PS[:, 1536:2048].rearrange("p (a n) -> p a n", a=4),
                          UPTO[:].unsqueeze(1).to_broadcast([P, 4, P]), ALU.mult).then_inc(cb_ok, 1)
        dve.wait_ge(cb_ok, 2)
        for tt in range(TT):
            dve.wait_ge(xs_ps, tt + 1)
            dve.tensor_copy(XSN[:, tt, 512:1024], PS[:, 512:1024]).then_inc(xs_sb, 1)
        for tt in range(TT):
            dve.wait_ge(lm_ok, tt + 1)
            for g in range(2):
                m = LM[:, 8 * g:8 * g + 8, :]
                last = dve.tensor_tensor(m, m, CBM[:, tt, g, :].unsqueeze(1).to_broadcast([P, 8, P]), ALU.mult)
            last.then_inc(m_ok, 1)
            dve.wait_ge(y_ps, tt + 1)
            dve.wait_ge(yz_ok, tt + 1)
            y = YS[:, tt, :]
            chain(dve.tensor_tensor(y, y, PS[:, 0:1024], ALU.add))
            if tt:
                chain(dve.tensor_tensor(XDD[:].rearrange("p (h d) -> p h d", d=64),
                                        PS[:, 1024:2048].rearrange("p (h d) -> p h d", d=64),
                                        SS[:, 15, 16:32].unsqueeze(2).to_broadcast([P, 16, 64]), ALU.mult))
                chain(dve.tensor_tensor(y, y, XDD[:], ALU.add))
            dve.wait_ge(z_silu, 1)
            dve.tensor_tensor(y.rearrange("p (a n) -> p a n", a=2), y.rearrange("p (a n) -> p a n", a=2),
                              Z[:, :, tt, :], ALU.mult).then_inc(y_done, 1)
        dve.wait_ge(y_done, 2)
        prenorm(3, AO, "attn", HTH, HTL)
        prenorm(4, YS, "ssd", HTH, HTL, 8, groups=2)
        split_run(BASE["w_out"] + PB, 16 - 1)
        post_add(1, 1.0, 5, BASE["w_out"] + PB + 16 - 1)
        junction(5, "xa", 3)
        plain("xa_q", 2, mixer_dst)
        for tt in range(TT):
            dve.wait_ge(xs_sc, tt + 1)
            s = slice(tt * 4, tt * 4 + 4)
            chain(dve.reduce_max(STAT[:, 24:32][:, s], ACC[:, tt, :].rearrange("p (h m) -> p h m", h=4), AX_X))
            dve.tensor_scalar(STAT[:, 32:40][:, s], STAT[:, 24:32][:, s], -1.0 / 16, None, ALU.mult).then_inc(xs_max, 1)
        for tt in range(TT):
            dve.wait_ge(xs_exp, tt + 1)
            s = slice(tt * 4, tt * 4 + 4)
            chain(dve.reciprocal(STAT[:, 48:56][:, s], STAT[:, 40:48][:, s]))
            dve.tensor_tensor(PE_[:, tt, :, :], PE_[:, tt, :, :],
                              STAT[:, 48:56][:, s].unsqueeze(2).to_broadcast([P, 4, SEQ]), ALU.mult).then_inc(xs_norm, 1)
        dve.wait_ge(xp_ps, 2)
        dve.tensor_copy(PT[:, 4:8, :], XT_PS[:, 4:8, :]).then_inc(xp_sb, 1)
        for bank in range(4):
            dve.wait_ge(xo_high, bank + 1)
            k2 = slice(2 * bank, 2 * bank + 2)
            dve.tensor_tensor(HTL[:, k2, :], PS[:, 2048 + bank * 512:2560 + bank * 512].rearrange("p (k t) -> p k t", k=2),
                              HTH[:, k2, :].bitcast(F32), ALU.subtract).then_inc(xo_low, 1)
        split_run(BASE["xa_o"] + PB, 8 - 1)
        post_add(2, 1.0, 6, BASE["xa_o"] + PB + 8 - 1)
        prenorm(6, H, "ffn2", begun=True)
        ffn_up("ffn2_up", 1)
        split_run(BASE["ffn2_down"] + PB, FFN_KT - 1)
        post_add(3, 0.5, 7, BASE["ffn2_down"] + PB + FFN_KT - 1)
        prenorm(7, H, "mix2", begun=True)
        lb = COLS[:, LB:LB + 8].rearrange("p (r f) -> p r f", r=2)
        chain(dve.tensor_tensor(LBS[:, 4, :], lb[:, 0, :], lb[:, 1, :], ALU.max))
        dve.tensor_tensor(LBS[:, 0:2, :], lb, LBS[:, 4, :].unsqueeze(1).to_broadcast([P, 2, 4]),
                          ALU.subtract).then_inc(hg_d, 1)

        def chunks(t):
            return t[:].rearrange("p h (n c) -> p (h n) c", c=HG_CHUNK)

        def after_f():
            dve.wait_ge(hg_a, 1)
            chain(dve.tensor_tensor(LBS[:, 4, :], LBS[:, 2, :], LBS[:, 3, :], ALU.add))
            chain(dve.reciprocal(LBS[:, 5, :], LBS[:, 4, :]))
            chain(dve.tensor_tensor(LBS[:, 6, :], LBS[:, 2, :], LBS[:, 5, :], ALU.mult))
            chain(dve.tensor_scalar(LBS[:, 7, :], LBS[:, 6, :], -1.0, 1.0, ALU.mult, ALU.add))
            dve.wait_ge(hg_a, 2)
            for ft in range(4):
                last = dve.tensor_scalar(FG[:, ft, :], FG[:, ft, :], LBS[:, 7, ft:ft + 1], LBS[:, 6, ft:ft + 1],
                                         ALU.mult, ALU.add)
            last.then_inc(hg_d, 1)
            dve.wait_ge(hg_d, 2)
            chain(dve.tensor_scalar(KH[:], FG[:], -1.0, 1.0, ALU.mult, ALU.add))

        def after_g():
            dve.wait_ge(hg_a, 4)
            dve.wait_ge(hg_ok, 4)
            flat = GC[:].rearrange("p h t -> p (h t)")
            dve.tensor_tensor_scan(flat, CHUNK_ON[:], flat, 0.0, ALU.mult, ALU.add).then_inc(hg_d, 1)
            dve.wait_ge(hg_d, 3)
            dve.tensor_tensor(chunks(KEN), chunks(GC)[:, :, HG_CHUNK - 1:].to_broadcast([P, 32, HG_CHUNK]), chunks(GC),
                              ALU.subtract).then_inc(hg_d, 1)

        def after_v():
            dve.wait_ge(hg_a, 6)
            dve.scalar_tensor_tensor(QD[:], Q2, P ** -0.5, EG[:], ALU.mult, ALU.mult)
            dve.tensor_tensor(KD[:], KD[:], KH[:], ALU.mult).then_inc(hg_d, 1)

        def after_c():
            dve.wait_ge(hg_a, 7)
            dve.tensor_tensor(KEN[:], KEN[:], KH[:], ALU.mult).then_inc(hg_d, 1)

        plain("w_in_2", 7, mixer_dst, (after_f, lambda: None, after_g, after_v, after_c))
        dve.wait_ge(evac_a, EVAC["w_in_2"] + 7)
        dve.wait_ge(evac_d, EVAC["w_in_2"] + 7)
        chain(dve.tensor_tensor(U[:], CG, HC, ALU.mult))
        for ft in range(4):
            w = [COLS[:, CONV_W2 + 3 * ft + j:CONV_W2 + 3 * ft + j + 1] for j in range(3)]
            chain(dve.tensor_scalar(Y[:, ft, :], U[:, ft, :], w[2], None, ALU.mult))
            for back in (1, 2):
                chain(dve.scalar_tensor_tensor(Y[:, ft, back:], U[:, ft, :SEQ - back], w[2 - back], Y[:, ft, back:],
                                               ALU.mult, ALU.add))
        dve.tensor_tensor(Y[:], Y[:], BG, ALU.mult).then_inc(c2_d, 1)
        dve.wait_ge(hg_p, 2)
        for tt in range(TT):
            last = dve.copy_predicated(ABD[:, tt, :, :], IN_CHUNK[:].bitcast(U32).unsqueeze(1).to_broadcast([P, 4, P]),
                                       PS[:, 1024 + tt * 512:1536 + tt * 512].rearrange("p (h n) -> p h n", h=4))
        last.then_inc(hg_d, 1)
        dve.wait_ge(s_ok, 1)
        for n in range(1, 7):
            if n == 4:
                dve.wait_ge(c2_p, 1)
                chain(dve.tensor_scalar(MS[:].rearrange("p f t -> p (f t)"), PS[:, 1024:2048], EPS, None, ALU.add))
                dve.reciprocal(MS[:], MS[:]).then_inc(c2_d, 1)
                dve.wait_ge(kv_ps, 2)
            if n > 1:
                dve.wait_ge(s_ok, n)
            for h in range(4):
                last = dve.scalar_tensor_tensor(
                    ST2[:, n, h, :], ST2[:, n - 1, h, :], EG[:, h, (n + 1) * HG_CHUNK - 1:(n + 1) * HG_CHUNK],
                    PS[:, 2048 + n % 4 * 512 + h * P:2048 + n % 4 * 512 + (h + 1) * P], ALU.mult, ALU.add)
            last.then_inc(s_ok, 1)
        dve.wait_ge(c2_a, 2)
        for ft in range(4):
            last = dve.scalar_tensor_tensor(Y[:, ft, :], Y[:, ft, :], COLS[:, CONV_GAIN2 + ft:CONV_GAIN2 + ft + 1],
                                            MS[:, ft, :], ALU.mult, ALU.mult)
        last.then_inc(c2_d, 1)
        dve.wait_ge(c2_a, 3)
        dve.tensor_tensor(XTL[:, 0:4, :], Y[:], XTH[:, 0:4, :].bitcast(F32), ALU.subtract).then_inc(c2_d, 1)
        dve.wait_ge(hg_a, 9)
        chain(dve.tensor_scalar(STAT[:, 40:48], STAT[:, 32:40], 1.0 / P, EPS, ALU.mult, ALU.add))
        dve.reciprocal(STAT[:, 40:48], STAT[:, 40:48]).then_inc(hg_d, 1)
        dve.wait_ge(hg_a, 10)
        for tt in range(TT):
            o = U[:, 2 * tt:2 * tt + 2, :].rearrange("p a t -> p (a t)").rearrange("p (h n) -> p h n", h=4)
            chain(dve.tensor_tensor(o, PS[:, tt * 512:tt * 512 + 512].rearrange("p (h n) -> p h n", h=4),
                                    STAT[:, 48 + tt * 4:52 + tt * 4].unsqueeze(2).to_broadcast([P, 4, P]), ALU.mult))
            last = dve.tensor_tensor(o, o, G2[:, tt, :].rearrange("p (h n) -> p h n", h=4), ALU.mult)
        last.then_inc(hg_d, 1)
        dve.wait_ge(hg_a, 11)
        dve.scalar_tensor_tensor(XTL[:, 4:8, :], XT_PS[:, 4:8, :], COLS[:, HG_GAIN:HG_GAIN + 1],
                                 XTH[:, 4:8, :].bitcast(F32), ALU.mult, ALU.subtract).then_inc(hg_d, 1)
        split_run(BASE["w_out_2"] + PB, 8 - 1)
        for tt in range(TT):
            if tt:
                dve.wait_ge(w_used, BASE["peer_q"])
            else:
                dve.wait_ge(acc0_done, 5)
            dve.tensor_tensor(H[:, tt, :], H[:, tt, :], ACC[:, tt, :], ALU.add).then_inc(h_done, 1)
        split(BASE["w_out_2"] + PB + 8 - 1, 1)
        prenorm(8, H, "peer")
        plain("peer_q", 4, mixer_dst)

        b = BASE["peer"]
        ticks = [0, 0]

        def tick(long=False):
            ticks[0] += not long
            if (long or ticks[0] % 5 == 0) and ticks[1] < SEARCH:
                split(b + PB + ticks[1], 1)
                ticks[1] += 1

        def best16(values, rows, top, places):
            def each(instruction):
                for r in range(rows):
                    last = instruction(r)
                    if r < rows - 1:
                        tick()
                chain(last)
                tick()

            each(lambda r: dve.max(top[:, r, 0:8], values[:, r, :]))
            each(lambda r: dve.max_index(places[:, r, 0:8], top[:, r, 0:8], values[:, r, :]))
            each(lambda r: dve.match_replace(values[:, r, :], top[:, r, 0:8], values[:, r, :], -3.0e38))
            each(lambda r: dve.max(top[:, r, 8:16], values[:, r, :]))
            each(lambda r: dve.max_index(places[:, r, 8:16], top[:, r, 8:16], values[:, r, :]))

        def keys_of(tt):
            dve.wait_ge(hot_ok, 2 * tt + 2)
            for p in range(2):
                dve.reduce_sum(ROUTE[:, tt, p, :], HOT[:, p, :, :], AX_X).then_inc(hot_used, 1)
                tick(long=True)

        dve.wait_ge(iota_ok, 1)
        for tt in range(TT):
            dve.wait_ge(ks_sb, tt + 1)
            best16(SC[:, tt, :, :], 16, TOP[:, tt, :, :], TOP_AT[:, tt, :, :])
            dve.tensor_copy(TOP_ATF[:, tt, :, :], TOP_AT[:, tt, :, :])
            chain(dve.tensor_tensor(CAND[:, tt, :, :].rearrange("p h (a b) -> p h a b", a=16),
                                    TOP[:, tt, 0:16:2, :].unsqueeze(3).to_broadcast([P, 8, 16, 16]),
                                    TOP[:, tt, 1:16:2, :].unsqueeze(2).to_broadcast([P, 8, 16, 16]), ALU.add))
            tick(long=True)
            if tt:
                keys_of(0)
            best16(CAND[:, tt, :, :], 8, CTOP[:, tt, :, :], CAT[:, tt, :, :])
            at_ = CAT[:, tt, :, :].rearrange("p h k -> p (h k)")
            dve.tensor_scalar(CDIG[:, tt, 0, :], at_, 4, None, ALU.logical_shift_right)
            chain(dve.tensor_scalar(CDIG[:, tt, 1, :], at_, 15, None, ALU.bitwise_and))
            chain(dve.tensor_copy(CDIGF[:, tt, :, :], CDIG[:, tt, :, :]))
            if tt:
                dve.wait_ge(hot_used, 2 * tt)
            for p in range(2):
                dve.tensor_tensor(HOT[:, p, :, :], CDIGF[:, tt, p, :].unsqueeze(2).to_broadcast([P, 128, 16]),
                                  IOTA[:, 0:16].unsqueeze(1).to_broadcast([P, 128, 16]),
                                  ALU.is_equal).then_inc(hot_one, 1)
                tick(long=True)
            chain(dve.tensor_copy(GSUM[:, tt, 8:16].unsqueeze(2), CTOP[:, tt, :, 0:1]))
            dve.tensor_tensor(CTOP[:, tt, :, :], CTOP[:, tt, :, :],
                              GSUM[:, tt, 8:16].unsqueeze(2).to_broadcast([P, 8, 16]), ALU.subtract).then_inc(gd_ok, 1)
        split(b + PB + ticks[1], SEARCH - 2 - ticks[1])
        ticks[1] = SEARCH - 2
        keys_of(1)
        for tt in range(TT):
            dve.wait_ge(gexp_ok, tt + 1)
            chain(dve.reduce_sum(GSUM[:, tt, 0:8], CTOP[:, tt, :, :], AX_X))
            chain(dve.reciprocal(GSUM[:, tt, 0:8], GSUM[:, tt, 0:8]))
            dve.tensor_tensor(ROUTE[:, tt, 2, :].rearrange("p (h k) -> p h k", h=8), CTOP[:, tt, :, :],
                              GSUM[:, tt, 0:8].unsqueeze(2).to_broadcast([P, 8, 16]), ALU.mult).then_inc(route_ok, 1)

        def gate_hot(group, dyn=None, late=True):
            if late:
                dve.wait_ge(g_ps, at(group - 1, dyn))
            t, q = bass.ds(at(4 * group, dyn, 4), 4), 4 * (group % 2)
            for p, hot, done in ((0, OA, key1_ok), (1, OB, key2_ok)):
                dve.tensor_tensor(hot[:, q:q + 4, :], IOTA[:].unsqueeze(1).to_broadcast([P, 4, P]),
                                  ROUTE_T[:, p, t].unsqueeze(2).to_broadcast([P, 4, P]), ALU.is_equal).then_inc(done, 1)

        dve.wait_ge(rt_ok, 2)
        for g in range(GROUPS):
            gate_hot(g, late=g >= 2)
        split(b + SEARCH + 4, 1)
        for n in range(1, EARLY - SEARCH):
            with dve.Fori(0, GROUPS // 2) as i:
                for g in range(2):
                    gate_hot(GROUPS * n + g, i * 2)
            split(b + SEARCH + 4 + n, 1)

        def low(v, dyn=None):
            dve.wait_ge(wt_high, at(v + 1, dyn, 8))
            dve.tensor_tensor(WTL[:, v % 4, :], GE[:, v % 4, :], WTH[:, v % 4, :].bitcast(F32),
                              ALU.subtract).then_inc(wt_low, 1)

        m = b + EARLY
        for k in range(4):
            low(k)
        with dve.Fori(0, TURNS - 1) as i:
            for j in range(TURN):
                if j >= 4:
                    low(j, i)
                split(m + 4 + j, 1, i * TURN)
        m, v = m + (TURNS - 1) * TURN, (TURNS - 1) * 8
        for j in range(8):
            if j >= 4:
                low(v + j)
            split(m + 4 + j, 1)
        dve.wait_ge(row_in, 16 * 5)
        for tt in range(TT):
            dve.wait_ge(psq_done, 9 + tt)
            inverse(STAT[:, 16 + tt:17 + tt], STAT[:, 18 + tt:19 + tt]).then_inc(pinv_done, 1)
            dve.wait_ge(prs_done, 9 + tt)
            dve.scalar_tensor_tensor(TMP[:, tt, :], ACC[:, tt, :], STAT[:, 20 + tt:21 + tt],
                                     ROWG[:], ALU.mult, ALU.mult).then_inc(final_ok, 1)

    @block.tensor
    def _(pe):
        def product(out, high, low, w_hi, w_lo, start, stop):
            pe.matmul(out, high, w_hi, start=start, stop=False, skip_group_check=True)
            pe.matmul(out, low, w_hi, start=False, stop=False, skip_group_check=True)
            return pe.matmul(out, high, w_lo, start=False, stop=stop, skip_group_check=True)

        def transpose_norm(k):
            for tt, ready in enumerate((xn_act, xn_dve)):
                pe.wait_ge(ready, k + 1)
                for kt in range(KT):
                    last = pe.transpose(XT_PS[:, kt, tt * P:(tt + 1) * P], XN[:, tt, kt * P:(kt + 1) * P], IDENT[:])
                    if tt == TT - 1 and kt % 2:
                        last.then_inc(xt_ps, 1)
            pe.wait_ge(xt_low, (k + 1) * KT)

        def panel_tokens(n0, pair, dyn=None, blocks=range(PB), high=XTH, low=XTL):
            for b in blocks:
                s = (n0 + b) % SLOTS
                pe.wait_ge(w_split, at(n0 + b + 1, dyn))
                for kt in (2 * b, 2 * b + 1):
                    w = slice((kt % 2) * 512, (kt % 2) * 512 + 512)
                    for tt in range(TT):
                        t = slice(tt * P, (tt + 1) * P)
                        last = product(pair[:, tt * 512:(tt + 1) * 512], high[:, kt, t], low[:, kt, t],
                                       WH[:, s, w], WL[:, s, w], kt == 0, kt == KT - 1)
                last.then_inc(w_used, 1)

        def panel_features(n0, pair, dyn=None, blocks=range(PB), high=XTH, low=XTL):
            for b in blocks:
                s = (n0 + b) % SLOTS
                pe.wait_ge(w_split, at(n0 + b + 1, dyn))
                for kt in (2 * b, 2 * b + 1):
                    for ft in range(4):
                        w = slice((kt % 2) * 512 + ft * P, (kt % 2) * 512 + (ft + 1) * P)
                        last = product(pair[:, ft * SEQ:(ft + 1) * SEQ], WH[:, s, w], WL[:, s, w],
                                       high[:, kt, :], low[:, kt, :], kt == 0 and ft % 2 == 0, kt == KT - 1)
                last.then_inc(w_used, 1)

        def plain(stage, kinds):
            for n, kind in enumerate(kinds):
                if n >= 2:
                    pe.wait_ge(evac_a, EVAC[stage] + n - 1)
                    pe.wait_ge(evac_d, EVAC[stage] + n - 1)
                (panel_tokens if kind == "t" else panel_features)(BASE[stage] + PB * n, PAIR[n % 2])

        def ffn_up(stage, f):
            b, e = BASE[stage], f * FFN_PANELS

            def up(p, parity, dyn=None):
                if dyn is not None or e + p >= 2:
                    pe.wait_ge(hidden_done, at(e + p - 1, dyn))
                panel_tokens(b + PB * p, PAIR[parity], None if dyn is None else dyn * PB)

            def turn(p, parity, dyn=None):
                pe.wait_ge(hidden_done, at(e + p + 1, dyn))
                if dyn is not None or e + p >= 2:
                    pe.wait_ge(ht_low, at(e + p - 1, dyn))
                for ft in range(2):
                    for tt in range(TT):
                        o = 512 * parity + ft * SEQ + tt * P
                        last = pe.transpose(ACC[:, 0, o:o + P], HN[:, parity, tt, ft * P:(ft + 1) * P], IDENT[:])
                last.then_inc(ht_ps, 1)

            up(0, 0)
            up(1, 1)
            turn(0, 0)
            with pe.Fori(0, (FFN_PANELS - 3) // 2) as i:
                for p in (2, 3):
                    up(p, p % 2, i * 2)
                    turn(p - 1, (p - 1) % 2, i * 2)
            p = FFN_PANELS - 1
            up(p, p % 2)
            turn(p - 1, (p - 1) % 2)
            turn(p, p % 2)
            pe.wait_ge(ht_low, e + FFN_PANELS)

        def rows_product(stage, kts, high=HTH, low=HTL):
            for kt in range(kts):
                n = BASE[stage] + kt
                pe.wait_ge(w_split, n + 1)
                for tt in range(TT):
                    t = slice(tt * P, (tt + 1) * P)
                    for half in range(2):
                        w = slice(half * 512, half * 512 + 512)
                        last = product(ACC[:, tt, w], high[:, kt, t], low[:, kt, t],
                                       WH[:, n % SLOTS, w], WL[:, n % SLOTS, w], kt == 0, kt == kts - 1)
                    if kt == kts - 1 and tt == 0:
                        last.then_inc(acc0_done, 1)
                last.then_inc(w_used, 1)

        pe.wait_ge(ident_ok, 1)

        def kv_panel(n, blocks=range(PB)):
            (panel_features if n < 2 else panel_tokens)(BASE[f"kv{n}"], PAIR[0], None, blocks, MTH, MTL)

        def kv_out(n):
            pe.wait_ge(evac_a, EVAC[f"kv{n}"] + 1)
            pe.wait_ge(evac_d, EVAC[f"kv{n}"] + 1)

        transpose_norm(0)
        transpose_norm(1)
        ffn_up("ffn1_up", 0)
        rows_product("ffn1_down", FFN_KT)
        kv_panel(0)
        kv_out(0)
        transpose_norm(2)
        plain("w_in", "fffftt")
        pe.wait_ge(masks_ok, 5)
        pe.wait_ge(evac_a, EVAC["w_in"] + 4)
        pe.wait_ge(evac_d, EVAC["w_in"] + 4)

        def scores(k):
            if k:
                pe.wait_ge(sc_sb, k)
            for h in range(2):
                d = slice(64 * h, 64 * h + 64)
                pe.matmul(S_PS[:, h, 0:SEQ], KTT[d, k, 0:P], QT[d, k, :], start=True, stop=True)
                last = pe.matmul(S_PS[:, h, SEQ:384], KTT[d, k, P:SEQ], QT[d, k, P:SEQ], start=True, stop=True)
            last.then_inc(sc_ps, 1)

        def suffix_sums(k):
            pe.wait_ge(sp_done, k + 1)
            if k:
                pe.wait_ge(loga_done, k)
            if k >= 2:
                pe.wait_ge(o_done, k - 1)
            for h in range(2):
                pe.matmul(C_PS[:, h, 0:384], FROM[:], by_head(SPL, k)[:, h, :], start=True, stop=False)
                last = pe.matmul(C_PS[:, h, P:SEQ], ONES[:], by_head(SPL, k)[:, h, SEQ:384], start=False, stop=True)
            last.then_inc(sum_ps, 1)

        def weighted_values(k):
            a = by_head(LOGA, k)
            pe.wait_ge(a_done, k + 1)
            if k:
                pe.wait_ge(o_done, k)
            for h in range(2):
                c = 2 * k + h
                o = [C_PS[:, h, 384 + tt * 64:448 + tt * 64] for tt in range(TT)]
                v = [V[:, c // 8, tt, c % 8 * 64:c % 8 * 64 + 64] for tt in range(TT)]
                pe.matmul(o[0], a[:, h, 0:P], v[0], start=True, stop=True)
                pe.matmul(o[1], a[:, h, P:SEQ], v[0], start=True, stop=False)
                last = pe.matmul(o[1], a[:, h, SEQ:384], v[1], start=False, stop=True)
            last.then_inc(o_ps, 1)

        for k in range(10):
            if k == 0:
                pe.wait_ge(evac_a, EVAC["w_in"] + 6)
                pe.wait_ge(evac_d, EVAC["w_in"] + 6)
            if k < 8:
                scores(k)
            if 1 <= k <= 8:
                suffix_sums(k - 1)
            if k >= 2:
                weighted_values(k - 2)
            n = 6 + k // 2
            if k % 2 == 0:
                pe.wait_ge(evac_a, EVAC["w_in"] + n - 1)
                pe.wait_ge(evac_d, EVAC["w_in"] + n - 1)
            (panel_tokens if n >= 9 else panel_features)(BASE["w_in"] + PB * n, PAIR[n % 2], None,
                                                        range(k % 2 * 2, k % 2 * 2 + 2))
        pe.wait_ge(wdt_ok, 1)
        pe.wait_ge(evac_a, EVAC["w_in"] + 10)
        pe.wait_ge(evac_d, EVAC["w_in"] + 10)
        for tt in range(TT):
            for kt in range(KT):
                t, w = slice(tt * P, (tt + 1) * P), slice(kt * 16, kt * 16 + 16)
                last = product(PS[:, 1024 + tt * 16:1040 + tt * 16], XTH[:, kt, t], XTL[:, kt, t],
                               WDTH[:, w], WDTL[:, w], kt == 0, kt == KT - 1)
        last.then_inc(dt_ps, 1)
        pe.wait_ge(evac_a, EVAC["w_in"] + 11)
        pe.wait_ge(evac_d, EVAC["w_in"] + 11)
        kv_panel(1, range(0, 2))
        pe.wait_ge(dt_d, 3)
        pe.matmul(PS[:, 1088:1120], UPTO[:], SS[:, 12, :], start=True, stop=True)
        pe.matmul(PS[:, 1120:1136], ONES[:], SS[:, 12, 0:16], start=True, stop=True).then_inc(acs_ps, 1)

        def row_sums(tt):
            pe.wait_ge(au_ok, tt + 1)
            if tt:
                pe.wait_ge(lm_ok, tt)
            for q in range(4):
                o = PS[:, 2048 + q * 512:2560 + q * 512]
                pe.matmul(o, ONES[:], AU[:, 4 * q:4 * q + 4, :].rearrange("p h n -> p (h n)"),
                          start=True, stop=False)
                last = pe.matmul(o.rearrange("p (h n) -> p h n", h=4), IDENT[:],
                                 FUTURE[:].unsqueeze(1).to_broadcast([P, 4, P]), start=False, stop=True)
            last.then_inc(row_ps, 1)

        kv_panel(1, range(2, 4))
        pe.wait_ge(o_done, 8)
        row_sums(0)
        kv_out(1)
        kv_panel(2)
        kv_out(2)
        def xs_tokens(tt):
            if tt:
                pe.wait_ge(xs_sb, 2 * tt)
            for ft in range(8):
                last = pe.transpose(PS[:, ft * P:(ft + 1) * P], CV[:, ft, tt * P:(tt + 1) * P], IDENT[:])
            last.then_inc(xs_ps, 1)

        pe.wait_ge(cv_done, 3)
        pe.wait_ge(acs_ok, 1)
        for g in range(2):
            pe.transpose(PS[:, 1152 + g * P:1280 + g * P], CV[:, 8 + g, 0:P], IDENT[:])
        for tt in range(TT):
            for g in range(2):
                o, t = 1536 + (2 * tt + g) * P, slice(tt * P, (tt + 1) * P)
                last = pe.matmul(PS[:, o:o + P], CV[:, 8 + g, t], CV[:, 10 + g, t], start=True, stop=True)
        last.then_inc(cb_ps, 1)
        xs_tokens(0)
        xs_tokens(1)
        pe.wait_ge(xd_ok, 2)
        pe.wait_ge(cb_ok, 2)
        for g in range(2):
            last = pe.matmul(PS[:, 1024 + g * 512:1536 + g * 512], BN[:, g, :], XDD[:, g * 512:(g + 1) * 512],
                             start=True, stop=True)
        last.then_inc(st_ps, 1)
        for tt in range(TT):
            pe.wait_ge(m_ok, tt + 1)
            pe.wait_ge(xd_ok, (1, 3)[tt])
            pe.wait_ge(xs_sb, 4)
            if tt:
                pe.wait_ge(y_done, 1)
            for h in range(16):
                last = pe.matmul(PS[:, h * 64:(h + 1) * 64], LM[:, h, :], XD[:, tt, h * 64:(h + 1) * 64],
                                 start=True, stop=True)
            if tt:
                pe.wait_ge(st_ok, 1)
                for g in range(2):
                    last = pe.matmul(PS[:, 1024 + g * 512:1536 + g * 512], CV[:, 10 + g, P:SEQ],
                                     ST[:, g * 512:(g + 1) * 512], start=True, stop=True)
            else:
                row_sums(1)
            last.then_inc(y_ps, 1)
        pe.wait_ge(y_done, 2)
        transpose_norm(3)
        transpose_norm(4)
        rows_product("w_out", 16)
        kv_panel(3)
        kv_out(3)
        transpose_norm(5)
        plain("xa_q", "ff")
        pe.wait_ge(evac_a, EVAC["xa_q"] + 2)
        pe.wait_ge(evac_d, EVAC["xa_q"] + 2)
        for tt in range(TT):
            for h in range(4):
                for ft in (2 * h, 2 * h + 1):
                    last = pe.matmul(ACC[:, tt, h * SEQ:(h + 1) * SEQ], QT[:, ft, tt * P:(tt + 1) * P], XAK[:, ft, :],
                                     start=ft % 2 == 0, stop=ft % 2 == 1)
            last.then_inc(xs_sc, 1)
        for half in range(2):
            for h in (2 * half, 2 * half + 1):
                for tt in range(TT):
                    pe.wait_ge(xs_norm, tt + 1)
                    for mt in range(2):
                        last = pe.transpose(XT_PS[:, 2 * h + mt, tt * P:(tt + 1) * P],
                                            PE_[:, tt, h, mt * P:(mt + 1) * P], IDENT[:])
            last.then_inc(xp_ps, 1)
        pe.wait_ge(xp_sb, 2)
        for ft in range(8):
            for mt in range(2):
                last = pe.matmul(PS[:, 2048 + ft * SEQ:2048 + (ft + 1) * SEQ],
                                 XAV[:, ft // 4, mt, ft % 4 * P:ft % 4 * P + P], PT[:, ft // 2 * 2 + mt, :],
                                 start=mt == 0, stop=mt == 1)
            if ft % 2:
                last.then_inc(xo_ps, 1)
        pe.wait_ge(xo_low, 4)
        rows_product("xa_o", 8)
        transpose_norm(6)
        ffn_up("ffn2_up", 1)
        rows_product("ffn2_down", FFN_KT)
        transpose_norm(7)
        plain("w_in_2", "ffttfff")
        pe.wait_ge(evac_a, EVAC["w_in_2"] + 7)
        pe.wait_ge(evac_d, EVAC["w_in_2"] + 7)
        pe.wait_ge(hg_d, 6)
        for tt in range(TT):
            for h in range(4):
                last = pe.transpose(PS[:, (tt * 4 + h) * P:(tt * 4 + h + 1) * P], KEN[:, h, tt * P:(tt + 1) * P], IDENT[:])
        last.then_inc(hg_p, 1)
        for tt in range(TT):
            for h in range(4):
                o, t = 1024 + (tt * 4 + h) * P, slice(tt * P, (tt + 1) * P)
                last = pe.matmul(PS[:, o:o + P], KD[:, h, t], QD[:, h, t], start=True, stop=True)
        last.then_inc(hg_p, 1)

        def chunk_kv(tt):
            for j in range(4 - tt):
                rows = slice(HG_CHUNK * j, HG_CHUNK * (j + 1))
                for h in range(4):
                    last = pe.matmul(PS[:, 2048 + j * 512 + h * P:2048 + j * 512 + (h + 1) * P], KE[rows, tt, h, :],
                                     V2[rows, tt, h * P:(h + 1) * P], start=True, stop=True,
                                     tile_position=(HG_CHUNK * j, 0))
            last.then_inc(kv_ps, 1)

        pe.wait_ge(hg_a, 8)
        chunk_kv(0)
        pe.wait_ge(c2_a, 1)
        pe.wait_ge(hg_d, 7)
        for half in range(2):
            last = pe.matmul(PS[:, 1024 + half * 512:1536 + half * 512], GROUP64[:],
                             MS[:, 2 * half:2 * half + 2, :].rearrange("p f t -> p (f t)"), start=True, stop=True)
        last.then_inc(c2_p, 1)
        pe.wait_ge(s_ok, 4)
        chunk_kv(1)
        for tt in range(TT):
            for h in range(4):
                o = tt * 512 + h * P
                last = pe.matmul(PS[:, o:o + P], ABD[:, tt, h, :], V2[:, tt, h * P:(h + 1) * P],
                                 start=h == 0, stop=False, skip_group_check=True)
            if tt == 0:
                last.then_inc(hg_p, 1)
            else:
                pe.wait_ge(s_ok, 7)
            for n in range(max(1, 4 * tt), 4 * tt + 4):
                rows = slice(HG_CHUNK * (n % 4), HG_CHUNK * (n % 4 + 1))
                if n > 1:
                    pe.wait_ge(s_ok, n)
                for h in range(4):
                    o = tt * 512 + h * P
                    last = pe.matmul(PS[rows, o:o + P], QD[:, h, n * HG_CHUNK:(n + 1) * HG_CHUNK],
                                     ST2[:, n - 1, h, :], start=False, stop=True, skip_group_check=True)
        last.then_inc(hg_p, 1)
        pe.wait_ge(hg_d, 9)
        for tt in range(TT):
            o = U[:, 2 * tt:2 * tt + 2, :].rearrange("p a t -> p (a t)")
            for h in range(4):
                last = pe.transpose(XT_PS[:, 4 + h, tt * P:(tt + 1) * P], o[:, h * P:(h + 1) * P], IDENT[:])
        last.then_inc(hg_p, 1)
        pe.wait_ge(hg_d, 10)
        pe.wait_ge(c2_d, 4)
        rows_product("w_out_2", 8, XTH, XTL)
        transpose_norm(8)
        plain("peer_q", "ffff")
        pe.wait_ge(keys_in, 16)
        pe.wait_ge(evac_a, EVAC["peer_q"] + 4)
        pe.wait_ge(evac_d, EVAC["peer_q"] + 4)
        b = BASE["peer"]

        def u_block(n, bank, dyn=None):
            s = n % SLOTS
            pe.wait_ge(w_split, at(n + 1, dyn))
            o = PS[:, bank * 512:bank * 512 + SEQ]
            for kt in range(KT):
                w = slice(kt * P, (kt + 1) * P)
                last = product(o, WH[:, s, w], WL[:, s, w], XTH[:, kt, :], XTL[:, kt, :], kt == 0, kt == KT - 1)
            last.then_inc(w_used, 1)

        def early_tile(n, dyn=None, late=True):
            if late:
                pe.wait_ge(gelu_ok, at(n - 1, dyn))
            u_block(b + n, n % 2, dyn)

        for tt in range(TT):
            if tt:
                pe.wait_ge(ks_sb, tt)
            for hp in range(16):
                last = pe.matmul(PS[:, 2048 + hp * P:2048 + (hp + 1) * P], QP[:, hp, tt * P:(tt + 1) * P], KEYS[:, hp, :],
                                 start=True, stop=True)
            last.then_inc(ks_ps, 1)
            early_tile(tt, late=False)
        pe.wait_ge(ks_sb, 2)
        for tt in range(TT):
            for half in range(2):
                w = slice(half * 512, half * 512 + 512)
                last = pe.matmul(ACC[:, tt, w], IDENT[:], H[:, tt, w], start=True, stop=False, skip_group_check=True)
        last.then_inc(injected, 1)
        early_tile(2)
        early_tile(3)
        with pe.Fori(1, SEARCH // 4) as i:
            for n in range(4):
                early_tile(n, i * 4)
        for tt in range(TT):
            pe.wait_ge(route_ok, tt + 1)
            pe.wait_ge(hot_used, 2 * tt + 2)
            if tt:
                pe.wait_ge(rt_ok, tt)
            for a in range(3):
                last = pe.transpose(PS[:, 1024 + a * P:1152 + a * P], ROUTE[:, tt, a, :], IDENT[:])
            last.then_inc(rt_ps, 1)

        def gates(group, dyn=None, late=True):
            pe.wait_ge(hot4_ok, at(group + 1, dyn))
            pe.wait_ge(key2_ok, at(group + 1, dyn))
            if late:
                pe.wait_ge(g_sb, at(group - 1, dyn))
            q = group % 2
            for j in range(4):
                o = 1024 + 512 * q + j * P
                last = pe.matmul(PS[:, o:o + P], OB[:, 4 * q + j, :], OA[:, 4 * q + j, :], start=True, stop=True)
            last.then_inc(g_ps, 1)

        for n in range(EARLY - SEARCH):
            early_tile(SEARCH + n)
            if n == 0:
                pe.wait_ge(rt_ok, 2)
                gates(0, late=False)
                gates(1, late=False)
            first = 1 if n == 0 else 0
            with pe.Fori(first, GROUPS // 2) as i:
                for g in range(2):
                    gates(GROUPS * n + g, i * 2)

        def v_block(n, v, dyn=None):
            s = n % SLOTS
            pe.wait_ge(w_split, at(n + 1, dyn, TURN))
            pe.wait_ge(wt_low, at(v + 1, dyn, 8))
            for tt in range(TT):
                t = slice(tt * P, (tt + 1) * P)
                for half in range(2):
                    w = slice(half * 512, half * 512 + 512)
                    last = product(ACC[:, tt, w], WTH[:, v % 4, t], WTL[:, v % 4, t], WH[:, s, w], WL[:, s, w],
                                   False, dyn is None and v == 2 * EARLY - 1)
                if dyn is None and v == 2 * EARLY - 1 and tt == 0:
                    last.then_inc(acc0_done, 1)
            last.then_inc(w_used, 1)

        m = b + EARLY
        pe.wait_ge(g_sb, 64)
        pe.wait_ge(gelu_ok, EARLY)
        with pe.Fori(0, TURNS - 1) as i:
            for k in range(4):
                pe.wait_ge(gelu_ok, i * 4 + (EARLY - 3 + k))
                u_block(m + k, k, i * TURN)
            for j in range(8):
                v_block(m + 4 + j, j, i)
        m, v = m + (TURNS - 1) * TURN, (TURNS - 1) * 8
        for k in range(4):
            pe.wait_ge(gelu_ok, 2 * EARLY - 7 + k)
            u_block(m + k, k)
        for j in range(8):
            v_block(m + 4 + j, v + j)

    ctx.close()


def panels(w):
    n = w.shape[1] // 512
    return w.reshape(PB, 2, P, n, 512).transpose(3, 0, 2, 1, 4).reshape(n * PB, P, BLK)


def row_blocks(w):
    return w.reshape(-1, P, BLK)


def gate_up(w):
    return w.reshape(D, 2, FFN_PANELS, 256).transpose(0, 2, 1, 3).reshape(D, 2 * D_FF)


def col(v):
    return v.reshape(-1, P).T


def kernel(**inputs):
    import concourse.bacc as bacc
    from concourse.bass_utils import run_bass_kernel_spmd

    a = {k: np.ascontiguousarray(v) for k, v in inputs.items()}
    g = {k: (v[0] if v.shape[0] == 1 and k not in ("hg_lb_logits_2", "norm_f_2") else v) for k, v in a.items()}
    u = g["peer_u_2"].reshape(P, P, KT, P).transpose(0, 3, 2, 1).reshape(P, P, BLK)
    v = g["peer_v_2"].reshape(P, P, BLK)
    turns = [part.reshape(TURNS, 4, P, BLK) for part in (u[EARLY:], v[:EARLY], v[EARLY:])]
    kv = panels(g["xa_wkv"])
    parts = [
        panels(gate_up(g["ffn1_w_gu"])), row_blocks(g["ffn1_w_down"]), kv[:PB],
        panels(np.concatenate([g["w_in"][:, :3072], g["w_in"][:, 4096:5632], g["w_in"][:, 3072:4096]], axis=1)), kv[PB:3 * PB],
        row_blocks(g["w_out"]), kv[3 * PB:], panels(g["xa_wq"]), row_blocks(g["xa_wo"]),
        panels(gate_up(g["ffn2_w_gu"])), row_blocks(g["ffn2_w_down"]),
        panels(g["w_in_2"].reshape(D, 7, 512)[:, [4, 3, 6, 5, 0, 1, 2]].reshape(D, 3584)),
        row_blocks(g["w_out_2"]), panels(g["peer_wq_2"]),
        u[:EARLY], np.stack(turns, axis=1).reshape(-1, P, BLK),
    ]
    cols = np.concatenate(
        [col(g[k]) for k in ("mem_g", "ffn1_pre_g", "mix_pre_g", "xa_pre_g", "ffn2_pre_g", "norm_mix_2",
                             "norm_ffn_2", "attn_norm_g", "ssd_norm_g", "conv_gain_2", "hg_gain_2", "conv_b")]
        + [g["conv_w"].reshape(4, 12, P).transpose(2, 1, 0).reshape(P, 48),
           g["conv_w_2"].reshape(3, 4, P).transpose(2, 1, 0).reshape(P, 12),
           g["hg_lb_logits_2"].reshape(2, 4, P).transpose(2, 0, 1).reshape(P, 8)], axis=1)
    arrays = {
        "stream": np.concatenate(parts, axis=0),
        "w_dt": g["w_in"][:, 5632:].reshape(KT, P, 16).transpose(1, 0, 2).reshape(P, KT * 16),
        "cols": cols,
        "small_row": np.concatenate([g["dt_bias"], g["a_log"], g["d_skip"]]).reshape(1, 48),
        "rows": np.stack([g["ffn1_post_g"], g["mix_post_g"], g["xa_post_g"], g["ffn2_post_g"], g["norm_f_2"]]),
        "x": a["x"].reshape(SEQ, D),
        "mem": a["mem"].reshape(SEQ, D),
        "keys": g["peer_keys_2"].reshape(16, P, P).transpose(2, 0, 1),
    }
    nc = bacc.Bacc("TRN2", target_bir_lowering=False, num_devices=1)
    ins = [nc.dram_tensor(f"in_{k}", v.shape, F32, kind="ExternalInput").ap() for k, v in arrays.items()]
    out = nc.dram_tensor("out", (SEQ, D), F32, kind="ExternalOutput").ap()
    early = nc.dram_tensor("early_gelu", (EARLY, P, SEQ), F32, kind="Internal").ap()
    build(nc, *ins, early, out)
    r = run_bass_kernel_spmd(nc, [{f"in_{k}": np.ascontiguousarray(v) for k, v in arrays.items()}], core_ids=[0])
    return r.results[0]["out"].reshape(1, SEQ, D)
```
